# Optimizing a Trainium2 kernel written in Bass

```python
import jax, jax.numpy as jnp
from jax import lax
import numpy as np

D_MODEL = 1024
BATCH = 1
SEQ = 512
DEPTH = 2

D_MIX = 1024
MLA_HEADS = 8
QK_NOPE = 64
QK_ROPE = 32
QK_HEAD = QK_NOPE + QK_ROPE
V_HEAD = 64
Q_LORA = 384
KV_LORA = 256
MLA_WIDTH = MLA_HEADS * V_HEAD
ROPE_THETA = 10000.0
Q_BLOCK = 128
POOL_WINDOWS = (2, 4, 8, 16)
POOL_GROUPS = len(POOL_WINDOWS)
POOL_WIDTH = D_MIX - MLA_WIDTH
POOL_GROUP_DIM = POOL_WIDTH // POOL_GROUPS
D_IN = Q_LORA + KV_LORA + QK_ROPE + POOL_WIDTH
D_FF = 2816
EPS = 1e-6

kernel_name = "hybrid_mla_pool_macaron_encoder"

def rmsnorm(x, g):
    xf = x.astype(jnp.float32)
    y = xf * lax.rsqrt(jnp.mean(xf * xf, axis=-1, keepdims=True) + EPS)
    return (y * g.astype(jnp.float32)).astype(x.dtype)

def swiglu(h, w_gu, w_down):
    gu = h @ w_gu
    g, u = gu[..., :D_FF], gu[..., D_FF:]
    return (jax.nn.silu(g) * u) @ w_down

def rope_tables(seq):
    pos = jnp.arange(seq, dtype=jnp.float32)
    inv = ROPE_THETA ** (-jnp.arange(0, QK_ROPE, 2, dtype=jnp.float32) / QK_ROPE)
    ang = pos[:, None] * inv[None, :]
    return jnp.cos(ang), jnp.sin(ang)

def apply_rope(t, cos, sin):
    tf = t.astype(jnp.float32)
    half = QK_ROPE // 2
    t1, t2 = tf[..., :half], tf[..., half:]
    c, s = cos[None, :, None, :], sin[None, :, None, :]
    out = jnp.concatenate([t1 * c - t2 * s, t2 * c + t1 * s], axis=-1)
    return out.astype(t.dtype)

def bidir_attention(q, k, v):
    B, S, H, Dq = q.shape
    nb = S // Q_BLOCK
    qb = jnp.moveaxis((q * (Dq ** -0.5)).reshape(B, nb, Q_BLOCK, H, Dq), 1, 0)

    def block(q_blk):
        s = jnp.einsum('bqhd,bkhd->bhqk', q_blk, k, preferred_element_type=jnp.float32)
        p = jax.nn.softmax(s, axis=-1).astype(v.dtype)
        return jnp.einsum('bhqk,bkhd->bqhd', p, v)

    o = lax.map(block, qb)
    return jnp.moveaxis(o, 0, 1).reshape(B, S, H * V_HEAD)

def mla_mixer(c_q, c_kv, k_pe, q_lat_norm, kv_lat_norm, w_uq, w_uk, w_uv, q_norm, k_norm, cos, sin):
    B, S, _ = c_q.shape
    c_q = rmsnorm(c_q, q_lat_norm)
    c_kv = rmsnorm(c_kv, kv_lat_norm)
    q = (c_q @ w_uq).reshape(B, S, MLA_HEADS, QK_HEAD)
    k_nope = (c_kv @ w_uk).reshape(B, S, MLA_HEADS, QK_NOPE)
    v = (c_kv @ w_uv).reshape(B, S, MLA_HEADS, V_HEAD)
    k_pe_h = jnp.broadcast_to(k_pe[:, :, None, :], (B, S, MLA_HEADS, QK_ROPE))
    k = jnp.concatenate([k_nope, k_pe_h], axis=-1)
    q = rmsnorm(q, q_norm)
    k = rmsnorm(k, k_norm)
    q = jnp.concatenate([q[..., :QK_NOPE], apply_rope(q[..., QK_NOPE:], cos, sin)], axis=-1)
    k = jnp.concatenate([k[..., :QK_NOPE], apply_rope(k[..., QK_NOPE:], cos, sin)], axis=-1)
    return bidir_attention(q, k, v)

def pool_mixer(p, w_pool, pool_scale):
    B, S, C = p.shape
    pf = p.astype(jnp.float32)
    cs = jnp.concatenate([jnp.zeros((B, 1, C), jnp.float32), jnp.cumsum(pf, axis=1)], axis=1)
    idx = jnp.arange(S)
    outs = []
    for g, w in enumerate(POOL_WINDOWS):
        left = w // 2
        right = w - 1 - left
        lo = jnp.clip(idx - left, 0, S)
        hi = jnp.clip(idx + right + 1, 0, S)
        csg = cs[..., g * POOL_GROUP_DIM:(g + 1) * POOL_GROUP_DIM]
        wsum = jnp.take(csg, hi, axis=1) - jnp.take(csg, lo, axis=1)
        cnt = (hi - lo).astype(jnp.float32)[None, :, None]
        outs.append(wsum / cnt)
    pooled = jnp.stack(outs, axis=2)
    mixed = (pooled - pf.reshape(B, S, POOL_GROUPS, POOL_GROUP_DIM)).astype(p.dtype)
    y = jnp.einsum('bsgc,gcd->bsgd', mixed, w_pool).reshape(B, S, C)
    return y * pool_scale

def setup_inputs(seed: int = 0) -> dict:
    key = jax.random.key(seed)
    ks = jax.random.split(key, 20)
    f32 = jnp.float32

    def w(k, shape, fan_in):
        return jax.random.normal(k, shape, f32) * (fan_in ** -0.5)

    def gain(k, shape):
        return 1.0 + 0.02 * jax.random.normal(k, shape, f32)

    return {
        "x": jax.random.normal(ks[0], (BATCH, SEQ, D_MODEL), f32),
        "ffn1_norm": gain(ks[1], (DEPTH, D_MODEL)),
        "ffn1_w_gu": w(ks[2], (DEPTH, D_MODEL, 2 * D_FF), D_MODEL),
        "ffn1_w_down": w(ks[3], (DEPTH, D_FF, D_MODEL), D_FF),
        "mix_norm": gain(ks[4], (DEPTH, D_MODEL)),
        "w_in": w(ks[5], (DEPTH, D_MODEL, D_IN), D_MODEL),
        "q_lat_norm": gain(ks[6], (DEPTH, Q_LORA)),
        "kv_lat_norm": gain(ks[7], (DEPTH, KV_LORA)),
        "w_uq": w(ks[8], (DEPTH, Q_LORA, MLA_HEADS * QK_HEAD), Q_LORA),
        "w_uk": w(ks[9], (DEPTH, KV_LORA, MLA_HEADS * QK_NOPE), KV_LORA),
        "w_uv": w(ks[10], (DEPTH, KV_LORA, MLA_HEADS * V_HEAD), KV_LORA),
        "q_norm": gain(ks[11], (DEPTH, QK_HEAD)),
        "k_norm": gain(ks[12], (DEPTH, QK_HEAD)),
        "w_pool": w(ks[13], (DEPTH, POOL_GROUPS, POOL_GROUP_DIM, POOL_GROUP_DIM), POOL_GROUP_DIM),
        "pool_scale": gain(ks[14], (DEPTH, POOL_WIDTH)),
        "w_out": w(ks[15], (DEPTH, D_MIX, D_MODEL), D_MIX),
        "ffn2_norm": gain(ks[16], (DEPTH, D_MODEL)),
        "ffn2_w_gu": w(ks[17], (DEPTH, D_MODEL, 2 * D_FF), D_MODEL),
        "ffn2_w_down": w(ks[18], (DEPTH, D_FF, D_MODEL), D_FF),
    }

def reference(x, ffn1_norm, ffn1_w_gu, ffn1_w_down, mix_norm, w_in, q_lat_norm, kv_lat_norm,
              w_uq, w_uk, w_uv, q_norm, k_norm, w_pool, pool_scale, w_out,
              ffn2_norm, ffn2_w_gu, ffn2_w_down):
    S = x.shape[1]
    cos, sin = rope_tables(S)
    o_kv = Q_LORA
    o_pe = Q_LORA + KV_LORA
    o_pool = Q_LORA + KV_LORA + QK_ROPE
    for l in range(DEPTH):
        x = x + 0.5 * swiglu(rmsnorm(x, ffn1_norm[l]), ffn1_w_gu[l], ffn1_w_down[l])
        z = rmsnorm(x, mix_norm[l]) @ w_in[l]
        a = mla_mixer(z[..., :o_kv], z[..., o_kv:o_pe], z[..., o_pe:o_pool],
                      q_lat_norm[l], kv_lat_norm[l], w_uq[l], w_uk[l], w_uv[l],
                      q_norm[l], k_norm[l], cos, sin)
        b = pool_mixer(z[..., o_pool:], w_pool[l], pool_scale[l])
        x = x + jnp.concatenate([a, b], axis=-1) @ w_out[l]
        x = x + 0.5 * swiglu(rmsnorm(x, ffn2_norm[l]), ffn2_w_gu[l], ffn2_w_down[l])
    return x


_drawn_inputs = setup_inputs


def setup_inputs(seed=0):
    import zlib

    import numpy as np

    out = dict(_drawn_inputs(seed))
    spreads = {}
    factors = {'ffn1_norm': 4.879,
     'mix_norm': 3.926,
     'q_lat_norm': 8.0,
     'kv_lat_norm': 8.0,
     'q_norm': 8.0,
     'k_norm': 8.0,
     'pool_scale': 4.023,
     'ffn2_norm': 6.246}
    for name, (base, spread) in spreads.items():
        noise = np.random.default_rng([zlib.crc32(name.encode()), seed]).standard_normal(out[name].shape)
        drawn = base * np.exp(spread * noise) if base else spread * noise
        out[name] = __import__('jax').numpy.asarray(drawn.astype(out[name].dtype))
    for name, factor in factors.items():
        out[name] = (out[name] * factor).astype(out[name].dtype)
    return out
```

```python
from contextlib import ExitStack

import concourse.bass as bass
from concourse import mybir

F32 = mybir.dt.float32
F32R = mybir.dt.float32r
ACT = mybir.ActivationFunctionType
ALU = mybir.AluOpType
AX_X = mybir.AxisListType.X

P = 128
EPS = 1e-6
QK_NOPE, QK_ROPE, V_HEAD = 64, 32, 64
QK = QK_NOPE + QK_ROPE
PAD = 8
RING = 2
BANKS = 4


def build_trunk(nc, x_in, ffn1_norm, ffn1_w_gu, ffn1_w_down, mix_norm, w_in, q_lat_norm, kv_lat_norm,
                w_uq, w_uk, w_uv, q_norm, k_norm, w_pool, pool_scale, w_out,
                ffn2_norm, ffn2_w_gu, ffn2_w_down, rope_cos, rope_sin, pool_edge, y_out):
    _, S, D = x_in.shape
    DEPTH = ffn1_w_gu.shape[0]
    F = ffn1_w_down.shape[1]
    QL, KVL = w_uq.shape[1], w_uk.shape[1]
    HEADS = w_uq.shape[2] // QK
    PG = w_pool.shape[1]
    DT, TT, FT = D // P, S // P, F // P
    QT, KT = QL // P, KVL // P
    CAT = HEADS * V_HEAD // P
    O_KV, O_PE, O_POOL = QL, QL + KVL, QL + KVL + QK_ROPE
    SCALE = float(QK) ** -0.5
    assert S == 512 and DT == 8 and TT == 4 and QT == 3 and KT == 2 and PG == 4 and HEADS == 8

    CHUNKS = [8, 8, FT - 16]
    assert all(n % 2 == 0 and 0 < n <= 8 for n in CHUNKS)
    FFN_PAIRS = FT + len(CHUNKS) * DT // 2
    MIX_PAIRS, OUT_PAIRS = 8, DT // 2
    MIX_GROUPS = 10 + 4 + 4 + 6 + 4
    PAIR_MIX = FFN_PAIRS
    PAIR_OUT = PAIR_MIX + MIX_PAIRS
    PAIR_FFN2 = PAIR_OUT + OUT_PAIRS
    PAIRS = PAIR_FFN2 + FFN_PAIRS
    GROUP_MIX = 2 * FFN_PAIRS
    GROUP_UV = GROUP_MIX + 10
    GROUP_UK, GROUP_UQ, GROUP_POOL = GROUP_UV + 4, GROUP_UV + 8, GROUP_UV + 14
    GROUP_OUT = GROUP_MIX + MIX_GROUPS
    GROUP_FFN2 = GROUP_OUT + 2 * OUT_PAIRS
    GROUPS = GROUP_FFN2 + 2 * FFN_PAIRS
    assert PAIRS % RING == 0 and PAIR_MIX % RING == 0 and PAIR_FFN2 % RING == 0
    assert GROUPS % BANKS == 0 and GROUP_MIX % BANKS == 0 and GROUP_FFN2 % BANKS == 0 and GROUP_OUT % BANKS == 0
    NORMS = 5
    N_FFN1, N_MIX, N_QL, N_KVL, N_FFN2 = range(NORMS)

    V_FFN1, V_MIX, V_FFN2 = 0, DT, 2 * DT
    V_QL = 3 * DT
    V_KVL = V_QL + QT
    V_PS = V_KVL + KT
    V_QN, V_KN, V_QPE, V_KPE = V_PS + PG, V_PS + PG + 1, V_PS + PG + 2, V_PS + PG + 3
    VECS = V_KPE + 1
    DVE_STEPS = 9
    X_LINKS = 2 * DT - 2
    POOL_STEPS = 3 * X_LINKS + 2 * QT - 2 + 2 * KT - 2 + PG * (PG + 1) // 2
    VROWS = DEPTH * VECS + DT

    with ExitStack() as ctx:
        TB = 4 * S
        arena_bytes = 103 * TB
        arena = ctx.enter_context(nc.sbuf_tensor("arena", [P, arena_bytes // 4], F32))
        base = nc.sbuf_base - arena_bytes
        used = [0]

        def place(name, shape, dt, at=None):
            size = 4
            for n in shape[1:]:
                size *= n
            if at is None:
                at = used[0]
                used[0] += (size + 31) // 32 * 32
                assert used[0] <= arena_bytes, name
            return nc.alloc_sbuf_tensor_at(name, shape, dt, offset=base + at), at

        w_raw = [place(f"w_raw{b}", [P, 2048], F32)[0] for b in range(RING)]
        w_hi = [place(f"w_hi{b}", [P, 2048], F32R)[0] for b in range(RING)]
        w_lo = [place(f"w_lo{b}", [P, 2048], F32R)[0] for b in range(RING)]
        x, _ = place("x", [P, DT, S], F32)
        xg_hi, at_xg_hi = place("xg_hi", [P, DT, S], F32R)
        xg_lo, at_xg_lo = place("xg_lo", [P, DT, S], F32R)
        sq_k = [place(f"sq_k{i}", [P, S], F32, at_xg_hi + i * TB)[0] for i in range(2)]
        sq_q = [place(f"sq_q{i}", [P, S], F32, at_xg_hi + (2 + i) * TB)[0] for i in range(2)]
        head_rms = [place(f"head_rms{i}", [P, S], F32, at_xg_lo + i * TB)[0] for i in range(2)]
        q_rope, _ = place("q_rope", [P, 2, S], F32, at_xg_lo + 2 * TB)
        h_hi, _ = place("h_hi", [P, 8, S], F32R)
        h_lo, _ = place("h_lo", [P, 8, S], F32R)
        v_hi, _ = place("v_hi", [P, TT, P], F32R)
        v_lo, _ = place("v_lo", [P, TT, P], F32R)
        q_all, at_q = place("q_all", [P, HEADS, S], F32)
        k_all, at_k = place("k_all", [P, HEADS, S], F32)
        v_all, _ = place("v_all", [P, TT, HEADS * V_HEAD], F32)
        gate = [place(f"gate{i}", [P, S], F32, at_q + i * TB)[0] for i in range(2)]
        up = [place(f"up{i}", [P, S], F32, at_q + (2 + i) * TB)[0] for i in range(2)]
        silu = [place(f"silu{i}", [P, S], F32, at_q + (4 + i) * TB)[0] for i in range(2)]
        hid = [place(f"hid{i}", [P, S], F32, at_q + (6 + i) * TB)[0] for i in range(2)]
        PW = S + 2 * PAD
        zp, _ = place("zp", [P, PG, PW], F32, at_q)
        win_a, _ = place("win_a", [P, PW], F32, at_q + 4 * 4 * PW)
        win_b, _ = place("win_b", [P, PW], F32, at_q + 5 * 4 * PW)
        win_s, _ = place("win_s", [P, PW], F32, at_q + 6 * 4 * PW)
        assert 7 * 4 * PW <= HEADS * TB
        x_tok, _ = place("x_tok", [P, TT, D], F32, at_k)
        y_tok, _ = place("y_tok", [P, TT, D], F32, at_k)
        prob, at_a = place("prob", [P, 2, TT, S], F32)
        z, _ = place("z", [P, QT + KT, S], F32, at_a)
        q_pe, _ = place("q_pe", [P, 2, S], F32, at_a)
        rot_a, _ = place("rot_a", [P, S], F32, at_a + 2 * TB)
        rot_b, _ = place("rot_b", [P, S], F32, at_a + 3 * TB)
        k_pe, _ = place("k_pe", [P, S], F32, at_a + 5 * TB)
        sumsq_l = [place(f"sumsq_l{i}", [P, S], F32, at_a + (6 + i) * TB)[0] for i in range(2)]
        cos_t, _ = place("cos_t", [P, S], F32)
        sin_t, _ = place("sin_t", [P, S], F32)
        k_rot, _ = place("k_rot", [P, S], F32)
        rstd_x, _ = place("rstd_x", [P, S], F32)
        rstd_l, _ = place("rstd_l", [P, S], F32)
        sumsq_x, _ = place("sumsq_x", [P, S], F32)
        square, _ = place("square", [P, S], F32)
        ones, _ = place("ones", [P, P], F32)
        ident, _ = place("ident", [P, P], F32)
        gain_rows, _ = place("gain_rows", [P, P], F32)
        gains, _ = place("gains", [P, P], F32)
        edge, _ = place("edge", [P, PG, 2 * PAD], F32)
        eps_t, _ = place("eps_t", [P, 1], F32)
        row_max, _ = place("row_max", [P, 2, TT], F32)
        neg_max, _ = place("neg_max", [P, 2, TT], F32)
        row_sum, _ = place("row_sum", [P, 2, TT], F32)
        row_inv, _ = place("row_inv", [P, 2, TT], F32)

        bank = [ctx.enter_context(nc.psum_tensor(f"bank{i}", [P, S], F32)) for i in range(8)]
        SUMS, TRANS, OUT = 4, 5, 7

        def sem(name):
            return ctx.enter_context(nc.semaphore(name))

        const_loaded, memset_done, ident_done = sem("const_loaded"), sem("memset_done"), sem("ident_done")
        gains_t, gains_done = sem("gains_t"), sem("gains_done")
        x_loaded, x_turned = sem("x_loaded"), sem("x_turned")
        y_turned, y_copied, y_stored = sem("y_turned"), sem("y_copied"), sem("y_stored")
        raw_loaded = [sem(f"raw_loaded{b}") for b in range(RING)]
        hi_split, lo_split = sem("hi_split"), sem("lo_split")
        acc_done, evac_done = sem("acc_done"), sem("evac_done")
        x_done, xg_hi_done, xg_lo_done = sem("x_done"), sem("xg_hi_done"), sem("xg_lo_done")
        pool_step = sem("pool_step")
        sumsq_done, sums_done, rms_done, rstd_done = sem("sumsq_done"), sem("sums_done"), sem("rms_done"), sem("rstd_done")
        silu_done, hid_done, h_hi_done, h_lo_done = sem("silu_done"), sem("hid_done"), sem("h_hi_done"), sem("h_lo_done")
        dve_step = sem("dve_step")
        lat_scaled, lat_hi, lat_lo = sem("lat_scaled"), sem("lat_hi"), sem("lat_lo")
        windowed, mixed_done, mixed_hi, mixed_lo = sem("windowed"), sem("mixed_done"), sem("mixed_hi"), sem("mixed_lo")
        pooled_hi, pooled_lo = sem("pooled_hi"), sem("pooled_lo")
        k_rope_done, k_filled, q_rope_done, q_filled = sem("k_rope_done"), sem("k_filled"), sem("q_rope_done"), sem("q_filled")
        head_sq, q_sq_pe, head_sums, head_rms_done, head_inv, head_normed = (
            sem("head_sq"), sem("q_sq_pe"), sem("head_sums"), sem("head_rms_done"), sem("head_inv"), sem("head_normed"))
        qk_hi, qk_lo, v_hi_done, v_lo_done = sem("qk_hi"), sem("qk_lo"), sem("v_hi_done"), sem("v_lo_done")
        scores_done, max_done, neg_done, exp_done = sem("scores_done"), sem("max_done"), sem("neg_done"), sem("exp_done")
        inv_done, prob_done, trans_done = sem("inv_done"), sem("prob_done"), sem("trans_done")
        pt_hi_done, pt_lo_done, pt_used = sem("pt_hi_done"), sem("pt_lo_done"), sem("pt_used")
        o_hi_done, o_lo_done = sem("o_hi_done"), sem("o_lo_done")
        C_TRANS, C_PTLO, C_PTUSED, C_OLO = 2 * TT, 2, TT, 1

        def rows(w):
            return w.rearrange("l (k p) n -> l p k n", p=P)

        def gain(l, c):
            return gains[:, bass.ds(l * VECS + c, 1)]

        def pairs_of(buf, width):
            return buf[:, 0:8 * width].rearrange("p (k n) -> p k n", n=width)


        def chunk_start(c):
            return sum(CHUNKS[:c]) + c * DT // 2

        def used_at(p):
            if p < PAIR_MIX:
                return 2 * p + 2
            if p < PAIR_OUT:
                return [GROUP_MIX + 2, GROUP_MIX + 4, GROUP_MIX + 6, GROUP_MIX + 8, GROUP_UV, GROUP_UQ,
                        GROUP_POOL, GROUP_OUT][p - PAIR_MIX]
            return (GROUP_OUT if p < PAIR_FFN2 else GROUP_FFN2) + 2 * (p - (PAIR_OUT if p < PAIR_FFN2 else PAIR_FFN2)) + 2

        def split_parts(p, raw, split):
            if not isinstance(p, int) or p not in (PAIR_MIX + 6, PAIR_MIX + 7):
                return [(raw[:, :], split[:, :])]
            slots = 2 if p == PAIR_MIX + 6 else 1
            v_raw, v_split = (b[:, 0:1024 * slots].rearrange("p (k n) -> p k n", k=slots) for b in (raw, split))
            heads = v_raw[:, :, 0:HEADS * QK].rearrange("p k (h n) -> p k h n", n=QK)
            out = []
            for a, b, c0 in ((0, QK_NOPE, 0), (QK_NOPE, QK, HEADS * QK_NOPE)):
                dst = v_split[:, :, c0:c0 + HEADS * (b - a)].rearrange("p k (h n) -> p k h n", n=b - a)
                out.append((heads[:, :, :, a:b], dst))
            if slots == 1:
                out.append((raw[:, 1024:1024 + PG * P], split[:, 1024:1024 + PG * P]))
            return out

        def wait_x(eng, l, n, d):
            if n == 0:
                eng.wait_ge(x_done, d + 1)
            else:
                end = (GROUP_MIX, GROUP_FFN2, GROUPS)[n - 1]
                eng.wait_ge(evac_done, l * GROUPS + end - DT + d + 1 + BANKS)

        pooled = [place(f"pooled{i}", [P, S], F32, at_a + (4 + 2 * i) * TB)[0] for i in range(2)]

        block = ctx.enter_context(nc.Block())

        @block.sync
        def _(sp):
            for t in range(TT):
                sp.dma_start(x_tok[:, t, :], x_in[0, t * P:(t + 1) * P, :]).then_inc(x_loaded, 16)
            sp.dma_start(cos_t[:, :], rope_cos).then_inc(const_loaded, 16)
            sp.dma_start(sin_t[:, :], rope_sin).then_inc(const_loaded, 16)
            sp.dma_start(edge[:, :, :].rearrange("p g n -> p (g n)"), pool_edge).then_inc(const_loaded, 16)

            def wait_free(l, p):
                sp.wait_ge(hi_split, l * PAIRS + p + 1)
                sp.wait_ge(lo_split, l * PAIRS + p + 1)

            def load_columns(l, p, b, w, r0, blocks, col, width=256):
                wait_free(l, p)
                half = blocks // 2
                dst = pairs_of(w_raw[b], width)
                for k in (0, half):
                    sp.dma_start(dst[:, k:k + half, :],
                                 rows(w)[l, :, r0 + k:r0 + k + half, col]).then_inc(raw_loaded[b], 16)

            def load_ffn(l, p0, w_gu, w_down):
                for c, n in enumerate(CHUNKS):
                    pc, f0 = p0 + chunk_start(c), P * sum(CHUNKS[:c])
                    with sp.Fori(0, n // 2) as i:
                        load_columns(l, pc + 2 * i, 0, w_gu, 0, DT, bass.ds(f0 + 256 * i, 256))
                        load_columns(l, pc + 2 * i + 1, 1, w_gu, 0, DT, bass.ds(F + f0 + 256 * i, 256))
                    with sp.Fori(0, DT // 4) as i:
                        for b in range(2):
                            load_columns(l, pc + n + 2 * i + b, b, w_down, f0 // P, n,
                                         bass.ds(512 * i + 256 * b, 256))

            with sp.Fori(0, DEPTH) as l:
                load_ffn(l, 0, ffn1_w_gu, ffn1_w_down)
                p = PAIR_MIX
                for col, width in ((0, 256), (256, 256), (512, 160), (O_POOL, 256), (O_POOL + 256, 256)):
                    load_columns(l, p, p % RING, w_in, 0, DT, slice(col, col + width), width)
                    p += 1
                wait_free(l, p)
                sp.dma_start(w_raw[p % RING][:, 0:1024].rearrange("p (k n) -> p k n", k=KT),
                             rows(w_uv)[l]).then_inc(raw_loaded[p % RING], 16)
                sp.dma_start(w_raw[p % RING][:, 1024:2048].rearrange("p (k n) -> p k n", k=KT),
                             rows(w_uk)[l]).then_inc(raw_loaded[p % RING], 16)
                p += 1
                wait_free(l, p)
                for k in range(2):
                    sp.dma_start(w_raw[p % RING][:, 1024 * k:1024 * k + HEADS * QK],
                                 rows(w_uq)[l, :, k, :]).then_inc(raw_loaded[p % RING], 16)
                p += 1
                wait_free(l, p)
                sp.dma_start(w_raw[p % RING][:, 0:HEADS * QK], rows(w_uq)[l, :, 2, :]).then_inc(raw_loaded[p % RING], 16)
                sp.dma_start(w_raw[p % RING][:, 1024:1024 + PG * P].rearrange("p (g n) -> p g n", g=PG),
                             w_pool.rearrange("l g c d -> l c g d")[l]).then_inc(raw_loaded[p % RING], 16)
                with sp.Fori(0, OUT_PAIRS // 2) as i:
                    for b in range(2):
                        load_columns(l, PAIR_OUT + 2 * i + b, b, w_out, 0, DT, bass.ds(512 * i + 256 * b, 256))
                load_ffn(l, PAIR_FFN2, ffn2_w_gu, ffn2_w_down)
            for t in range(TT):
                sp.wait_ge(y_copied, 2 * t + 2)
                sp.dma_start(y_out[0, t * P:(t + 1) * P, :], y_tok[:, t, :]).then_inc(y_stored, 16)
            sp.wait_ge(y_stored, 16 * TT)

        @block.scalar
        def _(act):
            act.sem_inc(hi_split, RING)
            act.wait_ge(memset_done, 1)
            for l in range(DEPTH):
                r = l * VECS
                for v, w, n in ((V_FFN1, ffn1_norm, DT), (V_MIX, mix_norm, DT), (V_FFN2, ffn2_norm, DT),
                                (V_QL, q_lat_norm, QT), (V_KVL, kv_lat_norm, KT), (V_PS, pool_scale, PG)):
                    act.dma_start(gain_rows[r + v:r + v + n, :], w[l].rearrange("(k p) -> k p", p=P)).then_inc(gains_t, 16)
                for v, w in ((V_QN, q_norm), (V_KN, k_norm)):
                    act.dma_start(gain_rows[r + v:r + v + 1, 0:QK_NOPE], w[l:l + 1, 0:QK_NOPE]).then_inc(gains_t, 16)
                for j in range(P // QK_ROPE):
                    act.dma_start(gain_rows[r + V_QPE:r + V_QPE + 1, j * QK_ROPE:(j + 1) * QK_ROPE],
                                  q_norm[l:l + 1, QK_NOPE:QK]).then_inc(gains_t, 16)
                act.dma_start(gain_rows[r + V_KPE:r + V_KPE + 1, QK_NOPE:QK],
                              k_norm[l:l + 1, QK_NOPE:QK]).then_inc(gains_t, 16)
            act.dma_start(gain_rows[DEPTH * VECS:VROWS, :], ffn1_norm[0].rearrange("(k p) -> k p", p=P)).then_inc(gains_t, 16)

            def split_hi(l, b, loaded, used, p=0):
                act.wait_ge(raw_loaded[b], l * (16 * PAIRS) + loaded)
                if used is not None:
                    act.wait_ge(acc_done, l * GROUPS + used)
                for src, dst in split_parts(p, w_raw[b], w_hi[b]):
                    last = nc.scalar.activation(dst, src, ACT.Copy)
                last.then_inc(hi_split, 1)

            def split_hi_at(l, p):
                split_hi(l, p % RING, 32 * (p // RING + 1), used_at(p - RING) if p >= RING else None, p)

            def rms(l, n, dst, width):
                act.wait_ge(sums_done, l * NORMS + n + 1)
                nc.scalar.activation(dst[:, :], bank[SUMS][:, :], ACT.Sqrt, bias=eps_t[:, 0:1],
                                     scale=1.0 / width).then_inc(rms_done, 1)

            def gain_x(l, n, v, d):
                wait_x(act, l, n, d)
                nc.scalar.activation(xg_hi[:, d, :], x[:, d, :], ACT.Copy, scale=gain(l, v + d)).then_inc(xg_hi_done, 1)

            def ffn(l, which, p0, g0, norm, next_norm, next_v, last):
                for c, n in enumerate(CHUNKS):
                    pc = p0 + chunk_start(c)
                    f0 = which * FT + sum(CHUNKS[:c])

                    def gate_up(i):
                        g = g0 + 2 * (pc - p0) + 4 * i
                        for j in range(2):
                            act.wait_ge(evac_done, l * GROUPS + g + j + 1 + BANKS)
                            nc.scalar.activation(silu[j][:, :], gate[j][:, :], ACT.Silu).then_inc(silu_done, 1)
                        split_hi(l, 0, 16 * (pc + 2 * i + 2) + 32, g + 2)
                        for j in range(2):
                            act.wait_ge(hid_done, l * 2 * FT + f0 + 2 * i + j + 1)
                            nc.scalar.activation(h_hi[:, bass.ds(2 * i + j, 1), :], hid[j][:, :].rearrange("p (o s) -> p o s", o=1),
                                                 ACT.Copy).then_inc(h_hi_done, 1)
                        split_hi(l, 1, 16 * (pc + 2 * i + 2) + 32, g + 4)

                    if c == 0:
                        rms(l, norm, rstd_x, D)
                    with act.Fori(0, n // 2) as i:
                        gate_up(i)
                    pd = pc + n
                    if c < len(CHUNKS) - 1:
                        with act.Fori(0, DT // 4) as i:
                            for b in range(2):
                                split_hi(l, b, 16 * (pd + 2 * i + 2) + 32, g0 + 2 * (pd - p0) + 4 * i + 2 * b + 2)
                    else:
                        finish_x(l, pd, next_norm, next_v, last)

            def finish_x(l, pd, next_norm, next_v, last=False, late=False):
                for i in range(DT // 2):
                    for d in (2 * i, 2 * i + 1):
                        if not late:
                            gain_x(l, next_norm, next_v, d)
                    if not (last and i >= DT // 2 - RING):
                        split_hi_at(l, pd + i + 2)
                if late:
                    wait_x(act, l, next_norm, DT - 1)
                    for d in range(DT):
                        gain_x(l, next_norm, next_v, d)

            act.wait_ge(gains_done, 1)
            act.wait_ge(memset_done, 2)
            for d in range(DT):
                gain_x(0, 0, V_FFN1, d)
            with act.Fori(0, DEPTH) as l:
                for p in range(RING):
                    split_hi_at(l, p)
                ffn(l, 0, 0, 0, N_FFN1, 1, V_MIX, False)

                rms(l, N_MIX, rstd_x, D)
                for p in (PAIR_MIX + 2, PAIR_MIX + 3, PAIR_MIX + 4):
                    split_hi_at(l, p)
                for n, t0, width in ((N_QL, 0, QT), (N_KVL, QT, KT)):
                    rms(l, n, rstd_l, width * P)
                    for t in range(t0, t0 + width):
                        act.wait_ge(lat_scaled, l * (QT + KT) + t + 1)
                        nc.scalar.activation(h_hi[:, t, :], z[:, t, :], ACT.Copy, scale=gain(l, V_QL + t)).then_inc(lat_hi, 1)
                for p in (PAIR_MIX + 5, PAIR_MIX + 6):
                    split_hi_at(l, p)
                act.wait_ge(acc_done, l * GROUPS + GROUP_UV)
                act.wait_ge(k_rope_done, l + 1)
                for i in range(2):
                    nc.scalar.activation(sq_k[i][QK_NOPE:QK, :], k_pe[QK_NOPE:QK, :], ACT.Square).then_inc(k_filled, 1)
                nc.scalar.activation(k_all[QK_NOPE:QK, :, :],
                                     k_rot[QK_NOPE:QK, :].rearrange("p (o s) -> p o s", o=1).to_broadcast([QK_ROPE, HEADS, S]),
                                     ACT.Copy).then_inc(k_filled, 1)
                split_hi_at(l, PAIR_MIX + 7)
                for g in range(PG):
                    act.wait_ge(mixed_done, l * PG + g + 1)
                    dst = h_hi[:, QT + KT + g, :] if g < 3 else v_hi[:, :, :].rearrange("p t n -> p (t n)")
                    nc.scalar.activation(dst, zp[:, g, PAD:PAD + S], ACT.Copy).then_inc(mixed_hi, 1)
                split_hi_at(l, PAIR_MIX + 8)

                def head_root(e):
                    act.wait_ge(head_sums, l * 16 + e + 1)
                    if e >= 2:
                        act.wait_ge(head_normed, l * 16 + e - 1)
                    nc.scalar.activation(head_rms[e % 2][0:QK, :], bank[SUMS + e % 2][0:QK, :], ACT.Sqrt,
                                         bias=eps_t[0:QK, 0:1], scale=1.0 / QK).then_inc(head_rms_done, 1)

                for e in range(HEADS):
                    head_root(e)
                for g in range(PG):
                    act.wait_ge(evac_done, l * GROUPS + GROUP_POOL + g + 1 + BANKS)
                    nc.scalar.activation(xg_hi[:, CAT + g, :], pooled[g % 2][:, :], ACT.Copy).then_inc(pooled_hi, 1)
                split_hi_at(l, PAIR_MIX + 9)

                def square_pe(h):
                    j = h % 4
                    if h >= 2:
                        act.wait_ge(head_sums, l * 16 + HEADS + h - 1)
                    nc.scalar.activation(sq_q[h % 2][QK_NOPE:QK, :], q_pe[32 * j:32 * j + 32, h // 4, :],
                                         ACT.Square).then_inc(q_sq_pe, 1)

                act.wait_ge(q_rope_done, 2 * l + 2)
                for h in range(HEADS):
                    j = h % 4
                    nc.scalar.activation(q_all[QK_NOPE:QK, h, :], q_rope[32 * j:32 * j + 32, h // 4, :],
                                         ACT.Copy).then_inc(q_filled, 1)
                    square_pe(h)
                    if h >= 1:
                        head_root(HEADS + h - 1)
                head_root(2 * HEADS - 1)

                def split_qk(h, s):
                    ix = slice(h, h + 1) if isinstance(h, int) else bass.ds(h, 1)
                    for src, o in ((q_all, 0), (k_all, 2)):
                        last = nc.scalar.activation(h_hi[0:QK, o + s:o + s + 1, :], src[0:QK, ix, :], ACT.Copy)
                    last.then_inc(qk_hi, 1)

                def exponent(h, s, t):
                    act.wait_ge(neg_done, l * 32 + 4 * h + t + 1)
                    act.wait_ge(trans_done, l * 32 + 4 * h + 4)
                    nc.scalar.activation(prob[:, s, t, :], bank[t][:, :], ACT.Exp, bias=neg_max[:, s, t:t + 1],
                                         scale=SCALE, accum_out=row_sum[:, s, t:t + 1]).then_inc(exp_done, 1)

                def prob_t_hi(h, t):
                    act.wait_ge(trans_done, l * 32 + 4 * h + t + 1 + C_TRANS)
                    act.wait_ge(pt_used, l * 32 + 4 * h + t + 1)
                    nc.scalar.activation(h_hi[:, 4 + t, :], bank[TRANS + t % 2][:, :], ACT.Copy).then_inc(pt_hi_done, 1)

                def head_pair(hp, last):
                    for s in range(2):
                        h = 2 * hp + s
                        if not last:
                            act.wait_ge(scores_done, l * 32 + 4 * h + 4)
                            split_qk(h + 2, s)
                        for t in range(TT):
                            if not (last and s == 1):
                                exponent(h + 1, 1 - s, t)
                            if t == 2 and s == 0:
                                act.wait_ge(pt_used, l * 32 + 8 * hp + C_PTUSED)
                                nc.scalar.activation(v_hi[:, :, :], v_all[:, :, bass.ds(P * hp, P)],
                                                     ACT.Copy).then_inc(v_hi_done, 1)
                            prob_t_hi(h, t)
                        act.wait_ge(pt_used, l * 32 + 4 * h + 4 + C_PTUSED)
                        nc.scalar.activation(xg_hi[64 * s:64 * s + 64, bass.ds(hp, 1), :],
                                             bank[OUT][64 * s:64 * s + 64, :].rearrange("p (o s) -> p o s", o=1),
                                             ACT.Copy).then_inc(o_hi_done, 1)

                act.wait_ge(head_normed, l * 16 + 16)
                for h in range(2):
                    split_qk(h, h)
                for t in range(TT):
                    exponent(0, 0, t)
                with act.Fori(0, HEADS // 2 - 1) as hp:
                    head_pair(hp, False)
                head_pair(HEADS // 2 - 1, True)

                finish_x(l, PAIR_OUT, 2, V_FFN2, late=True)
                ffn(l, 1, PAIR_FFN2, GROUP_FFN2, N_FFN2, 3, VECS + V_FFN1, True)

        @block.tensor
        def _(pe):
            pe.sem_inc(trans_done, C_TRANS)
            pe.sem_inc(pt_used, C_PTUSED)
            pe.wait_ge(memset_done, 2)
            pe.wait_ge(ident_done, 1)
            pe.wait_ge(gains_t, 16 * (13 * DEPTH + 1))
            nc.tensor.transpose(bank[SUMS][:, 0:P], gain_rows[:, :], ident[:, :]).then_inc(x_turned, 1)
            pe.wait_ge(x_loaded, 16 * TT)
            for d in range(DT):
                if d >= BANKS:
                    pe.wait_ge(x_done, d - BANKS + 1)
                for t in range(TT):
                    last = nc.tensor.transpose(bank[d % BANKS][:, t * P:(t + 1) * P], x_tok[:, t, d * P:(d + 1) * P], ident[:, :])
                last.then_inc(x_turned, 1)
            pe.wait_ge(x_done, DT)

            def mm3(out, whi, wlo, xhi, xlo, first, last):
                nc.tensor.matmul(out, whi, xhi, start=first, stop=False)
                nc.tensor.matmul(out, whi, xlo, start=False, stop=False)
                return nc.tensor.matmul(out, wlo, xhi, start=False, stop=last)

            def wait_pair(l, p):
                pe.wait_ge(lo_split, l * PAIRS + p + 1 + RING)

            def wait_bank(l, g):
                pe.wait_ge(evac_done, l * GROUPS + g + 1)

            def sums(l, n, src):
                pe.wait_ge(sumsq_done, l * NORMS + n + 1)
                if n == N_KVL:
                    pe.wait_ge(rms_done, l * NORMS + n)
                nc.tensor.matmul(bank[SUMS][:, :], ones[:, :], src[:, :], start=True, stop=True).then_inc(sums_done, 1)

            def column_tile(l, g, bk, b, c0, width, hi, lo, order, ready, blocks=DT, cols=P):
                wait_bank(l, g)
                whi, wlo = pairs_of(w_hi[b], width), pairs_of(w_lo[b], width)
                for n, k in enumerate(order):
                    ready(k)
                    last = mm3(bank[bk][0:cols, :], whi[:, k, c0:c0 + cols], wlo[:, k, c0:c0 + cols],
                               hi[:, k, :], lo[:, k, :], n == 0, n == blocks - 1)
                return last.then_inc(acc_done, 1)

            def wait_xg(l, n):
                def ready(k):
                    pe.wait_ge(xg_lo_done, (3 * l + n) * DT + k + 1)
                return ready

            def nothing(k):
                pass

            def ffn(l, which, p0, g0, norm, x_norm):
                for c, n in enumerate(CHUNKS):
                    pc, gc = p0 + chunk_start(c), g0 + 2 * chunk_start(c)
                    f0 = which * FT + sum(CHUNKS[:c])

                    def gate_up(i, first):
                        for b in range(2):
                            wait_pair(l, pc + 2 * i + b)
                            for j in range(2):
                                column_tile(l, gc + 4 * i + 2 * b + j, 2 * b + j, b, P * j, 256, xg_hi, xg_lo,
                                                   range(DT), wait_xg(l, x_norm) if first and b + j == 0 else nothing)
                                if first and b + j == 0:
                                    sums(l, norm, sumsq_x)

                    if c == 0:
                        gate_up(0, True)
                    with pe.Fori(1 if c == 0 else 0, n // 2) as i:
                        gate_up(i, False)

                    def wait_h(k):
                        pe.wait_ge(h_lo_done, l * 2 * FT + f0 + k + 1)

                    with pe.Fori(0, DT // 4) as i:
                        for b in range(2):
                            wait_pair(l, pc + n + 2 * i + b)
                            for j in range(2):
                                column_tile(l, gc + 2 * n + 4 * i + 2 * b + j, 2 * b + j, b, P * j, 256, h_hi, h_lo,
                                            range(n), wait_h if b + j == 0 else nothing, blocks=n)

            with pe.Fori(0, DEPTH) as l:
                ffn(l, 0, 0, 0, N_FFN1, 0)

                g = GROUP_MIX
                for p, tiles in ((0, ((0, 256), (P, 256))), (1, ((0, 256), (P, 256))), (2, ((0, 160), (64, 160))),
                                 (3, ((0, 256), (P, 256))), (4, ((0, 256), (P, 256)))):
                    wait_pair(l, PAIR_MIX + p)
                    for j, (c0, width) in enumerate(tiles):
                        cols = QK if (p, j) == (2, 1) else P
                        column_tile(l, g, g % BANKS, (PAIR_MIX + p) % RING, c0, width, xg_hi, xg_lo, range(DT),
                                    wait_xg(l, 1) if g == GROUP_MIX else nothing, cols=cols)
                        if g == GROUP_MIX:
                            sums(l, N_MIX, sumsq_x)
                        if g == GROUP_MIX + 6:
                            sums(l, N_QL, sumsq_l[0])
                        if g == GROUP_MIX + 7:
                            sums(l, N_KVL, sumsq_l[1])
                        g += 1

                b = (PAIR_MIX + 5) % RING
                wait_pair(l, PAIR_MIX + 5)
                pe.wait_ge(lat_lo, l * (QT + KT) + QT + KT)
                for t in range(TT):
                    wait_bank(l, GROUP_UV + t)
                    for k in range(KT):
                        c_hi, c_lo = (h[:, QT + k, t * P:(t + 1) * P] for h in (h_hi, h_lo))
                        wv_hi, wv_lo = (w[b][:, 512 * k:512 * k + 512] for w in (w_hi, w_lo))
                        last = mm3(bank[(GROUP_UV + t) % BANKS][:, :], c_hi, c_lo, wv_hi, wv_lo, k == 0, k == KT - 1)
                    last.then_inc(acc_done, 1)
                for r in range(4):
                    wait_bank(l, GROUP_UK + r)
                    for k in range(KT):
                        c0 = 1024 + 512 * k + P * r
                        last = mm3(bank[(GROUP_UK + r) % BANKS][:, :], w_hi[b][:, c0:c0 + P], w_lo[b][:, c0:c0 + P],
                                   h_hi[:, QT + k, :], h_lo[:, QT + k, :], k == 0, k == KT - 1)
                    last.then_inc(acc_done, 1)

                b0, b1 = (PAIR_MIX + 6) % RING, (PAIR_MIX + 7) % RING

                def uq(k, r):
                    bb, c0 = (b0, 1024 * k) if k < 2 else (b1, 0)
                    return [w[bb][:, c0 + P * r:c0 + P * r + P] for w in (w_hi, w_lo)]

                wait_pair(l, PAIR_MIX + 6)
                for k in range(QT):
                    if k == 2:
                        wait_pair(l, PAIR_MIX + 7)
                    for r in range(4):
                        if k == 0:
                            wait_bank(l, GROUP_UQ + r)
                        last = mm3(bank[(GROUP_UQ + r) % BANKS][:, :], *uq(k, r), h_hi[:, k, :], h_lo[:, k, :], k == 0, k == QT - 1)
                        if k == QT - 1:
                            last.then_inc(acc_done, 1)
                for r in (4, 5):
                    wait_bank(l, GROUP_UQ + r)
                    for k in range(QT):
                        last = mm3(bank[(GROUP_UQ + r) % BANKS][:, :], *uq(k, r), h_hi[:, k, :], h_lo[:, k, :], k == 0, k == QT - 1)
                    last.then_inc(acc_done, 1)

                def head_sum(e):
                    pe.wait_ge(head_sq, l * 16 + e + 1)
                    if e >= 2:
                        pe.wait_ge(head_rms_done, l * 16 + e - 1)
                    if e < HEADS:
                        pe.wait_ge(k_filled, 3 * l + 3)
                    else:
                        pe.wait_ge(q_sq_pe, l * HEADS + e - HEADS + 1)
                    sq = sq_k if e < HEADS else sq_q
                    nc.tensor.matmul(bank[SUMS + e % 2][0:QK, :], ones[0:QK, 0:QK], sq[e % 2][0:QK, :],
                                     start=True, stop=True).then_inc(head_sums, 1)

                for e in range(HEADS):
                    head_sum(e)

                for g in range(PG):
                    wait_bank(l, GROUP_POOL + g)
                    pe.wait_ge(mixed_lo, l * PG + g + 1)
                    m_hi = h_hi[:, QT + KT + g, :] if g < 3 else v_hi[:, :, :].rearrange("p t n -> p (t n)")
                    m_lo = h_lo[:, QT + KT + g, :] if g < 3 else v_lo[:, :, :].rearrange("p t n -> p (t n)")
                    c0 = 1024 + P * g
                    mm3(bank[(GROUP_POOL + g) % BANKS][:, :], w_hi[b1][:, c0:c0 + P], w_lo[b1][:, c0:c0 + P],
                        m_hi, m_lo, True, True).then_inc(acc_done, 1)
                for e in range(HEADS, 2 * HEADS):
                    head_sum(e)

                def scores(h, s, first=False):
                    pe.wait_ge(qk_lo, l * 8 + h + 1)
                    for t in range(TT):
                        if first:
                            wait_bank(l, GROUP_OUT + t)
                        else:
                            pe.wait_ge(exp_done, l * 32 + 4 * h - 4 + t + 1)
                        mm3(bank[t][:, :], h_hi[0:QK, s, t * P:(t + 1) * P], h_lo[0:QK, s, t * P:(t + 1) * P],
                            h_hi[0:QK, 2 + s, :], h_lo[0:QK, 2 + s, :], True, True).then_inc(scores_done, 1)

                def weigh(h, s, hp):
                    for t in range(TT):
                        pe.wait_ge(pt_lo_done, l * 32 + 4 * h + t + 1)
                        for q in range(TT):
                            if t == 0:
                                pe.wait_ge(prob_done, l * 32 + 4 * h + q + 1)
                            last = nc.tensor.transpose(bank[TRANS + t % 2][:, q * P:(q + 1) * P],
                                                       prob[:, s, q, t * P:(t + 1) * P], ident[:, :])
                        last.then_inc(trans_done, 1)
                        if t >= 1:
                            values(h, s, hp, t - 1)
                    values(h, s, hp, TT - 1)

                def values(h, s, hp, t):
                    pe.wait_ge(pt_lo_done, l * 32 + 4 * h + t + 1 + C_PTLO)
                    if t == 0:
                        pe.wait_ge(o_lo_done, l * 8 + h + 1)
                        if s == 0:
                            pe.wait_ge(v_lo_done, l * 4 + hp + 1)
                    nc.tensor.matmul(bank[OUT][:, :], v_hi[:, t, :], h_hi[:, 4 + t, :], start=t == 0, stop=False)
                    nc.tensor.matmul(bank[OUT][:, :], v_lo[:, t, :], h_hi[:, 4 + t, :], start=False, stop=False)
                    last = nc.tensor.matmul(bank[OUT][:, :], v_hi[:, t, :], h_lo[:, 4 + t, :], start=False, stop=t == TT - 1)
                    last.then_inc(pt_used, 1)

                scores(0, 0, True)

                def head_pair(hp, last):
                    scores(2 * hp + 1, 1)
                    weigh(2 * hp, 0, hp)
                    if not last:
                        scores(2 * hp + 2, 0)
                    weigh(2 * hp + 1, 1, hp)

                with pe.Fori(0, HEADS // 2 - 1) as hp:
                    head_pair(hp, False)
                head_pair(HEADS // 2 - 1, True)

                def wait_cat(k):
                    if k < CAT:
                        pe.wait_ge(o_lo_done, l * 8 + 2 * k + 2 + C_OLO)
                    else:
                        pe.wait_ge(pooled_lo, l * PG + k - CAT + 1)

                with pe.Fori(0, OUT_PAIRS // 2) as i:
                    for b in range(2):
                        wait_pair(l, PAIR_OUT + 2 * i + b)
                        for j in range(2):
                            column_tile(l, GROUP_OUT + 4 * i + 2 * b + j, 2 * b + j, b, P * j, 256, xg_hi, xg_lo,
                                        (4, 5, 6, 7, 0, 1, 2, 3), wait_cat if b + j == 0 else nothing)
                ffn(l, 1, PAIR_FFN2, GROUP_FFN2, N_FFN2, 2)

            pe.wait_ge(evac_done, DEPTH * GROUPS + BANKS)
            for n in range(2 * TT):
                t, half = n // 2, n % 2
                if n >= BANKS:
                    pe.wait_ge(y_copied, n - BANKS + 1)
                for d in range(4):
                    last = nc.tensor.transpose(bank[n % BANKS][:, d * P:(d + 1) * P], x[:, 4 * half + d, t * P:(t + 1) * P], ident[:, :])
                last.then_inc(y_turned, 1)

        @block.vector
        def _(dve):
            V = nc.vector
            dve.sem_inc(evac_done, BANKS)
            dve.sem_inc(lo_split, RING)
            dve.sem_inc(pt_lo_done, C_PTLO)
            dve.sem_inc(o_lo_done, C_OLO)
            V.memset(gain_rows[:, :], 1.0).then_inc(memset_done, 1)
            V.memset(ones[:, :], 1.0)
            V.memset(eps_t[:, :], EPS).then_inc(memset_done, 1)
            dve.wait_ge(x_turned, 1)
            V.tensor_copy(gains[:, :], bank[SUMS][:, 0:P]).then_inc(gains_done, 1)
            for d in range(DT):
                dve.wait_ge(x_turned, d + 2)
                V.tensor_copy(x[:, d, :], bank[d % BANKS][:, :]).then_inc(x_done, 1)
            dve.wait_ge(gains_done, 1)

            def gain_x(l, n, v, d):
                dve.wait_ge(xg_hi_done, (3 * l + n) * DT + d + 1)
                wait_x(dve, l, n, d)
                V.scalar_tensor_tensor(out=xg_lo[:, d, :], in0=x[:, d, :], scalar=gain(l, v + d),
                                       in1=xg_hi[:, d, :].bitcast(F32), op0=ALU.mult, op1=ALU.subtract).then_inc(xg_lo_done, 1)

            def split_lo(l, p, b):
                dve.wait_ge(hi_split, l * PAIRS + p + 1 + RING)
                for (src, dst), (_, hi) in zip(split_parts(p, w_raw[b], w_lo[b]), split_parts(p, w_raw[b], w_hi[b])):
                    last = V.tensor_tensor(dst, src, hi.bitcast(F32), ALU.subtract)
                last.then_inc(lo_split, 1)

            def split_lo_at(l, p):
                split_lo(l, p, p % RING)

            def wait_group(l, g):
                dve.wait_ge(acc_done, l * GROUPS + g + 1)
                dve.wait_ge(evac_done, l * GROUPS + g + BANKS)

            def rstd(l, n, dst):
                dve.wait_ge(rms_done, l * NORMS + n + 1)
                V.reciprocal(dst[:, :], dst[:, :]).then_inc(rstd_done, 1)

            def wait_rstd(l, n):
                dve.wait_ge(rstd_done, l * NORMS + n + 1)

            def add_to_x(l, g, bk, d, factor):
                wait_group(l, g)
                xd = x[:, d, :] if isinstance(d, int) else x[:, bass.ds(d, 1), :]
                ps = bank[bk][:, :] if isinstance(d, int) else bank[bk][:, :].rearrange("p (o s) -> p o s", o=1)
                V.scalar_tensor_tensor(out=xd, in0=ps, scalar=factor, in1=xd, op0=ALU.mult, op1=ALU.add).then_inc(evac_done, 1)

            def finish_x(l, pd, gd, factor, next_norm, next_v, last=False, late=False):
                for i in range(DT // 2):
                    for d in (2 * i, 2 * i + 1):
                        add_to_x(l, gd + d, d % BANKS, d, factor)
                        if not late:
                            gain_x(l, next_norm, next_v, d)
                    if not (last and i >= DT // 2 - RING):
                        split_lo_at(l, pd + i + 2)
                if late:
                    for d in range(DT):
                        gain_x(l, next_norm, next_v, d)

            def ffn(l, which, p0, g0, norm, next_norm, next_v, last):
                for c, n in enumerate(CHUNKS):
                    pc, gc = p0 + chunk_start(c), g0 + 2 * chunk_start(c)
                    f0 = which * FT + sum(CHUNKS[:c])
                    if c == 0:
                        rstd(l, norm, rstd_x)
                    with dve.Fori(0, n // 2) as i:
                        wait_rstd(l, norm)
                        for j in range(2):
                            wait_group(l, gc + 4 * i + j)
                            V.tensor_tensor(gate[j][:, :], bank[j][:, :], rstd_x[:, :], ALU.mult).then_inc(evac_done, 1)
                        split_lo(l, pc + 2 * i + 2, 0)
                        for j in range(2):
                            f = l * 2 * FT + f0 + 2 * i + j
                            wait_group(l, gc + 4 * i + 2 + j)
                            V.tensor_tensor(up[j][:, :], bank[2 + j][:, :], rstd_x[:, :], ALU.mult).then_inc(evac_done, 1)
                            dve.wait_ge(evac_done, l * GROUPS + gc + 4 * i + 3 + j + BANKS)
                            dve.wait_ge(silu_done, f + 1)
                            V.tensor_tensor(hid[j][:, :], silu[j][:, :], up[j][:, :], ALU.mult).then_inc(hid_done, 1)
                            dve.wait_ge(h_hi_done, f + 1)
                            dve.wait_ge(hid_done, f + 1)
                            o1 = "p (o s) -> p o s"
                            V.tensor_tensor(h_lo[:, bass.ds(2 * i + j, 1), :], hid[j][:, :].rearrange(o1, o=1),
                                            h_hi[:, bass.ds(2 * i + j, 1), :].bitcast(F32), ALU.subtract).then_inc(h_lo_done, 1)
                        split_lo(l, pc + 2 * i + 3, 1)
                    pd, gd = pc + n, gc + 2 * n
                    if c < len(CHUNKS) - 1:
                        with dve.Fori(0, DT // 4) as i:
                            for b in range(2):
                                for j in range(2):
                                    add_to_x(l, gd + 4 * i + 2 * b + j, 2 * b + j, 4 * i + 2 * b + j, 0.5)
                                split_lo(l, pd + 2 * i + b + 2, b)
                    else:
                        finish_x(l, pd, gd, 0.5, next_norm, next_v, last)

            for d in range(DT):
                gain_x(0, 0, V_FFN1, d)
            dve.wait_ge(const_loaded, 48)
            swap = [(i + 16) % 32 for i in range(32)]
            with dve.Fori(0, DEPTH) as l:
                step = [0]

                def link(ins):
                    step[0] += 1
                    ins.then_inc(dve_step, 1)
                    dve.wait_ge(dve_step, l * DVE_STEPS + step[0])

                for p in range(RING):
                    split_lo_at(l, p)
                ffn(l, 0, 0, 0, N_FFN1, 1, V_MIX, False)

                rstd(l, N_MIX, rstd_x)
                wait_rstd(l, N_MIX)
                M = GROUP_MIX

                def scale_group(m, dst, rows=slice(0, P)):
                    wait_group(l, M + m)
                    V.tensor_tensor(dst, bank[(M + m) % BANKS][rows, :], rstd_x[rows, :], ALU.mult).then_inc(evac_done, 1)

                scale_group(0, z[:, 0, :])
                scale_group(1, z[:, 1, :])
                split_lo_at(l, PAIR_MIX + 2)
                scale_group(2, z[:, 2, :])
                scale_group(3, z[:, 3, :])
                split_lo_at(l, PAIR_MIX + 3)
                scale_group(4, z[:, 4, :])
                scale_group(5, k_pe[QK_NOPE:QK, :], slice(QK_NOPE, QK))
                split_lo_at(l, PAIR_MIX + 4)

                def latent(n, t0, width):
                    rstd(l, n, rstd_l)
                    wait_rstd(l, n)
                    for t in range(t0, t0 + width):
                        V.tensor_tensor(z[:, t, :], z[:, t, :], rstd_l[:, :], ALU.mult).then_inc(lat_scaled, 1)
                    for t in range(t0, t0 + width):
                        dve.wait_ge(lat_hi, l * (QT + KT) + t + 1)
                        dve.wait_ge(lat_scaled, l * (QT + KT) + t + 1)
                        V.scalar_tensor_tensor(out=h_lo[:, t, :], in0=z[:, t, :], scalar=gain(l, V_QL + t),
                                               in1=h_hi[:, t, :].bitcast(F32), op0=ALU.mult, op1=ALU.subtract).then_inc(lat_lo, 1)

                latent(N_QL, 0, QT)
                for side in (slice(0, PAD), slice(PAD + S, PW)):
                    V.memset(zp[:, :, side], 0.0)
                scale_group(6, zp[:, 0, PAD:PAD + S])
                latent(N_KVL, QT, KT)
                scale_group(7, zp[:, 1, PAD:PAD + S])
                split_lo_at(l, PAIR_MIX + 5)

                def rope(dst, src, g, scaled, tmp, rows):
                    link(V.tensor_scalar(scaled, src, g, None, ALU.mult))
                    src = scaled
                    V.tensor_tensor(dst, src, cos_t[rows, :], ALU.mult)
                    link(V.stream_shuffle(tmp, src, swap))
                    link(V.tensor_tensor(tmp, tmp, sin_t[rows, :], ALU.mult))
                    return V.tensor_tensor(dst, dst, tmp, ALU.add)

                R = slice(QK_NOPE, QK)
                rope(k_rot[R, :], k_pe[R, :], gains[R, bass.ds(l * VECS + V_KPE, 1)], rot_a[R, :], rot_b[R, :], R).then_inc(k_rope_done, 1)
                scale_group(8, zp[:, 2, PAD:PAD + S])
                scale_group(9, zp[:, 3, PAD:PAD + S])
                split_lo_at(l, PAIR_MIX + 6)

                def copy_group(g, *parts):
                    wait_group(l, g)
                    for dst, rows in parts:
                        last = V.tensor_copy(dst, bank[g % BANKS][rows, :])
                    last.then_inc(evac_done, 1)

                LOW, HIGH, ALL = slice(0, 64), slice(64, P), slice(0, P)
                for t in range(TT):
                    copy_group(GROUP_UV + t, (v_all[:, t, :], ALL))
                for r in range(4):
                    copy_group(GROUP_UK + r, (k_all[0:64, 2 * r, :], LOW), (k_all[0:64, 2 * r + 1, :], HIGH))
                split_lo_at(l, PAIR_MIX + 7)
                for g in range(PG):
                    dve.wait_ge(windowed, l * PG + g + 1)
                    V.scalar_tensor_tensor(out=zp[:, g, PAD:PAD + S], in0=win_s[:, PAD:PAD + S], scalar=0.5 ** (g + 1),
                                           in1=zp[:, g, PAD:PAD + S], op0=ALU.mult, op1=ALU.subtract).then_inc(mixed_done, 1)
                    dst = h_lo[:, QT + KT + g, :] if g < 3 else v_lo[:, :, :].rearrange("p t n -> p (t n)")
                    hi = h_hi[:, QT + KT + g, :] if g < 3 else v_hi[:, :, :].rearrange("p t n -> p (t n)")
                    dve.wait_ge(mixed_done, l * PG + g + 1)
                    dve.wait_ge(mixed_hi, l * PG + g + 1)
                    V.tensor_tensor(dst, zp[:, g, PAD:PAD + S], hi.bitcast(F32), ALU.subtract).then_inc(mixed_lo, 1)
                dve.wait_ge(mixed_lo, l * PG + PG)
                for r in range(4):
                    copy_group(GROUP_UQ + r, (q_all[0:64, 2 * r, :], LOW), (q_all[0:64, 2 * r + 1, :], HIGH))
                for r in range(2):
                    copy_group(GROUP_UQ + 4 + r, (q_pe[:, r, :], ALL))
                split_lo_at(l, PAIR_MIX + 8)

                def head_norm(e):
                    h = e % HEADS
                    raw = (k_all if e < HEADS else q_all)[0:QK, h, :]
                    dve.wait_ge(head_rms_done, l * 16 + e + 1)
                    V.reciprocal(head_rms[e % 2][0:QK, :], head_rms[e % 2][0:QK, :]).then_inc(head_inv, 1)
                    dve.wait_ge(head_inv, l * 16 + e + 1)
                    if e >= HEADS:
                        dve.wait_ge(q_filled, l * HEADS + h + 1)
                    v = V_KN if e < HEADS else V_QN
                    V.scalar_tensor_tensor(out=raw, in0=raw, scalar=gains[0:QK, bass.ds(l * VECS + v, 1)],
                                           in1=head_rms[e % 2][0:QK, :], op0=ALU.mult, op1=ALU.mult).then_inc(head_normed, 1)

                dve.wait_ge(evac_done, l * GROUPS + GROUP_POOL + BANKS)
                dve.wait_ge(k_filled, 3 * l + 3)
                for e in range(HEADS):
                    head_norm(e)
                for r in range(2):
                    rope(q_rope[:, r, :], q_pe[:, r, :], gain(l, V_QPE), rot_a[:, :], rot_b[:, :], ALL).then_inc(q_rope_done, 1)
                    dve.wait_ge(q_rope_done, 2 * l + r + 1)
                for g in range(PG):
                    wait_group(l, GROUP_POOL + g)
                    V.tensor_scalar(pooled[g % 2][:, :], bank[(GROUP_POOL + g) % BANKS][:, :], gain(l, V_PS + g), None,
                                    ALU.mult).then_inc(evac_done, 1)
                    dve.wait_ge(pooled_hi, l * PG + g + 1)
                    dve.wait_ge(evac_done, l * GROUPS + GROUP_POOL + g + 1 + BANKS)
                    V.tensor_tensor(xg_lo[:, CAT + g, :], pooled[g % 2][:, :], xg_hi[:, CAT + g, :].bitcast(F32),
                                    ALU.subtract).then_inc(pooled_lo, 1)
                split_lo_at(l, PAIR_MIX + 9)
                for e in range(HEADS, 2 * HEADS):
                    head_norm(e)

                def maximum(h, s, t):
                    dve.wait_ge(scores_done, l * 32 + 4 * h + t + 1)
                    V.reduce_max(row_max[:, s, t:t + 1], bank[t][:, :], AX_X).then_inc(max_done, 1)
                    dve.wait_ge(max_done, l * 32 + 4 * h + t + 1)
                    V.tensor_scalar(neg_max[:, s, t:t + 1], row_max[:, s, t:t + 1], -SCALE, None, ALU.mult).then_inc(neg_done, 1)

                def inverse(h, s, t):
                    dve.wait_ge(exp_done, l * 32 + 4 * h + t + 1)
                    V.reciprocal(row_inv[:, s, t:t + 1], row_sum[:, s, t:t + 1]).then_inc(inv_done, 1)

                def prob_t_lo(h, t):
                    dve.wait_ge(pt_hi_done, l * 32 + 4 * h + t + 1)
                    V.tensor_tensor(h_lo[:, 4 + t, :], bank[TRANS + t % 2][:, :], h_hi[:, 4 + t, :].bitcast(F32),
                                    ALU.subtract).then_inc(pt_lo_done, 1)

                def head_pair(hp, last):
                    for s in range(2):
                        h = 2 * hp + s
                        for t in range(TT):
                            if not (last and s == 1):
                                maximum(h + 1, 1 - s, t)
                            if t == 2 and s == 0:
                                dve.wait_ge(v_hi_done, l * 4 + hp + 1)
                                V.tensor_tensor(v_lo[:, :, :], v_all[:, :, bass.ds(P * hp, P)], v_hi[:, :, :].bitcast(F32),
                                                ALU.subtract).then_inc(v_lo_done, 1)
                            prob_t_lo(h, t)
                            if t >= 1 and not (last and s == 1):
                                inverse(h + 1, 1 - s, t - 1)
                        if not (last and s == 1):
                            inverse(h + 1, 1 - s, TT - 1)
                        dve.wait_ge(o_hi_done, l * 8 + h + 1)
                        V.tensor_tensor(xg_lo[64 * s:64 * s + 64, bass.ds(hp, 1), :],
                                        bank[OUT][64 * s:64 * s + 64, :].rearrange("p (o s) -> p o s", o=1),
                                        xg_hi[64 * s:64 * s + 64, bass.ds(hp, 1), :].bitcast(F32),
                                        ALU.subtract).then_inc(o_lo_done, 1)

                for t in range(TT):
                    maximum(0, 0, t)
                for t in range(TT):
                    inverse(0, 0, t)
                with dve.Fori(0, HEADS // 2 - 1) as hp:
                    head_pair(hp, False)
                head_pair(HEADS // 2 - 1, True)

                finish_x(l, PAIR_OUT, GROUP_OUT, 1.0, 2, V_FFN2, late=True)
                ffn(l, 1, PAIR_FFN2, GROUP_FFN2, N_FFN2, 3, VECS + V_FFN1, True)
                assert step[0] == DVE_STEPS, step[0]

            for n in range(2 * TT):
                t, half = n // 2, n % 2
                dve.wait_ge(y_turned, n + 1)
                V.tensor_copy(y_tok[:, t, 512 * half:512 * half + 512], bank[n % BANKS][:, :]).then_inc(y_copied, 1)

        @block.gpsimd
        def _(pool):
            G = nc.gpsimd
            G.memset(ident[:, :], 0.0).then_inc(pool_step, 1)
            pool.wait_ge(pool_step, 1)
            G.affine_select(out=ident[:, :], in_=ident[:, :], compare_op=ALU.not_equal, fill=1.0,
                            base=0, pattern=[[-1, P]], channel_multiplier=1).then_inc(ident_done, 1)
            step = [0]

            def link(l, ins, base):
                step[0] += 1
                ins.then_inc(pool_step, 1)
                pool.wait_ge(pool_step, l * POOL_STEPS + base + step[0])

            def sum_squares(l, tiles, total, wait, base):
                for n, t in enumerate(tiles):
                    wait(n)
                    sq = G.tensor_tensor(total[:, :] if n == 0 else square[:, :], t, t, ALU.mult)
                    if n:
                        link(l, sq, base)
                        last = G.tensor_tensor(total[:, :], total[:, :], square[:, :], ALU.add)
                        if n < len(tiles) - 1:
                            link(l, last, base)
                    else:
                        first = sq
                        link(l, first, base)
                last.then_inc(sumsq_done, 1)

            def x_squares(l, n, base):
                sum_squares(l, [x[:, d, :] for d in range(DT)], sumsq_x,
                            lambda d: wait_x(pool, l, n, d), base)

            x_squares(0, 0, 1)
            B = 1 + step[0]
            assert step[0] == X_LINKS
            step[0] = 0
            with pool.Fori(0, DEPTH) as l:
                x_squares(l, 1, B)
                M = l * GROUPS + GROUP_MIX + 1 + BANKS
                sum_squares(l, [z[:, t, :] for t in range(QT)], sumsq_l[0], lambda t: pool.wait_ge(evac_done, M + t), B)
                sum_squares(l, [z[:, QT + t, :] for t in range(KT)], sumsq_l[1], lambda t: pool.wait_ge(evac_done, M + QT + t), B)
                for g in range(PG):
                    pool.wait_ge(evac_done, M + 6 + g)
                    src, a, b = zp[:, g, :], 0, PW
                    for n in range(g + 1):
                        s0, s1 = (1, 0) if n == 0 else (2 ** (n - 1), 2 ** (n - 1))
                        lo, hi = a + s0, b - s1
                        final = n == g
                        dst = win_s if final else (win_a, win_b)[n % 2]
                        if final and g >= 1:
                            pool.wait_ge(mixed_done, l * PG + g)
                        src0 = src[:, lo - s0:hi - s0]
                        src1 = src[:, lo + s1:hi + s1]
                        link(l, G.tensor_tensor(dst[:, lo:hi], src0, src1, ALU.add), B)
                        src, a, b = dst, lo, hi
                    G.tensor_tensor(win_s[:, PAD:2 * PAD], win_s[:, PAD:2 * PAD], edge[:, g, 0:PAD], ALU.mult)
                    G.tensor_tensor(win_s[:, S:S + PAD], win_s[:, S:S + PAD], edge[:, g, PAD:2 * PAD],
                                    ALU.mult).then_inc(windowed, 1)
                for e in range(2 * HEADS):
                    h = e % HEADS
                    raw = (k_all if e < HEADS else q_all)[0:QK_NOPE, h, :]
                    if e == 0:
                        pool.wait_ge(evac_done, l * GROUPS + GROUP_UK + 4 + BANKS)
                    if e == HEADS:
                        pool.wait_ge(evac_done, l * GROUPS + GROUP_UQ + 4 + BANKS)
                    if e >= 2:
                        pool.wait_ge(head_sums, l * 16 + e - 1)
                    G.tensor_tensor((sq_k if e < HEADS else sq_q)[e % 2][0:QK_NOPE, :], raw, raw, ALU.mult).then_inc(head_sq, 1)

                def split_qk(h, s, dyn):
                    ix = bass.ds(h, 1) if dyn else slice(h, h + 1)
                    pool.wait_ge(qk_hi, l * 8 + h + 1)
                    for src, o in ((q_all, 0), (k_all, 2)):
                        last = G.tensor_tensor(h_lo[0:QK, o + s:o + s + 1, :], src[0:QK, ix, :],
                                               h_hi[0:QK, o + s:o + s + 1, :].bitcast(F32), ALU.subtract)
                    last.then_inc(qk_lo, 1)

                def normalise(h, s, t):
                    pool.wait_ge(inv_done, l * 32 + 4 * h + t + 1)
                    G.tensor_tensor(prob[:, s, t, :], prob[:, s, t, :], row_inv[:, s, t:t + 1].to_broadcast([P, S]),
                                    ALU.mult).then_inc(prob_done, 1)

                for h in range(2):
                    split_qk(h, h, False)
                for t in range(TT):
                    normalise(0, 0, t)

                def head_pair(hp, last):
                    for s in range(2):
                        h = 2 * hp + s
                        if not last:
                            split_qk(h + 2, s, True)
                        if not (last and s == 1):
                            for t in range(TT):
                                normalise(h + 1, 1 - s, t)

                with pool.Fori(0, HEADS // 2 - 1) as hp:
                    head_pair(hp, False)
                head_pair(HEADS // 2 - 1, True)
                x_squares(l, 2, B)
                x_squares(l, 3, B)
                assert step[0] == POOL_STEPS, step[0]


_INS = ["x", "ffn1_norm", "ffn1_w_gu", "ffn1_w_down", "mix_norm", "w_in", "q_lat_norm", "kv_lat_norm",
        "w_uq", "w_uk", "w_uv", "q_norm", "k_norm", "w_pool", "pool_scale", "w_out",
        "ffn2_norm", "ffn2_w_gu", "ffn2_w_down"]


def shape_tables(seq):
    import numpy as np

    half = QK_ROPE // 2
    inv = np.float32(10000.0) ** (-np.arange(0, QK_ROPE, 2, dtype=np.float32) / np.float32(QK_ROPE))
    ang = np.arange(seq, dtype=np.float32)[None, :] * inv.astype(np.float32)[:, None]
    cos, sin = np.cos(ang).astype(np.float32), np.sin(ang).astype(np.float32)
    groups = P // QK_ROPE
    rope_cos = np.tile(np.concatenate([cos, cos]), (groups, 1))
    rope_sin = np.tile(np.concatenate([-sin, sin]), (groups, 1))
    pos = np.concatenate([np.arange(PAD), np.arange(seq - PAD, seq)])
    edge = []
    for w in (2, 4, 8, 16):
        count = np.minimum(pos + w // 2, seq) - np.maximum(pos - w // 2, 0)
        edge.append(w / count)
    edge = np.tile(np.concatenate(edge).astype(np.float32)[None, :], (P, 1))
    assert rope_cos.shape == (P, seq) and half == 16
    return {"rope_cos": rope_cos, "rope_sin": rope_sin, "pool_edge": edge}


def kernel(**inputs):
    import numpy as np
    import concourse.bacc as bacc
    from concourse.bass_utils import run_bass_kernel_spmd

    nc = bacc.Bacc("TRN2", target_bir_lowering=False, num_devices=1)
    arrays, args = {}, []
    given = {name: np.ascontiguousarray(inputs[name]) for name in _INS}
    shape = given["x"].shape
    given.update(shape_tables(shape[1]))
    for name, a in given.items():
        arrays[f"in_{name}"] = a
        args.append(nc.dram_tensor(f"in_{name}", a.shape, mybir.dt.from_np(a.dtype), kind="ExternalInput").ap())
    args.append(nc.dram_tensor("out_y", shape, F32, kind="ExternalOutput").ap())
    build_trunk(nc, *args)
    r = run_bass_kernel_spmd(nc, [arrays], core_ids=[0])
    return r.results[0]["out_y"]
```

```python
from contextlib import ExitStack

import concourse.bass as bass
from concourse import mybir

F32 = mybir.dt.float32
F32R = mybir.dt.float32r
ACT = mybir.ActivationFunctionType
ALU = mybir.AluOpType
AX_X = mybir.AxisListType.X

P = 128
EPS = 1e-6
QK_NOPE, QK_ROPE, V_HEAD = 64, 32, 64
QK = QK_NOPE + QK_ROPE
PAD = 8
RING = 2
BANKS = 4


def build_trunk(nc, x_in, ffn1_norm, ffn1_w_gu, ffn1_w_down, mix_norm, w_in, q_lat_norm, kv_lat_norm,
                w_uq, w_uk, w_uv, q_norm, k_norm, w_pool, pool_scale, w_out,
                ffn2_norm, ffn2_w_gu, ffn2_w_down, rope_cos, rope_sin, pool_edge, y_out):
    _, S, D = x_in.shape
    DEPTH = ffn1_w_gu.shape[0]
    F = ffn1_w_down.shape[1]
    QL, KVL = w_uq.shape[1], w_uk.shape[1]
    HEADS = w_uq.shape[2] // QK
    PG = w_pool.shape[1]
    DT, TT, FT = D // P, S // P, F // P
    QT, KT = QL // P, KVL // P
    CAT = HEADS * V_HEAD // P
    O_KV, O_PE, O_POOL = QL, QL + KVL, QL + KVL + QK_ROPE
    SCALE = float(QK) ** -0.5
    assert S == 512 and DT == 8 and TT == 4 and QT == 3 and KT == 2 and PG == 4 and HEADS == 8

    CHUNKS = [8, 8, FT - 16]
    assert all(n % 2 == 0 and 0 < n <= 8 for n in CHUNKS)
    FFN_PAIRS = FT + len(CHUNKS) * DT // 2
    MIX_PAIRS, OUT_PAIRS = 8, DT // 2
    MIX_GROUPS = 10 + 4 + 4 + 6 + 4
    PAIR_MIX = FFN_PAIRS
    PAIR_OUT = PAIR_MIX + MIX_PAIRS
    PAIR_FFN2 = PAIR_OUT + OUT_PAIRS
    PAIRS = PAIR_FFN2 + FFN_PAIRS
    GROUP_MIX = 2 * FFN_PAIRS
    GROUP_UK = GROUP_MIX + 10
    GROUP_UV, GROUP_UQ, GROUP_POOL = GROUP_UK + 4, GROUP_UK + 8, GROUP_UK + 14
    GROUP_OUT = GROUP_MIX + MIX_GROUPS
    GROUP_FFN2 = GROUP_OUT + 2 * DT
    GROUPS = GROUP_FFN2 + 2 * FFN_PAIRS
    ACT_GROUPS = GROUP_POOL - GROUP_UK
    DVE_GROUPS = GROUPS - ACT_GROUPS
    assert PAIRS % RING == 0 and PAIR_MIX % RING == 0 and PAIR_FFN2 % RING == 0
    assert GROUPS % BANKS == 0 and GROUP_MIX % BANKS == 0 and GROUP_FFN2 % BANKS == 0 and GROUP_OUT % BANKS == 0
    NORMS = 5
    N_FFN1, N_MIX, N_KVL, N_QL, N_FFN2 = range(NORMS)

    V_FFN1, V_MIX, V_FFN2 = 0, DT, 2 * DT
    V_KVL = 3 * DT
    V_QL = V_KVL + KT
    V_PS = V_QL + QT
    V_QN, V_KN, V_QPE, V_KPE = V_PS + PG, V_PS + PG + 1, V_PS + PG + 2, V_PS + PG + 3
    VECS = V_KPE + 1
    DVE_STEPS = 9
    X_LINKS = 2 * DT - 2
    POOL_STEPS = 3 * X_LINKS + 2 * QT - 2 + 2 * KT - 2 + PG * (PG + 1) // 2
    VROWS = DEPTH * VECS + DT

    with ExitStack() as ctx:
        TB = 4 * S
        arena_bytes = 103 * TB
        arena = ctx.enter_context(nc.sbuf_tensor("arena", [P, arena_bytes // 4], F32))
        base = nc.sbuf_base - arena_bytes
        used = [0]

        def place(name, shape, dt, at=None):
            size = 4
            for n in shape[1:]:
                size *= n
            if at is None:
                at = used[0]
                used[0] += (size + 31) // 32 * 32
                assert used[0] <= arena_bytes, name
            return nc.alloc_sbuf_tensor_at(name, shape, dt, offset=base + at), at

        w_raw = [place(f"w_raw{b}", [P, 2048], F32)[0] for b in range(RING)]
        w_hi = [place(f"w_hi{b}", [P, 2048], F32R)[0] for b in range(RING)]
        w_lo = [place(f"w_lo{b}", [P, 2048], F32R)[0] for b in range(RING)]
        x, _ = place("x", [P, DT, S], F32)
        xg_hi, at_xg_hi = place("xg_hi", [P, DT, S], F32R)
        xg_lo, at_xg_lo = place("xg_lo", [P, DT, S], F32R)
        sq_k = [place(f"sq_k{i}", [P, S], F32, at_xg_hi + i * TB)[0] for i in range(2)]
        sq_q = [place(f"sq_q{i}", [P, S], F32, at_xg_hi + (2 + i) * TB)[0] for i in range(2)]
        q_rope, _ = place("q_rope", [P, 2, S], F32, at_xg_lo + 2 * TB)
        h_hi, _ = place("h_hi", [P, 8, S], F32R)
        h_lo, _ = place("h_lo", [P, 8, S], F32R)
        v_hi, _ = place("v_hi", [P, TT, P], F32R)
        v_lo, _ = place("v_lo", [P, TT, P], F32R)
        q_all, at_q = place("q_all", [P, HEADS, S], F32)
        k_all, at_k = place("k_all", [P, HEADS, S], F32)
        v_all, _ = place("v_all", [P, TT, HEADS * V_HEAD], F32)
        gate = [place(f"gate{i}", [P, S], F32, at_q + i * TB)[0] for i in range(2)]
        up = [place(f"up{i}", [P, S], F32, at_q + (2 + i) * TB)[0] for i in range(2)]
        silu = [place(f"silu{i}", [P, S], F32, at_q + (4 + i) * TB)[0] for i in range(2)]
        hid = [place(f"hid{i}", [P, S], F32, at_q + (6 + i) * TB)[0] for i in range(2)]
        PW = S + 2 * PAD
        zp, _ = place("zp", [P, PG, PW], F32, at_q)
        win_a, _ = place("win_a", [P, PW], F32, at_q + 4 * 4 * PW)
        win_b, _ = place("win_b", [P, PW], F32, at_q + 5 * 4 * PW)
        win_s, _ = place("win_s", [P, PW], F32, at_q + 6 * 4 * PW)
        assert 7 * 4 * PW <= HEADS * TB
        x_tok, _ = place("x_tok", [P, TT, D], F32, at_k)
        y_tok, _ = place("y_tok", [P, TT, D], F32, at_k)
        prob, at_a = place("prob", [P, 2, TT, S], F32)
        z, _ = place("z", [P, QT + KT, S], F32, at_a)
        q_pe, _ = place("q_pe", [P, 2, S], F32, at_a)
        rot_a, _ = place("rot_a", [P, S], F32, at_a + 2 * TB)
        rot_b, _ = place("rot_b", [P, S], F32, at_a + 3 * TB)
        k_pe, _ = place("k_pe", [P, S], F32, at_a + 5 * TB)
        sumsq_l = [place(f"sumsq_l{i}", [P, S], F32, at_a + (6 + i) * TB)[0] for i in range(2)]
        cos_t, _ = place("cos_t", [P, S], F32)
        sin_t, _ = place("sin_t", [P, S], F32)
        k_rot, _ = place("k_rot", [P, S], F32)
        rstd_x, _ = place("rstd_x", [P, S], F32)
        rstd_l, _ = place("rstd_l", [P, S], F32)
        sumsq_x, _ = place("sumsq_x", [P, S], F32)
        square, _ = place("square", [P, S], F32)
        ones, _ = place("ones", [P, P], F32)
        ident, _ = place("ident", [P, P], F32)
        gain_rows, _ = place("gain_rows", [P, P], F32)
        gains, _ = place("gains", [P, P], F32)
        gains_qk, _ = place("gains_qk", [P, DEPTH], F32)
        edge, _ = place("edge", [P, PG, 2 * PAD], F32)
        eps_t, _ = place("eps_t", [P, 2], F32)
        k_rstd, _ = place("k_rstd", [P, HEADS * TT], F32)
        q_rstd, _ = place("q_rstd", [P, HEADS * TT], F32)
        row_max, _ = place("row_max", [P, 2, TT], F32)
        neg_max, _ = place("neg_max", [P, 2, TT], F32)
        row_sum, _ = place("row_sum", [P, 2, TT], F32)
        row_inv, _ = place("row_inv", [P, 2, TT], F32)

        bank = [ctx.enter_context(nc.psum_tensor(f"bank{i}", [P, S], F32)) for i in range(8)]
        SUMS, SPREAD, TRANS, OUT = 4, 5, 4, 7

        def sem(name):
            return ctx.enter_context(nc.semaphore(name))

        const_loaded, memset_done, ident_done = sem("const_loaded"), sem("memset_done"), sem("ident_done")
        gains_t, gains_done = sem("gains_t"), sem("gains_done")
        x_loaded, x_turned = sem("x_loaded"), sem("x_turned")
        y_turned, y_copied, y_stored = sem("y_turned"), sem("y_copied"), sem("y_stored")
        raw_loaded = [sem(f"raw_loaded{b}") for b in range(RING)]
        hi_split, lo_split = sem("hi_split"), sem("lo_split")
        acc_done, evac_done, evac_act = sem("acc_done"), sem("evac_done"), sem("evac_act")
        x_done, xg_hi_done, xg_lo_done = sem("x_done"), sem("xg_hi_done"), sem("xg_lo_done")
        pool_step = sem("pool_step")
        sumsq_done, sums_done, rms_done, rstd_done = sem("sumsq_done"), sem("sums_done"), sem("rms_done"), sem("rstd_done")
        silu_done, hid_done, h_hi_done, h_lo_done = sem("silu_done"), sem("hid_done"), sem("h_hi_done"), sem("h_lo_done")
        dve_step = sem("dve_step")
        lat_scaled, lat_hi, lat_lo = sem("lat_scaled"), sem("lat_hi"), sem("lat_lo")
        windowed, mixed_done, mixed_hi, mixed_lo = sem("windowed"), sem("mixed_done"), sem("mixed_hi"), sem("mixed_lo")
        pooled_hi, pooled_lo = sem("pooled_hi"), sem("pooled_lo")
        k_rope_done, k_filled, q_rope_done, q_filled = sem("k_rope_done"), sem("k_filled"), sem("q_rope_done"), sem("q_filled")
        k_sq, q_sq, head_sums, root_done, factor_done = sem("k_sq"), sem("q_sq"), sem("head_sums"), sem("root_done"), sem("factor_done")
        k_spread, k_normed = sem("k_spread"), sem("k_normed")
        qk_hi, qk_lo, v_hi_done, v_lo_done = sem("qk_hi"), sem("qk_lo"), sem("v_hi_done"), sem("v_lo_done")
        scores_done, max_done, neg_done, exp_done = sem("scores_done"), sem("max_done"), sem("neg_done"), sem("exp_done")
        inv_done, prob_done, prob_dve, trans_done = sem("inv_done"), sem("prob_done"), sem("prob_dve"), sem("trans_done")
        pt_hi_done, pt_lo_done, pt_used = sem("pt_hi_done"), sem("pt_lo_done"), sem("pt_used")
        o_hi_done, o_lo_done = sem("o_hi_done"), sem("o_lo_done")
        C_TRANS, C_PTLO, C_PTUSED, C_OLO = 2 * TT, 3, TT, 1

        def rows(w):
            return w.rearrange("l (k p) n -> l p k n", p=P)

        def gain(l, c):
            return gains[:, bass.ds(l * VECS + c, 1)]

        def pairs_of(buf, width, blocks=8, at=0):
            return buf[:, at:at + blocks * width].rearrange("p (k n) -> p k n", n=width)


        def chunk_start(c):
            return sum(CHUNKS[:c]) + c * DT // 2

        def used_at(p):
            if p < PAIR_MIX:
                return 2 * p + 2
            if p < PAIR_OUT:
                return [GROUP_MIX + 2, GROUP_MIX + 4, GROUP_MIX + 6, GROUP_MIX + 8, GROUP_UK, GROUP_UQ,
                        GROUP_POOL, GROUP_OUT][p - PAIR_MIX]
            if p < PAIR_FFN2:
                return GROUP_OUT + 4 * (p - PAIR_OUT) + 4
            return GROUP_FFN2 + 2 * (p - PAIR_FFN2) + 2

        def wait_evac(eng, l, g, back=0):
            start, add = (g, 0) if isinstance(g, int) else g
            if GROUP_UK <= start - back < GROUP_POOL:
                eng.wait_ge(evac_act, l * ACT_GROUPS + start - back - GROUP_UK + 1)
            else:
                skipped = ACT_GROUPS if start - back >= GROUP_POOL else 0
                eng.wait_ge(evac_done, l * DVE_GROUPS + (start - back - skipped + 1 + BANKS) + add)

        def split_parts(p, raw, split):
            if not isinstance(p, int) or p not in (PAIR_MIX + 6, PAIR_MIX + 7):
                return [(raw[:, :], split[:, :])]
            slots = 2 if p == PAIR_MIX + 6 else 1
            v_raw, v_split = (b[:, 0:1024 * slots].rearrange("p (k n) -> p k n", k=slots) for b in (raw, split))
            heads = v_raw[:, :, 0:HEADS * QK].rearrange("p k (h n) -> p k h n", n=QK)
            out = []
            for a, b, c0 in ((0, QK_NOPE, 0), (QK_NOPE, QK, HEADS * QK_NOPE)):
                dst = v_split[:, :, c0:c0 + HEADS * (b - a)].rearrange("p k (h n) -> p k h n", n=b - a)
                out.append((heads[:, :, :, a:b], dst))
            if slots == 1:
                out.append((raw[:, 1024:1024 + PG * P], split[:, 1024:1024 + PG * P]))
            return out

        def wait_x(eng, l, n, d):
            if n == 0:
                eng.wait_ge(x_done, d + 1)
            else:
                end = (GROUP_MIX, GROUP_FFN2, GROUPS)[n - 1]
                wait_evac(eng, l, end - DT + d)

        pooled = [place(f"pooled{i}", [P, S], F32, at_a + (4 + 2 * i) * TB)[0] for i in range(2)]

        block = ctx.enter_context(nc.Block())

        @block.sync
        def _(sp):
            for t in range(TT):
                sp.dma_start(x_tok[:, t, :], x_in[0, t * P:(t + 1) * P, :]).then_inc(x_loaded, 16)
            sp.dma_start(cos_t[:, :], rope_cos).then_inc(const_loaded, 16)
            sp.dma_start(sin_t[:, :], rope_sin).then_inc(const_loaded, 16)
            sp.dma_start(edge[:, :, :].rearrange("p g n -> p (g n)"), pool_edge).then_inc(const_loaded, 16)

            def wait_free(l, p):
                sp.wait_ge(lo_split, l * PAIRS + p + 1)

            def load_columns(l, p, b, w, r0, blocks, col, width=256):
                wait_free(l, p)
                half = blocks // 2
                dst = pairs_of(w_raw[b], width, blocks)
                for k in (half, 0):
                    sp.dma_start(dst[:, k:k + half, :],
                                 rows(w)[l, :, r0 + k:r0 + k + half, col]).then_inc(raw_loaded[b], 16)

            def load_ffn(l, p0, w_gu, w_down):
                for c, n in enumerate(CHUNKS):
                    pc, f0 = p0 + chunk_start(c), P * sum(CHUNKS[:c])
                    with sp.Fori(0, n // 2) as i:
                        load_columns(l, pc + 2 * i, 0, w_gu, 0, DT, bass.ds(f0 + 256 * i, 256))
                        load_columns(l, pc + 2 * i + 1, 1, w_gu, 0, DT, bass.ds(F + f0 + 256 * i, 256))
                    with sp.Fori(0, DT // 4) as i:
                        for b in range(2):
                            load_columns(l, pc + n + 2 * i + b, b, w_down, f0 // P, n,
                                         bass.ds(512 * i + 256 * b, 256))

            with sp.Fori(0, DEPTH) as l:
                load_ffn(l, 0, ffn1_w_gu, ffn1_w_down)
                p = PAIR_MIX
                load_columns(l, p, p % RING, w_in, 0, DT, slice(O_KV, O_KV + 256))
                load_columns(l, p + 1, (p + 1) % RING, w_in, 0, DT, slice(0, 256))
                wait_free(l, p + 2)
                for at, col, width in ((0, 256, P), (1024, O_PE - QK_NOPE, QK)):
                    sp.dma_start(w_raw[p % RING][:, at:at + DT * width].rearrange("p (k n) -> p k n", k=DT),
                                 rows(w_in)[l, :, :, col:col + width]).then_inc(raw_loaded[p % RING], 16)
                load_columns(l, p + 3, (p + 3) % RING, w_in, 0, DT, slice(O_POOL, O_POOL + 256))
                load_columns(l, p + 4, p % RING, w_in, 0, DT, slice(O_POOL + 256, O_POOL + 512))
                p += 5
                wait_free(l, p)
                for at, w in ((0, w_uk), (1024, w_uv)):
                    sp.dma_start(w_raw[p % RING][:, at:at + 1024].rearrange("p (k n) -> p k n", k=KT),
                                 rows(w)[l]).then_inc(raw_loaded[p % RING], 16)
                p += 1
                wait_free(l, p)
                for k in range(2):
                    sp.dma_start(w_raw[p % RING][:, 1024 * k:1024 * k + HEADS * QK],
                                 rows(w_uq)[l, :, k, :]).then_inc(raw_loaded[p % RING], 16)
                p += 1
                wait_free(l, p)
                sp.dma_start(w_raw[p % RING][:, 0:HEADS * QK], rows(w_uq)[l, :, 2, :]).then_inc(raw_loaded[p % RING], 16)
                sp.dma_start(w_raw[p % RING][:, 1024:1024 + PG * P].rearrange("p (g n) -> p g n", g=PG),
                             w_pool.rearrange("l g c d -> l c g d")[l]).then_inc(raw_loaded[p % RING], 16)
                for n in range(OUT_PAIRS):
                    r0, c0 = (CAT, 0)[n // 2], 512 * (n % 2)
                    load_columns(l, PAIR_OUT + n, n % 2, w_out, r0, 4, slice(c0, c0 + 512), 512)
                load_ffn(l, PAIR_FFN2, ffn2_w_gu, ffn2_w_down)
            for t in range(TT):
                sp.wait_ge(y_copied, 2 * t + 2)
                sp.dma_start(y_out[0, t * P:(t + 1) * P, :], y_tok[:, t, :]).then_inc(y_stored, 16)
            sp.wait_ge(y_stored, 16 * TT)

        @block.scalar
        def _(act):
            act.sem_inc(hi_split, RING)
            act.wait_ge(memset_done, 1)
            for l in range(DEPTH):
                r = l * VECS
                for v, w, n in ((V_FFN1, ffn1_norm, DT), (V_MIX, mix_norm, DT), (V_FFN2, ffn2_norm, DT),
                                (V_QL, q_lat_norm, QT), (V_KVL, kv_lat_norm, KT), (V_PS, pool_scale, PG)):
                    act.dma_start(gain_rows[r + v:r + v + n, :], w[l].rearrange("(k p) -> k p", p=P)).then_inc(gains_t, 16)
                for v, w in ((V_QN, q_norm), (V_KN, k_norm)):
                    act.dma_start(gain_rows[r + v:r + v + 1, 0:QK_NOPE], w[l:l + 1, 0:QK_NOPE]).then_inc(gains_t, 16)
                for j in range(P // QK_ROPE):
                    act.dma_start(gain_rows[r + V_QPE:r + V_QPE + 1, j * QK_ROPE:(j + 1) * QK_ROPE],
                                  q_norm[l:l + 1, QK_NOPE:QK]).then_inc(gains_t, 16)
                act.dma_start(gain_rows[r + V_KPE:r + V_KPE + 1, QK_NOPE:QK],
                              k_norm[l:l + 1, QK_NOPE:QK]).then_inc(gains_t, 16)
            act.dma_start(gain_rows[DEPTH * VECS:VROWS, :], ffn1_norm[0].rearrange("(k p) -> k p", p=P)).then_inc(gains_t, 16)

            def split_hi(l, b, loaded, used, p=0):
                act.wait_ge(raw_loaded[b], l * (16 * PAIRS) + loaded)
                if used is not None:
                    act.wait_ge(acc_done, l * GROUPS + used)
                for src, dst in split_parts(p, w_raw[b], w_hi[b]):
                    last = nc.scalar.activation(dst, src, ACT.Copy)
                last.then_inc(hi_split, 1)

            def split_hi_at(l, p):
                split_hi(l, p % RING, 32 * (p // RING + 1), used_at(p - RING) if p >= RING else None, p)

            def rms(l, n, dst, width):
                act.wait_ge(sums_done, l * NORMS + n + 1)
                nc.scalar.activation(dst[:, :], bank[SUMS][:, :], ACT.Sqrt, bias=eps_t[:, 0:1],
                                     scale=1.0 / width).then_inc(rms_done, 1)

            def gain_x(l, n, v, d):
                wait_x(act, l, n, d)
                nc.scalar.activation(xg_hi[:, d, :], x[:, d, :], ACT.Copy, scale=gain(l, v + d)).then_inc(xg_hi_done, 1)

            def ffn(l, which, p0, g0, norm, next_norm, next_v, last):
                for c, n in enumerate(CHUNKS):
                    pc = p0 + chunk_start(c)
                    gc = g0 + 2 * (pc - p0)
                    f0 = which * FT + sum(CHUNKS[:c])

                    def gate_up(i):
                        g = gc + 4 * i
                        for j in range(2):
                            wait_evac(act, l, (gc + j, 4 * i))
                            nc.scalar.activation(silu[j][:, :], gate[j][:, :], ACT.Silu).then_inc(silu_done, 1)
                        split_hi(l, 0, 16 * (pc + 2 * i + 2) + 32, g + 2)
                        for j in range(2):
                            act.wait_ge(hid_done, l * 2 * FT + f0 + 2 * i + j + 1)
                            nc.scalar.activation(h_hi[:, bass.ds(2 * i + j, 1), :], hid[j][:, :].rearrange("p (o s) -> p o s", o=1),
                                                 ACT.Copy).then_inc(h_hi_done, 1)
                        split_hi(l, 1, 16 * (pc + 2 * i + 2) + 32, g + 4)

                    if c == 0:
                        rms(l, norm, rstd_x, D)
                    with act.Fori(0, n // 2) as i:
                        gate_up(i)
                    pd = pc + n
                    if c < len(CHUNKS) - 1:
                        with act.Fori(0, DT // 4) as i:
                            for b in range(2):
                                split_hi(l, b, 16 * (pd + 2 * i + 2) + 32, g0 + 2 * (pd - p0) + 4 * i + 2 * b + 2)
                    else:
                        finish_x(l, pd, next_norm, next_v, last)

            def finish_x(l, pd, next_norm, next_v, last=False):
                for i in range(DT // 2):
                    for d in (2 * i, 2 * i + 1):
                        gain_x(l, next_norm, next_v, d)
                    if not (last and i >= DT // 2 - RING):
                        split_hi_at(l, pd + i + 2)

            act.wait_ge(gains_done, 1)
            act.wait_ge(memset_done, 2)
            for d in range(DT):
                gain_x(0, 0, V_FFN1, d)
            with act.Fori(0, DEPTH) as l:
                for p in range(RING):
                    split_hi_at(l, p)
                ffn(l, 0, 0, 0, N_FFN1, 1, V_MIX, False)

                rms(l, N_MIX, rstd_x, D)
                split_hi_at(l, PAIR_MIX + 2)

                def latent_hi(n, t0, width):
                    for t in range(t0, t0 + width):
                        act.wait_ge(lat_scaled, l * (QT + KT) + t + 1)
                        nc.scalar.activation(h_hi[:, t, :], z[:, t, :], ACT.Copy, scale=gain(l, V_KVL + t)).then_inc(lat_hi, 1)

                rms(l, N_KVL, rstd_l, KVL)
                latent_hi(N_KVL, 0, KT)
                for p in (PAIR_MIX + 3, PAIR_MIX + 4):
                    split_hi_at(l, p)
                rms(l, N_QL, rstd_l, QL)
                latent_hi(N_QL, KT, QT)
                for p in (PAIR_MIX + 5, PAIR_MIX + 6):
                    split_hi_at(l, p)

                def take_group(g, *parts):
                    act.wait_ge(acc_done, l * GROUPS + g + 1)
                    for dst, rows_ in parts:
                        last = nc.scalar.activation(dst, bank[g % BANKS][rows_, :], ACT.Copy)
                    last.then_inc(evac_act, 1)

                LOW, HIGH, ALL = slice(0, 64), slice(64, P), slice(0, P)
                act.wait_ge(acc_done, l * GROUPS + GROUP_UK)
                act.wait_ge(k_rope_done, l + 1)
                for i in range(2):
                    nc.scalar.activation(sq_k[i][QK_NOPE:QK, :], k_pe[QK_NOPE:QK, :], ACT.Square).then_inc(k_filled, 1)
                for r in range(4):
                    take_group(GROUP_UK + r, (k_all[0:64, 2 * r, :], LOW), (k_all[0:64, 2 * r + 1, :], HIGH))
                for t in range(TT):
                    take_group(GROUP_UV + t, (v_all[:, t, :], ALL))
                split_hi_at(l, PAIR_MIX + 7)
                nc.scalar.activation(k_all[QK_NOPE:QK, :, :],
                                     k_rot[QK_NOPE:QK, :].rearrange("p (o s) -> p o s", o=1).to_broadcast([QK_ROPE, HEADS, S]),
                                     ACT.Copy).then_inc(k_filled, 1)
                for g in range(PG):
                    act.wait_ge(mixed_done, l * PG + g + 1)
                    nc.scalar.activation(xg_hi[:, CAT + g, :], zp[:, g, PAD:PAD + S], ACT.Copy).then_inc(mixed_hi, 1)
                act.wait_ge(mixed_lo, l * PG + PG)
                for r in range(4):
                    take_group(GROUP_UQ + r, (q_all[0:64, 2 * r, :], LOW), (q_all[0:64, 2 * r + 1, :], HIGH))
                for r in range(2):
                    take_group(GROUP_UQ + 4 + r, (q_pe[:, r, :], ALL))
                split_hi_at(l, PAIR_MIX + 8)

                def head_root(n, dst, eps, scale):
                    act.wait_ge(head_sums, l * 2 * HEADS + (n + 1) * HEADS)
                    nc.scalar.activation(dst[:, :], bank[SUMS][:, n * 32:n * 32 + 32], ACT.Sqrt,
                                         bias=eps_t[:, eps:eps + 1], scale=scale).then_inc(root_done, 1)

                head_root(0, k_rstd, 0, 1.0 / QK)
                for g in range(PG):
                    wait_evac(act, l, GROUP_POOL + g)
                    nc.scalar.activation(xg_hi[:, CAT + g, :], pooled[g % 2][:, :], ACT.Copy).then_inc(pooled_hi, 1)
                act.wait_ge(evac_act, l * ACT_GROUPS + ACT_GROUPS)
                for h in range(HEADS):
                    j = h % 4
                    if h >= 2:
                        act.wait_ge(head_sums, l * 2 * HEADS + HEADS + h - 1)
                    nc.scalar.activation(sq_q[h % 2][0:QK_NOPE, :], q_all[0:QK_NOPE, h, :], ACT.Square)
                    nc.scalar.activation(sq_q[h % 2][QK_NOPE:QK, :], q_pe[32 * j:32 * j + 32, h // 4, :],
                                         ACT.Square).then_inc(q_sq, 1)
                split_hi_at(l, PAIR_MIX + 9)
                act.wait_ge(q_rope_done, 2 * l + 2)
                for h in range(HEADS):
                    j = h % 4
                    nc.scalar.activation(q_all[QK_NOPE:QK, h, :], q_rope[32 * j:32 * j + 32, h // 4, :],
                                         ACT.Copy).then_inc(q_filled, 1)
                head_root(1, q_rstd, 1, 1.0)

                def split_qk(h, s):
                    ix = slice(h, h + 1) if isinstance(h, int) else bass.ds(h, 1)
                    for src, o in ((q_all, 0), (k_all, 2)):
                        last = nc.scalar.activation(h_hi[0:QK, o + s:o + s + 1, :], src[0:QK, ix, :], ACT.Copy)
                    last.then_inc(qk_hi, 1)

                def exponent(h, s, t):
                    act.wait_ge(trans_done, l * 32 + 4 * h + 4)
                    act.wait_ge(neg_done, l * 32 + 4 * h + t + 1)
                    col = slice(t, t + 1) if isinstance(h, int) else bass.ds(4 * h + t, 1)
                    col = slice(4 * h + t, 4 * h + t + 1) if isinstance(h, int) else col
                    nc.scalar.activation(prob[:, s, t, :], bank[t][:, :], ACT.Exp, bias=neg_max[:, s, t:t + 1],
                                         scale=q_rstd[:, col], accum_out=row_sum[:, s, t:t + 1]).then_inc(exp_done, 1)

                def prob_t_hi(h, t):
                    act.wait_ge(pt_used, l * 32 + 4 * h + t + 1)
                    act.wait_ge(trans_done, l * 32 + 4 * h + t + 1 + C_TRANS)
                    nc.scalar.activation(h_hi[:, 4 + t, :], bank[TRANS + t % 3][:, :], ACT.Copy).then_inc(pt_hi_done, 1)

                def split_v(hp):
                    act.wait_ge(pt_used, l * 32 + 8 * hp + C_PTUSED)
                    nc.scalar.activation(v_hi[:, :, :], v_all[:, :, bass.ds(P * hp, P)], ACT.Copy).then_inc(v_hi_done, 1)

                def head_pair(hp, last):
                    for s in range(2):
                        h = 2 * hp + s
                        if s == 0:
                            split_v(hp)
                        if not last:
                            act.wait_ge(scores_done, l * 32 + 4 * h + 4)
                            split_qk(h + 2, s)
                        more = not (last and s == 1)
                        for t in range(TT):
                            if more and t < 3:
                                exponent(h + 1, 1 - s, t)
                        for t in range(TT):
                            prob_t_hi(h, t)
                            if more and t == 0:
                                exponent(h + 1, 1 - s, 3)
                        act.wait_ge(pt_used, l * 32 + 4 * h + 4 + C_PTUSED)
                        nc.scalar.activation(xg_hi[64 * s:64 * s + 64, bass.ds(CAT + hp, 1), :],
                                             bank[OUT][64 * s:64 * s + 64, :].rearrange("p (o s) -> p o s", o=1),
                                             ACT.Copy).then_inc(o_hi_done, 1)

                act.wait_ge(q_filled, l * HEADS + HEADS)
                for h in range(2):
                    act.wait_ge(k_normed, l * HEADS + h + 1)
                    split_qk(h, h)
                split_hi_at(l, PAIR_MIX + 10)
                split_hi_at(l, PAIR_MIX + 11)
                act.wait_ge(k_normed, l * HEADS + HEADS)
                act.wait_ge(factor_done, 2 * l + 2)
                for t in range(TT):
                    exponent(0, 0, t)
                with act.Fori(0, HEADS // 2 - 1) as hp:
                    head_pair(hp, False)
                head_pair(HEADS // 2 - 1, True)

                for n in range(2):
                    for d in range(4):
                        if n == 0:
                            gain_x(l, 2, V_FFN2, d)
                    split_hi_at(l, PAIR_FFN2 + n)
                wait_x(act, l, 2, DT - 1)
                for d in range(4, DT):
                    gain_x(l, 2, V_FFN2, d)
                ffn(l, 1, PAIR_FFN2, GROUP_FFN2, N_FFN2, 3, VECS + V_FFN1, True)

        @block.tensor
        def _(pe):
            pe.sem_inc(trans_done, C_TRANS)
            pe.sem_inc(pt_used, C_PTUSED)
            pe.wait_ge(memset_done, 2)
            pe.wait_ge(ident_done, 1)
            pe.wait_ge(gains_t, 16 * (13 * DEPTH + 1))
            nc.tensor.transpose(bank[SUMS][:, 0:P], gain_rows[:, :], ident[:, :]).then_inc(x_turned, 1)
            pe.wait_ge(x_loaded, 16 * TT)
            for d in range(DT):
                if d >= BANKS:
                    pe.wait_ge(x_done, d - BANKS + 1)
                for t in range(TT):
                    last = nc.tensor.transpose(bank[d % BANKS][:, t * P:(t + 1) * P], x_tok[:, t, d * P:(d + 1) * P], ident[:, :])
                last.then_inc(x_turned, 1)
            pe.wait_ge(x_done, DT)

            def mm3(out, whi, wlo, xhi, xlo, first, last):
                nc.tensor.matmul(out, whi, xhi, start=first, stop=False)
                nc.tensor.matmul(out, whi, xlo, start=False, stop=False)
                return nc.tensor.matmul(out, wlo, xhi, start=False, stop=last)

            def wait_pair(l, p):
                pe.wait_ge(lo_split, l * PAIRS + p + 1 + RING)

            def wait_bank(l, g):
                wait_evac(pe, l, g, BANKS)

            def sums(l, n, src):
                pe.wait_ge(sumsq_done, l * NORMS + n + 1)
                if n == N_QL:
                    pe.wait_ge(rms_done, l * NORMS + n)
                nc.tensor.matmul(bank[SUMS][:, :], ones[:, :], src[:, :], start=True, stop=True).then_inc(sums_done, 1)

            def column_tile(l, g, bk, b, c0, width, hi, lo, order, ready, blocks=DT, cols=P, at=0):
                wait_bank(l, g)
                whi, wlo = pairs_of(w_hi[b], width, blocks, at), pairs_of(w_lo[b], width, blocks, at)
                for n, k in enumerate(order):
                    ready(k)
                    last = mm3(bank[bk][0:cols, :], whi[:, n, c0:c0 + cols], wlo[:, n, c0:c0 + cols],
                               hi[:, k, :], lo[:, k, :], n == 0, n == blocks - 1)
                return last.then_inc(acc_done, 1)

            def wait_xg(l, n):
                def ready(k):
                    pe.wait_ge(xg_lo_done, (3 * l + n) * DT + k + 1)
                return ready

            def nothing(k):
                pass

            def ffn(l, which, p0, g0, norm, x_norm):
                for c, n in enumerate(CHUNKS):
                    pc, gc = p0 + chunk_start(c), g0 + 2 * chunk_start(c)
                    f0 = which * FT + sum(CHUNKS[:c])

                    def gate_up(i, first):
                        for b in range(2):
                            wait_pair(l, pc + 2 * i + b)
                            for j in range(2):
                                column_tile(l, (gc + 2 * b + j, 4 * i), 2 * b + j, b, P * j, 256, xg_hi, xg_lo,
                                                   range(DT), wait_xg(l, x_norm) if first and b + j == 0 else nothing)
                                if first and b + j == 0:
                                    sums(l, norm, sumsq_x)

                    if c == 0:
                        gate_up(0, True)
                    with pe.Fori(1 if c == 0 else 0, n // 2) as i:
                        gate_up(i, False)

                    def wait_h(k):
                        pe.wait_ge(h_lo_done, l * 2 * FT + f0 + k + 1)

                    with pe.Fori(0, DT // 4) as i:
                        for b in range(2):
                            wait_pair(l, pc + n + 2 * i + b)
                            for j in range(2):
                                column_tile(l, (gc + 2 * n + 2 * b + j, 4 * i), 2 * b + j, b, P * j, 256, h_hi, h_lo,
                                            range(n), wait_h if b + j == 0 else nothing, blocks=n)

            with pe.Fori(0, DEPTH) as l:
                ffn(l, 0, 0, 0, N_FFN1, 0)

                g = GROUP_MIX
                for p in range(5):
                    wait_pair(l, PAIR_MIX + p)
                    for j in range(2):
                        c0, width, at, cols = (P * j, 256, 0, P) if p != 2 else (0, (P, QK)[j], 1024 * j, (P, QK)[j])
                        column_tile(l, g, g % BANKS, (PAIR_MIX + p) % RING, c0, width, xg_hi, xg_lo, range(DT),
                                    wait_xg(l, 1) if g == GROUP_MIX else nothing, cols=cols, at=at)
                        if g == GROUP_MIX:
                            sums(l, N_MIX, sumsq_x)
                        if g == GROUP_MIX + 3:
                            sums(l, N_KVL, sumsq_l[0])
                        if g == GROUP_MIX + 6:
                            sums(l, N_QL, sumsq_l[1])
                        g += 1

                b = (PAIR_MIX + 5) % RING
                wait_pair(l, PAIR_MIX + 5)
                pe.wait_ge(lat_lo, l * (QT + KT) + KT)
                for r in range(4):
                    wait_bank(l, GROUP_UK + r)
                    for k in range(KT):
                        c0 = 512 * k + P * r
                        last = mm3(bank[(GROUP_UK + r) % BANKS][:, :], w_hi[b][:, c0:c0 + P], w_lo[b][:, c0:c0 + P],
                                   h_hi[:, k, :], h_lo[:, k, :], k == 0, k == KT - 1)
                    last.then_inc(acc_done, 1)
                for t in range(TT):
                    wait_bank(l, GROUP_UV + t)
                    for k in range(KT):
                        c_hi, c_lo = (h[:, k, t * P:(t + 1) * P] for h in (h_hi, h_lo))
                        wv_hi, wv_lo = (w[b][:, 1024 + 512 * k:1536 + 512 * k] for w in (w_hi, w_lo))
                        last = mm3(bank[(GROUP_UV + t) % BANKS][:, :], c_hi, c_lo, wv_hi, wv_lo, k == 0, k == KT - 1)
                    last.then_inc(acc_done, 1)

                b0, b1 = (PAIR_MIX + 6) % RING, (PAIR_MIX + 7) % RING

                def uq(k, r):
                    bb, c0 = (b0, 1024 * k) if k < 2 else (b1, 0)
                    return [w[bb][:, c0 + P * r:c0 + P * r + P] for w in (w_hi, w_lo)]

                wait_pair(l, PAIR_MIX + 6)
                pe.wait_ge(lat_lo, l * (QT + KT) + QT + KT)
                for k in range(QT):
                    if k == 2:
                        wait_pair(l, PAIR_MIX + 7)
                    for r in range(4):
                        if k == 0:
                            wait_bank(l, GROUP_UQ + r)
                        last = mm3(bank[(GROUP_UQ + r) % BANKS][:, :], *uq(k, r), h_hi[:, KT + k, :], h_lo[:, KT + k, :],
                                   k == 0, k == QT - 1)
                        if k == QT - 1:
                            last.then_inc(acc_done, 1)
                for r in (4, 5):
                    wait_bank(l, GROUP_UQ + r)
                    for k in range(QT):
                        last = mm3(bank[(GROUP_UQ + r) % BANKS][:, :], *uq(k, r), h_hi[:, KT + k, :], h_lo[:, KT + k, :],
                                   k == 0, k == QT - 1)
                    last.then_inc(acc_done, 1)

                def head_sum(n, h):
                    if n == 0:
                        pe.wait_ge(k_sq, l * HEADS + h + 1)
                        pe.wait_ge(k_filled, 3 * l + 2)
                    else:
                        pe.wait_ge(q_sq, l * HEADS + h + 1)
                    sq = (sq_k, sq_q)[n]
                    for t in range(TT):
                        col = n * 32 + h * TT + t
                        last = nc.tensor.matmul(bank[SUMS][:, col:col + 1], sq[h % 2][0:QK, t * P:(t + 1) * P],
                                                ones[0:QK, 0:1], start=True, stop=True)
                    last.then_inc(head_sums, 1)

                for h in range(HEADS):
                    head_sum(0, h)

                for g in range(PG):
                    wait_bank(l, GROUP_POOL + g)
                    pe.wait_ge(mixed_lo, l * PG + g + 1)
                    c0 = 1024 + P * g
                    mm3(bank[(GROUP_POOL + g) % BANKS][:, :], w_hi[b1][:, c0:c0 + P], w_lo[b1][:, c0:c0 + P],
                        xg_hi[:, CAT + g, :], xg_lo[:, CAT + g, :], True, True).then_inc(acc_done, 1)
                for h in range(HEADS):
                    head_sum(1, h)

                def wait_pooled(k):
                    pe.wait_ge(pooled_lo, l * PG + k - CAT + 1)

                def wait_attended(k):
                    pe.wait_ge(o_lo_done, l * HEADS + 2 * (k - CAT) + 2 + C_OLO)

                def project(half, d, ready):
                    p = PAIR_OUT + 2 * half + d // 4
                    if d % 4 == 0:
                        wait_pair(l, p)
                    column_tile(l, GROUP_OUT + DT * half + d, d % BANKS, p % RING, P * (d % 4), 512, xg_hi, xg_lo,
                                range(CAT, DT), ready if d == 0 else nothing, blocks=4)

                for d in range(DT):
                    project(0, d, wait_pooled)
                    pe.wait_ge(factor_done, 2 * l + 1)
                    if d >= 2:
                        pe.wait_ge(k_normed, l * HEADS + d - 1)
                    for t in range(TT):
                        col = d * TT + t
                        last = nc.tensor.matmul(bank[SPREAD + d % 2][0:QK, t * P:(t + 1) * P],
                                                k_rstd[:, col:col + 1].to_broadcast([P, QK]), ident[:, :],
                                                start=True, stop=True)
                    last.then_inc(k_spread, 1)

                def scores(h, s, first=False):
                    pe.wait_ge(qk_lo, l * 8 + h + 1)
                    for t in range(TT):
                        if first:
                            wait_bank(l, GROUP_OUT + DT + t)
                        else:
                            pe.wait_ge(exp_done, l * 32 + 4 * h - 4 + t + 1)
                        mm3(bank[t][:, :], h_hi[0:QK, s, t * P:(t + 1) * P], h_lo[0:QK, s, t * P:(t + 1) * P],
                            h_hi[0:QK, 2 + s, :], h_lo[0:QK, 2 + s, :], True, True).then_inc(scores_done, 1)

                def turn(h, s, t):
                    pe.wait_ge(pt_lo_done, l * 32 + 4 * h + t + 1)
                    for q in range(TT):
                        if t == 0:
                            pe.wait_ge(prob_done if q % 2 == 0 else prob_dve, l * 16 + 2 * h + q // 2 + 1)
                        last = nc.tensor.transpose(bank[TRANS + t % 3][:, q * P:(q + 1) * P],
                                                   prob[:, s, q, t * P:(t + 1) * P], ident[:, :])
                    last.then_inc(trans_done, 1)

                def values(h, s, hp, t):
                    pe.wait_ge(pt_lo_done, l * 32 + 4 * h + t + 1 + C_PTLO)
                    if t == 0:
                        pe.wait_ge(o_lo_done, l * 8 + h + 1)
                        if s == 0:
                            pe.wait_ge(v_lo_done, l * 4 + hp + 1)
                    nc.tensor.matmul(bank[OUT][:, :], v_hi[:, t, :], h_hi[:, 4 + t, :], start=t == 0, stop=False)
                    nc.tensor.matmul(bank[OUT][:, :], v_lo[:, t, :], h_hi[:, 4 + t, :], start=False, stop=False)
                    nc.tensor.matmul(bank[OUT][:, :], v_hi[:, t, :], h_lo[:, 4 + t, :], start=False,
                                     stop=t == TT - 1).then_inc(pt_used, 1)

                def weigh(h, s, hp):
                    for t in range(3):
                        turn(h, s, t)
                    values(h, s, hp, 0)
                    turn(h, s, 3)
                    for t in range(1, TT):
                        values(h, s, hp, t)

                pe.wait_ge(k_normed, l * HEADS + HEADS)
                scores(0, 0, True)

                def head_pair(hp, last):
                    scores(2 * hp + 1, 1)
                    weigh(2 * hp, 0, hp)
                    if not last:
                        scores(2 * hp + 2, 0)
                    weigh(2 * hp + 1, 1, hp)

                with pe.Fori(0, HEADS // 2 - 1) as hp:
                    head_pair(hp, False)
                head_pair(HEADS // 2 - 1, True)

                for d in range(DT):
                    project(1, d, wait_attended)
                ffn(l, 1, PAIR_FFN2, GROUP_FFN2, N_FFN2, 2)

            pe.wait_ge(evac_done, DEPTH * DVE_GROUPS + BANKS)
            for n in range(2 * TT):
                t, half = n // 2, n % 2
                if n >= BANKS:
                    pe.wait_ge(y_copied, n - BANKS + 1)
                for d in range(4):
                    last = nc.tensor.transpose(bank[n % BANKS][:, d * P:(d + 1) * P], x[:, 4 * half + d, t * P:(t + 1) * P], ident[:, :])
                last.then_inc(y_turned, 1)

        @block.vector
        def _(dve):
            V = nc.vector
            dve.sem_inc(evac_done, BANKS)
            dve.sem_inc(lo_split, RING)
            dve.sem_inc(pt_lo_done, C_PTLO)
            dve.sem_inc(o_lo_done, C_OLO)
            V.memset(gain_rows[:, :], 1.0).then_inc(memset_done, 1)
            V.memset(ones[:, :], 1.0)
            V.memset(eps_t[:, 0:1], EPS)
            V.memset(eps_t[:, 1:2], EPS * QK).then_inc(memset_done, 1)
            dve.wait_ge(x_turned, 1)
            V.tensor_copy(gains[:, :], bank[SUMS][:, 0:P]).then_inc(gains_done, 1)
            dve.wait_ge(gains_done, 1)
            for l in range(DEPTH):
                k_col, q_col = l * VECS + V_KN, l * VECS + V_QN
                V.tensor_tensor(gains_qk[:, l:l + 1], gains[:, k_col:k_col + 1], gains[:, q_col:q_col + 1],
                                ALU.mult).then_inc(gains_done, 1)
            for d in range(DT):
                dve.wait_ge(x_turned, d + 2)
                V.tensor_copy(x[:, d, :], bank[d % BANKS][:, :]).then_inc(x_done, 1)
            dve.wait_ge(gains_done, 1 + DEPTH)

            def gain_x(l, n, v, d):
                dve.wait_ge(xg_hi_done, (3 * l + n) * DT + d + 1)
                wait_x(dve, l, n, d)
                V.scalar_tensor_tensor(out=xg_lo[:, d, :], in0=x[:, d, :], scalar=gain(l, v + d),
                                       in1=xg_hi[:, d, :].bitcast(F32), op0=ALU.mult, op1=ALU.subtract).then_inc(xg_lo_done, 1)

            def split_lo(l, p, b):
                dve.wait_ge(hi_split, l * PAIRS + p + 1 + RING)
                for (src, dst), (_, hi) in zip(split_parts(p, w_raw[b], w_lo[b]), split_parts(p, w_raw[b], w_hi[b])):
                    last = V.tensor_tensor(dst, src, hi.bitcast(F32), ALU.subtract)
                last.then_inc(lo_split, 1)

            def split_lo_at(l, p):
                split_lo(l, p, p % RING)

            def wait_group(l, g):
                start, add = (g, 0) if isinstance(g, int) else g
                dve.wait_ge(acc_done, l * GROUPS + start + 1 + add)
                skipped = ACT_GROUPS if start >= GROUP_POOL else 0
                dve.wait_ge(evac_done, l * DVE_GROUPS + (start - skipped + BANKS) + add)

            def rstd(l, n, dst):
                dve.wait_ge(rms_done, l * NORMS + n + 1)
                V.reciprocal(dst[:, :], dst[:, :]).then_inc(rstd_done, 1)

            def wait_rstd(l, n):
                dve.wait_ge(rstd_done, l * NORMS + n + 1)

            def add_to_x(l, g, bk, d, factor):
                wait_group(l, g)
                xd = x[:, d, :] if isinstance(d, int) else x[:, bass.ds(d, 1), :]
                ps = bank[bk][:, :] if isinstance(d, int) else bank[bk][:, :].rearrange("p (o s) -> p o s", o=1)
                V.scalar_tensor_tensor(out=xd, in0=ps, scalar=factor, in1=xd, op0=ALU.mult, op1=ALU.add).then_inc(evac_done, 1)

            def finish_x(l, pd, gd, factor, next_norm, next_v, last=False):
                for i in range(DT // 2):
                    for d in (2 * i, 2 * i + 1):
                        add_to_x(l, gd + d, d % BANKS, d, factor)
                        gain_x(l, next_norm, next_v, d)
                    if not (last and i >= DT // 2 - RING):
                        split_lo_at(l, pd + i + 2)

            def ffn(l, which, p0, g0, norm, next_norm, next_v, last):
                for c, n in enumerate(CHUNKS):
                    pc, gc = p0 + chunk_start(c), g0 + 2 * chunk_start(c)
                    f0 = which * FT + sum(CHUNKS[:c])
                    if c == 0:
                        rstd(l, norm, rstd_x)
                    with dve.Fori(0, n // 2) as i:
                        wait_rstd(l, norm)
                        for j in range(2):
                            wait_group(l, (gc + j, 4 * i))
                            V.tensor_tensor(gate[j][:, :], bank[j][:, :], rstd_x[:, :], ALU.mult).then_inc(evac_done, 1)
                        split_lo(l, pc + 2 * i + 2, 0)
                        for j in range(2):
                            f = l * 2 * FT + f0 + 2 * i + j
                            wait_group(l, (gc + 2 + j, 4 * i))
                            V.tensor_tensor(up[j][:, :], bank[2 + j][:, :], rstd_x[:, :], ALU.mult).then_inc(evac_done, 1)
                            wait_evac(dve, l, (gc + 2 + j, 4 * i))
                            dve.wait_ge(silu_done, f + 1)
                            V.tensor_tensor(hid[j][:, :], silu[j][:, :], up[j][:, :], ALU.mult).then_inc(hid_done, 1)
                            dve.wait_ge(h_hi_done, f + 1)
                            dve.wait_ge(hid_done, f + 1)
                            o1 = "p (o s) -> p o s"
                            V.tensor_tensor(h_lo[:, bass.ds(2 * i + j, 1), :], hid[j][:, :].rearrange(o1, o=1),
                                            h_hi[:, bass.ds(2 * i + j, 1), :].bitcast(F32), ALU.subtract).then_inc(h_lo_done, 1)
                        split_lo(l, pc + 2 * i + 3, 1)
                    pd, gd = pc + n, gc + 2 * n
                    if c < len(CHUNKS) - 1:
                        with dve.Fori(0, DT // 4) as i:
                            for b in range(2):
                                for j in range(2):
                                    add_to_x(l, (gd + 2 * b + j, 4 * i), 2 * b + j, 4 * i + 2 * b + j, 0.5)
                                split_lo(l, pd + 2 * i + b + 2, b)
                    else:
                        finish_x(l, pd, gd, 0.5, next_norm, next_v, last)

            for d in range(DT):
                gain_x(0, 0, V_FFN1, d)
            dve.wait_ge(const_loaded, 48)
            swap = [(i + 16) % 32 for i in range(32)]
            with dve.Fori(0, DEPTH) as l:
                step = [0]

                def link(ins):
                    step[0] += 1
                    ins.then_inc(dve_step, 1)
                    dve.wait_ge(dve_step, l * DVE_STEPS + step[0])

                for p in range(RING):
                    split_lo_at(l, p)
                ffn(l, 0, 0, 0, N_FFN1, 1, V_MIX, False)

                rstd(l, N_MIX, rstd_x)
                wait_rstd(l, N_MIX)
                M = GROUP_MIX
                ALL = slice(0, P)

                def scale_group(m, dst, rows_=ALL):
                    wait_group(l, M + m)
                    V.tensor_tensor(dst, bank[(M + m) % BANKS][rows_, :], rstd_x[rows_, :], ALU.mult).then_inc(evac_done, 1)

                def latent(t0, width):
                    for t in range(t0, t0 + width):
                        V.tensor_tensor(z[:, t, :], z[:, t, :], rstd_l[:, :], ALU.mult).then_inc(lat_scaled, 1)
                    for t in range(t0, t0 + width):
                        dve.wait_ge(lat_scaled, l * (QT + KT) + t + 1)
                        dve.wait_ge(lat_hi, l * (QT + KT) + t + 1)
                        V.scalar_tensor_tensor(out=h_lo[:, t, :], in0=z[:, t, :], scalar=gain(l, V_KVL + t),
                                               in1=h_hi[:, t, :].bitcast(F32), op0=ALU.mult, op1=ALU.subtract).then_inc(lat_lo, 1)

                for t in range(KT):
                    scale_group(t, z[:, t, :])
                split_lo_at(l, PAIR_MIX + 2)
                scale_group(2, z[:, KT, :])
                scale_group(3, z[:, KT + 1, :])
                rstd(l, N_KVL, rstd_l)
                wait_rstd(l, N_KVL)
                latent(0, KT)
                split_lo_at(l, PAIR_MIX + 3)
                scale_group(4, z[:, KT + 2, :])
                scale_group(5, k_pe[QK_NOPE:QK, :], slice(QK_NOPE, QK))
                split_lo_at(l, PAIR_MIX + 4)
                for side in (slice(0, PAD), slice(PAD + S, PW)):
                    V.memset(zp[:, :, side], 0.0)
                scale_group(6, zp[:, 0, PAD:PAD + S])
                rstd(l, N_QL, rstd_l)
                wait_rstd(l, N_QL)
                latent(KT, QT)
                scale_group(7, zp[:, 1, PAD:PAD + S])
                split_lo_at(l, PAIR_MIX + 5)

                def rope(dst, src, g, scaled, tmp, rows_):
                    link(V.tensor_scalar(scaled, src, g, None, ALU.mult))
                    V.tensor_tensor(dst, scaled, cos_t[rows_, :], ALU.mult)
                    link(V.stream_shuffle(tmp, scaled, swap))
                    link(V.tensor_tensor(tmp, tmp, sin_t[rows_, :], ALU.mult))
                    return V.tensor_tensor(dst, dst, tmp, ALU.add)

                R = slice(QK_NOPE, QK)
                dve.wait_ge(lat_lo, l * (QT + KT) + QT + KT)
                rope(k_rot[R, :], k_pe[R, :], gains[R, bass.ds(l * VECS + V_KPE, 1)], rot_a[R, :], rot_b[R, :], R).then_inc(k_rope_done, 1)
                scale_group(8, zp[:, 2, PAD:PAD + S])
                scale_group(9, zp[:, 3, PAD:PAD + S])
                split_lo_at(l, PAIR_MIX + 6)
                dve.wait_ge(evac_done, l * DVE_GROUPS + GROUP_UK + BANKS)
                for g in range(PG):
                    dve.wait_ge(windowed, l * PG + g + 1)
                    V.scalar_tensor_tensor(out=zp[:, g, PAD:PAD + S], in0=win_s[:, PAD:PAD + S], scalar=0.5 ** (g + 1),
                                           in1=zp[:, g, PAD:PAD + S], op0=ALU.mult, op1=ALU.subtract).then_inc(mixed_done, 1)
                    if g == 0:
                        split_lo_at(l, PAIR_MIX + 7)
                for g in range(PG):
                    dve.wait_ge(mixed_done, l * PG + g + 1)
                    dve.wait_ge(mixed_hi, l * PG + g + 1)
                    V.tensor_tensor(xg_lo[:, CAT + g, :], zp[:, g, PAD:PAD + S], xg_hi[:, CAT + g, :].bitcast(F32),
                                    ALU.subtract).then_inc(mixed_lo, 1)
                split_lo_at(l, PAIR_MIX + 8)
                dve.wait_ge(evac_act, l * ACT_GROUPS + ACT_GROUPS)
                for r in range(2):
                    rope(q_rope[:, r, :], q_pe[:, r, :], gain(l, V_QPE), rot_a[:, :], rot_b[:, :], ALL).then_inc(q_rope_done, 1)
                    dve.wait_ge(q_rope_done, 2 * l + r + 1)

                def head_factor(n, dst):
                    dve.wait_ge(root_done, 2 * l + n + 1)
                    V.reciprocal(dst[:, :], dst[:, :]).then_inc(factor_done, 1)

                head_factor(0, k_rstd)
                for g in range(PG):
                    wait_group(l, GROUP_POOL + g)
                    V.tensor_scalar(pooled[g % 2][:, :], bank[(GROUP_POOL + g) % BANKS][:, :], gain(l, V_PS + g), None,
                                    ALU.mult).then_inc(evac_done, 1)
                    wait_evac(dve, l, GROUP_POOL + g)
                    dve.wait_ge(pooled_hi, l * PG + g + 1)
                    V.tensor_tensor(xg_lo[:, CAT + g, :], pooled[g % 2][:, :], xg_hi[:, CAT + g, :].bitcast(F32),
                                    ALU.subtract).then_inc(pooled_lo, 1)
                split_lo_at(l, PAIR_MIX + 9)
                dve.wait_ge(k_filled, 3 * l + 3)
                for d in range(DT):
                    add_to_x(l, GROUP_OUT + d, d % BANKS, d, 1.0)
                    dve.wait_ge(k_spread, l * HEADS + d + 1)
                    V.scalar_tensor_tensor(out=k_all[0:QK, d, :], in0=k_all[0:QK, d, :], scalar=gains_qk[0:QK, bass.ds(l, 1)],
                                           in1=bank[SPREAD + d % 2][0:QK, :], op0=ALU.mult, op1=ALU.mult).then_inc(k_normed, 1)
                    if d == 1:
                        head_factor(1, q_rstd)
                split_lo_at(l, PAIR_MIX + 10)
                split_lo_at(l, PAIR_MIX + 11)

                dve.wait_ge(factor_done, 2 * l + 2)

                def maximum(h, s, t):
                    dve.wait_ge(scores_done, l * 32 + 4 * h + t + 1)
                    V.reduce_max(row_max[:, s, t:t + 1], bank[t][:, :], AX_X).then_inc(max_done, 1)
                    dve.wait_ge(max_done, l * 32 + 4 * h + t + 1)
                    col = slice(4 * h + t, 4 * h + t + 1) if isinstance(h, int) else bass.ds(4 * h + t, 1)
                    V.tensor_scalar(neg_max[:, s, t:t + 1], row_max[:, s, t:t + 1], q_rstd[:, col], -1.0,
                                    ALU.mult, ALU.mult).then_inc(neg_done, 1)

                def inverse(h, s, t):
                    dve.wait_ge(exp_done, l * 32 + 4 * h + t + 1)
                    V.reciprocal(row_inv[:, s, t:t + 1], row_sum[:, s, t:t + 1]).then_inc(inv_done, 1)
                    if t % 2:
                        dve.wait_ge(inv_done, l * 32 + 4 * h + t + 1)
                        V.tensor_scalar(prob[:, s, t, :], prob[:, s, t, :], row_inv[:, s, t:t + 1], None,
                                        ALU.mult).then_inc(prob_dve, 1)

                def prob_t_lo(h, t):
                    dve.wait_ge(pt_hi_done, l * 32 + 4 * h + t + 1)
                    V.tensor_tensor(h_lo[:, 4 + t, :], bank[TRANS + t % 3][:, :], h_hi[:, 4 + t, :].bitcast(F32),
                                    ALU.subtract).then_inc(pt_lo_done, 1)

                def head_pair(hp, last):
                    for s in range(2):
                        h, more = 2 * hp + s, not (last and s == 1)
                        if more:
                            for t in range(3):
                                maximum(h + 1, 1 - s, t)
                            inverse(h + 1, 1 - s, 0)
                            maximum(h + 1, 1 - s, 3)
                            inverse(h + 1, 1 - s, 1)
                        prob_t_lo(h, 0)
                        if more:
                            inverse(h + 1, 1 - s, 2)
                        prob_t_lo(h, 1)
                        if more:
                            inverse(h + 1, 1 - s, 3)
                        prob_t_lo(h, 2)
                        prob_t_lo(h, 3)
                        dve.wait_ge(o_hi_done, l * 8 + h + 1)
                        V.tensor_tensor(xg_lo[64 * s:64 * s + 64, bass.ds(CAT + hp, 1), :],
                                        bank[OUT][64 * s:64 * s + 64, :].rearrange("p (o s) -> p o s", o=1),
                                        xg_hi[64 * s:64 * s + 64, bass.ds(CAT + hp, 1), :].bitcast(F32),
                                        ALU.subtract).then_inc(o_lo_done, 1)

                for t in range(TT):
                    maximum(0, 0, t)
                for t in range(TT):
                    inverse(0, 0, t)
                with dve.Fori(0, HEADS // 2 - 1) as hp:
                    head_pair(hp, False)
                head_pair(HEADS // 2 - 1, True)

                for n in range(2):
                    for d in range(4 * n, 4 * n + 4):
                        add_to_x(l, GROUP_OUT + DT + d, d % BANKS, d, 1.0)
                        if n == 0:
                            gain_x(l, 2, V_FFN2, d)
                    split_lo_at(l, PAIR_FFN2 + n)
                for d in range(4, DT):
                    gain_x(l, 2, V_FFN2, d)
                ffn(l, 1, PAIR_FFN2, GROUP_FFN2, N_FFN2, 3, VECS + V_FFN1, True)
                assert step[0] == DVE_STEPS, step[0]

            for n in range(2 * TT):
                t, half = n // 2, n % 2
                dve.wait_ge(y_turned, n + 1)
                V.tensor_copy(y_tok[:, t, 512 * half:512 * half + 512], bank[n % BANKS][:, :]).then_inc(y_copied, 1)

        @block.gpsimd
        def _(pool):
            G = nc.gpsimd
            G.memset(ident[:, :], 0.0).then_inc(pool_step, 1)
            pool.wait_ge(pool_step, 1)
            G.affine_select(out=ident[:, :], in_=ident[:, :], compare_op=ALU.not_equal, fill=1.0,
                            base=0, pattern=[[-1, P]], channel_multiplier=1).then_inc(ident_done, 1)
            step = [0]

            def link(l, ins, base):
                step[0] += 1
                ins.then_inc(pool_step, 1)
                pool.wait_ge(pool_step, l * POOL_STEPS + base + step[0])

            def sum_squares(l, tiles, total, wait, base):
                for n, t in enumerate(tiles):
                    wait(n)
                    sq = G.tensor_tensor(total[:, :] if n == 0 else square[:, :], t, t, ALU.mult)
                    if n:
                        link(l, sq, base)
                        last = G.tensor_tensor(total[:, :], total[:, :], square[:, :], ALU.add)
                        if n < len(tiles) - 1:
                            link(l, last, base)
                    else:
                        first = sq
                        link(l, first, base)
                last.then_inc(sumsq_done, 1)

            def x_squares(l, n, base):
                sum_squares(l, [x[:, d, :] for d in range(DT)], sumsq_x,
                            lambda d: wait_x(pool, l, n, d), base)

            x_squares(0, 0, 1)
            B = 1 + step[0]
            assert step[0] == X_LINKS
            step[0] = 0
            with pool.Fori(0, DEPTH) as l:
                x_squares(l, 1, B)
                sum_squares(l, [z[:, t, :] for t in range(KT)], sumsq_l[0],
                            lambda t: wait_evac(pool, l, GROUP_MIX + t), B)
                sum_squares(l, [z[:, KT + t, :] for t in range(QT)], sumsq_l[1],
                            lambda t: wait_evac(pool, l, GROUP_MIX + KT + t), B)
                for g in range(PG):
                    wait_evac(pool, l, GROUP_MIX + 6 + g)
                    src, a, b = zp[:, g, :], 0, PW
                    for n in range(g + 1):
                        s0, s1 = (1, 0) if n == 0 else (2 ** (n - 1), 2 ** (n - 1))
                        lo, hi = a + s0, b - s1
                        final = n == g
                        dst = win_s if final else (win_a, win_b)[n % 2]
                        if final and g >= 1:
                            pool.wait_ge(mixed_done, l * PG + g)
                        src0 = src[:, lo - s0:hi - s0]
                        src1 = src[:, lo + s1:hi + s1]
                        link(l, G.tensor_tensor(dst[:, lo:hi], src0, src1, ALU.add), B)
                        src, a, b = dst, lo, hi
                    G.tensor_tensor(win_s[:, PAD:2 * PAD], win_s[:, PAD:2 * PAD], edge[:, g, 0:PAD], ALU.mult)
                    G.tensor_tensor(win_s[:, S:S + PAD], win_s[:, S:S + PAD], edge[:, g, PAD:2 * PAD],
                                    ALU.mult).then_inc(windowed, 1)
                for h in range(HEADS):
                    if h % 2 == 0:
                        wait_evac(pool, l, GROUP_UK + h // 2)
                    if h == 0:
                        pool.wait_ge(k_filled, 3 * l + 2)
                    if h >= 2:
                        pool.wait_ge(head_sums, l * 2 * HEADS + h - 1)
                    G.tensor_tensor(sq_k[h % 2][0:QK_NOPE, :], k_all[0:QK_NOPE, h, :], k_all[0:QK_NOPE, h, :],
                                    ALU.mult).then_inc(k_sq, 1)

                def split_qk(h, s, dyn):
                    ix = bass.ds(h, 1) if dyn else slice(h, h + 1)
                    pool.wait_ge(qk_hi, l * 8 + h + 1)
                    for src, o in ((q_all, 0), (k_all, 2)):
                        last = G.tensor_tensor(h_lo[0:QK, o + s:o + s + 1, :], src[0:QK, ix, :],
                                               h_hi[0:QK, o + s:o + s + 1, :].bitcast(F32), ALU.subtract)
                    last.then_inc(qk_lo, 1)

                def normalise(h, s, t):
                    pool.wait_ge(inv_done, l * 32 + 4 * h + t + 1)
                    G.tensor_tensor(prob[:, s, t, :], prob[:, s, t, :], row_inv[:, s, t:t + 1].to_broadcast([P, S]),
                                    ALU.mult).then_inc(prob_done, 1)

                def split_v(hp):
                    pool.wait_ge(v_hi_done, l * 4 + hp + 1)
                    G.tensor_tensor(v_lo[:, :, :], v_all[:, :, bass.ds(P * hp, P)], v_hi[:, :, :].bitcast(F32),
                                    ALU.subtract).then_inc(v_lo_done, 1)

                for h in range(2):
                    split_qk(h, h, False)
                for t in (0, 2):
                    normalise(0, 0, t)

                def head_pair(hp, last):
                    for s in range(2):
                        h = 2 * hp + s
                        if s == 0:
                            split_v(hp)
                        if not last:
                            split_qk(h + 2, s, True)
                        if not (last and s == 1):
                            for t in (0, 2):
                                normalise(h + 1, 1 - s, t)

                with pool.Fori(0, HEADS // 2 - 1) as hp:
                    head_pair(hp, False)
                head_pair(HEADS // 2 - 1, True)
                x_squares(l, 2, B)
                x_squares(l, 3, B)
                assert step[0] == POOL_STEPS, step[0]


_INS = ["x", "ffn1_norm", "ffn1_w_gu", "ffn1_w_down", "mix_norm", "w_in", "q_lat_norm", "kv_lat_norm",
        "w_uq", "w_uk", "w_uv", "q_norm", "k_norm", "w_pool", "pool_scale", "w_out",
        "ffn2_norm", "ffn2_w_gu", "ffn2_w_down"]


def shape_tables(seq):
    import numpy as np

    half = QK_ROPE // 2
    inv = np.float32(10000.0) ** (-np.arange(0, QK_ROPE, 2, dtype=np.float32) / np.float32(QK_ROPE))
    ang = np.arange(seq, dtype=np.float32)[None, :] * inv.astype(np.float32)[:, None]
    cos, sin = np.cos(ang).astype(np.float32), np.sin(ang).astype(np.float32)
    groups = P // QK_ROPE
    rope_cos = np.tile(np.concatenate([cos, cos]), (groups, 1))
    rope_sin = np.tile(np.concatenate([-sin, sin]), (groups, 1))
    pos = np.concatenate([np.arange(PAD), np.arange(seq - PAD, seq)])
    edge = []
    for w in (2, 4, 8, 16):
        count = np.minimum(pos + w // 2, seq) - np.maximum(pos - w // 2, 0)
        edge.append(w / count)
    edge = np.tile(np.concatenate(edge).astype(np.float32)[None, :], (P, 1))
    assert rope_cos.shape == (P, seq) and half == 16
    return {"rope_cos": rope_cos, "rope_sin": rope_sin, "pool_edge": edge}


def kernel(**inputs):
    import numpy as np
    import concourse.bacc as bacc
    from concourse.bass_utils import run_bass_kernel_spmd

    nc = bacc.Bacc("TRN2", target_bir_lowering=False, num_devices=1)
    arrays, args = {}, []
    given = {name: np.ascontiguousarray(inputs[name]) for name in _INS}
    shape = given["x"].shape
    given.update(shape_tables(shape[1]))
    for name, a in given.items():
        arrays[f"in_{name}"] = a
        args.append(nc.dram_tensor(f"in_{name}", a.shape, mybir.dt.from_np(a.dtype), kind="ExternalInput").ap())
    args.append(nc.dram_tensor("out_y", shape, F32, kind="ExternalOutput").ap())
    build_trunk(nc, *args)
    r = run_bass_kernel_spmd(nc, [arrays], core_ids=[0])
    return r.results[0]["out_y"]
```

```python
from contextlib import ExitStack

import concourse.bass as bass
from concourse import mybir

F32 = mybir.dt.float32
F32R = mybir.dt.float32r
ACT = mybir.ActivationFunctionType
ALU = mybir.AluOpType
AX_X = mybir.AxisListType.X

P = 128
EPS = 1e-6
QK_NOPE, QK_ROPE, V_HEAD = 64, 32, 64
QK = QK_NOPE + QK_ROPE
PAD = 8
RING = 2
BANKS = 4


def build_trunk(nc, x_in, ffn1_norm, ffn1_w_gu, ffn1_w_down, mix_norm, w_in, q_lat_norm, kv_lat_norm,
                w_uq, w_uk, w_uv, q_norm, k_norm, w_pool, pool_scale, w_out,
                ffn2_norm, ffn2_w_gu, ffn2_w_down, rope_cos, rope_sin, pool_edge, y_out):
    _, S, D = x_in.shape
    DEPTH = ffn1_w_gu.shape[0]
    F = ffn1_w_down.shape[1]
    QL, KVL = w_uq.shape[1], w_uk.shape[1]
    HEADS = w_uq.shape[2] // QK
    PG = w_pool.shape[1]
    DT, TT, FT = D // P, S // P, F // P
    QT, KT = QL // P, KVL // P
    CAT = HEADS * V_HEAD // P
    O_KV, O_PE, O_POOL = QL, QL + KVL, QL + KVL + QK_ROPE
    assert S == 512 and DT == 8 and TT == 4 and QT == 3 and KT == 2 and PG == 4 and HEADS == 8

    CHUNKS = [8, 8, FT - 16]
    assert all(n % 2 == 0 and 0 < n <= 8 for n in CHUNKS)
    FFN_PAIRS = FT + len(CHUNKS) * DT // 2
    MIX_PAIRS, OUT_PAIRS = 8, DT // 2
    MIX_GROUPS = 10 + 4 + 4 + 6 + 4
    PAIR_MIX = FFN_PAIRS
    PAIR_OUT = PAIR_MIX + MIX_PAIRS
    PAIR_FFN2 = PAIR_OUT + OUT_PAIRS
    PAIRS = PAIR_FFN2 + FFN_PAIRS
    GROUP_MIX = 2 * FFN_PAIRS
    GROUP_UK = GROUP_MIX + 10
    GROUP_UV, GROUP_UQ, GROUP_POOL = GROUP_UK + 4, GROUP_UK + 8, GROUP_UK + 14
    GROUP_OUT = GROUP_MIX + MIX_GROUPS
    GROUP_FFN2 = GROUP_OUT + 2 * DT
    GROUPS = GROUP_FFN2 + 2 * FFN_PAIRS
    ACT_GROUPS = GROUP_POOL - GROUP_UK
    DVE_GROUPS = GROUPS - ACT_GROUPS
    assert PAIRS % RING == 0 and PAIR_MIX % RING == 0 and PAIR_FFN2 % RING == 0
    assert GROUPS % BANKS == 0 and GROUP_MIX % BANKS == 0 and GROUP_FFN2 % BANKS == 0 and GROUP_OUT % BANKS == 0
    NORMS = 5
    N_FFN1, N_MIX, N_KVL, N_QL, N_FFN2 = range(NORMS)

    V_FFN1, V_MIX, V_FFN2 = (0, DT), (DEPTH * DT, DT), (2 * DEPTH * DT, DT)
    at = 3 * DEPTH * DT
    V_KVL, V_QL, V_PS = (at, KT), (at + DEPTH * KT, QT), (at + DEPTH * (KT + QT), PG)
    at += DEPTH * (KT + QT + PG)
    V_QN, V_KN, V_QPE, V_KPE = ((at + i * DEPTH, 1) for i in range(4))
    assert at + 4 * DEPTH <= P
    V_NEXT = (V_FFN1[0] + DT, DT)
    DVE_STEPS = 9
    X_LINKS = 2 * DT - 2
    POOL_STEPS = 3 * X_LINKS + 2 * QT - 2 + 2 * KT - 2 + PG * (PG + 1) // 2

    with ExitStack() as ctx:
        TB = 4 * S
        arena_bytes = 103 * TB
        arena = ctx.enter_context(nc.sbuf_tensor("arena", [P, arena_bytes // 4], F32))
        base = nc.sbuf_base - arena_bytes
        used = [0]

        def place(name, shape, dt, at=None):
            size = 4
            for n in shape[1:]:
                size *= n
            if at is None:
                at = used[0]
                used[0] += (size + 31) // 32 * 32
                assert used[0] <= arena_bytes, name
            return nc.alloc_sbuf_tensor_at(name, shape, dt, offset=base + at), at

        w_raw = [place(f"w_raw{b}", [P, 2048], F32)[0] for b in range(RING)]
        w_hi = [place(f"w_hi{b}", [P, 2048], F32R)[0] for b in range(RING)]
        w_lo = [place(f"w_lo{b}", [P, 2048], F32R)[0] for b in range(RING)]
        x, _ = place("x", [P, DT, S], F32)
        xg_hi, at_xg_hi = place("xg_hi", [P, DT, S], F32R)
        xg_lo, at_xg_lo = place("xg_lo", [P, DT, S], F32R)
        sq_k = [place(f"sq_k{i}", [P, S], F32, at_xg_hi + i * TB)[0] for i in range(4)]
        q_rope, _ = place("q_rope", [P, 2, S], F32, at_xg_lo + 2 * TB)
        h_hi, at_h_hi = place("h_hi", [P, 8, S], F32R)
        h_lo, at_h_lo = place("h_lo", [P, 8, S], F32R)
        sq_q = [place(f"sq_q{i}", [P, S], F32, (at_h_hi, at_h_lo)[i // 4] + (4 + i % 4) * TB)[0] for i in range(HEADS)]
        v_hi, at_v_hi = place("v_hi", [P, TT, P], F32R)
        v_lo, at_v_lo = place("v_lo", [P, TT, P], F32R)
        mix3_hi, _ = place("mix3_hi", [P, S], F32R, at_v_hi)
        mix3_lo, _ = place("mix3_lo", [P, S], F32R, at_v_lo)
        mix_hi = [h_hi[:, QT + KT + g, :] for g in range(PG - 1)] + [mix3_hi[:, :]]
        mix_lo = [h_lo[:, QT + KT + g, :] for g in range(PG - 1)] + [mix3_lo[:, :]]
        q_all, at_q = place("q_all", [P, HEADS, S], F32)
        k_all, at_k = place("k_all", [P, HEADS, S], F32)
        v_all, _ = place("v_all", [P, TT, HEADS * V_HEAD], F32)
        gate = [place(f"gate{i}", [P, S], F32, at_q + i * TB)[0] for i in range(2)]
        up = [place(f"up{i}", [P, S], F32, at_q + (2 + i) * TB)[0] for i in range(2)]
        silu = [place(f"silu{i}", [P, S], F32, at_q + (4 + i) * TB)[0] for i in range(2)]
        hid = [place(f"hid{i}", [P, S], F32, at_q + (6 + i) * TB)[0] for i in range(2)]
        PW = S + 2 * PAD
        zp, _ = place("zp", [P, PG, PW], F32, at_q)
        win_a, _ = place("win_a", [P, PW], F32, at_q + 4 * 4 * PW)
        win_b, _ = place("win_b", [P, PW], F32, at_q + 5 * 4 * PW)
        win_s, _ = place("win_s", [P, PW], F32, at_q + 6 * 4 * PW)
        assert 7 * 4 * PW <= HEADS * TB
        x_tok, _ = place("x_tok", [P, TT, D], F32, at_k)
        y_tok, _ = place("y_tok", [P, TT, D], F32, at_k)
        prob, at_a = place("prob", [P, 2, TT, S], F32)
        z, _ = place("z", [P, QT + KT, S], F32, at_a)
        q_pe, _ = place("q_pe", [P, 2, S], F32, at_a)
        rot_a, _ = place("rot_a", [P, S], F32, at_a + 2 * TB)
        rot_b, _ = place("rot_b", [P, S], F32, at_a + 3 * TB)
        k_pe, _ = place("k_pe", [P, S], F32, at_a + 5 * TB)
        sumsq_l = [place(f"sumsq_l{i}", [P, S], F32, at_a + (6 + i) * TB)[0] for i in range(2)]
        cos_t, _ = place("cos_t", [P, S], F32)
        sin_t, _ = place("sin_t", [P, S], F32)
        k_rot, _ = place("k_rot", [P, S], F32)
        rstd_x, _ = place("rstd_x", [P, S], F32)
        rstd_l, _ = place("rstd_l", [P, S], F32)
        sumsq_x, _ = place("sumsq_x", [P, S], F32)
        square, _ = place("square", [P, S], F32)
        ones, _ = place("ones", [P, P], F32)
        ident, _ = place("ident", [P, P], F32)
        gain_rows, _ = place("gain_rows", [P, P], F32)
        gains, _ = place("gains", [P, P], F32)
        gains_qk, _ = place("gains_qk", [P, DEPTH], F32)
        edge, _ = place("edge", [P, PG, 2 * PAD], F32)
        eps_t, _ = place("eps_t", [P, 2], F32)
        k_rstd, _ = place("k_rstd", [P, HEADS * TT], F32)
        q_rstd, _ = place("q_rstd", [P, HEADS * TT], F32)
        row_max, _ = place("row_max", [P, 2, TT], F32)
        neg_max, _ = place("neg_max", [P, 2, TT], F32)
        row_sum, _ = place("row_sum", [P, 2, TT], F32)
        row_inv, _ = place("row_inv", [P, 2, TT], F32)

        psum = ctx.enter_context(nc.psum_tensor("psum", [P, 8, S], F32))
        bank = [psum[:, i, :] for i in range(8)]
        SUMS, SPREAD, TRANS, OUT = 4, 5, 4, 7

        def sem(name):
            return ctx.enter_context(nc.semaphore(name))

        const_loaded, memset_done, ident_done = sem("const_loaded"), sem("memset_done"), sem("ident_done")
        gains_loaded, gains_turned, gains_done = sem("gains_loaded"), sem("gains_turned"), sem("gains_done")
        x_loaded, x_turned = [sem(f"x_loaded{t}") for t in range(TT)], sem("x_turned")
        y_turned, y_stored = sem("y_turned"), sem("y_stored")
        y_copied = [sem("y_copied_act"), sem("y_copied_dve")]
        raw_loaded = [sem(f"raw_loaded{b}") for b in range(RING)]
        hi_split, lo_split = sem("hi_split"), sem("lo_split")
        acc_done, evac_done, evac_act = sem("acc_done"), sem("evac_done"), sem("evac_act")
        x_done = [sem("x_done_dve"), sem("x_done_act")]
        DVE_TILES = 5
        xg_hi_done, xg_lo_done = sem("xg_hi_done"), sem("xg_lo_done")
        pool_step = sem("pool_step")
        sumsq_done, sums_done, rms_done, rstd_done = sem("sumsq_done"), sem("sums_done"), sem("rms_done"), sem("rstd_done")
        silu_done, hid_done, h_hi_done, h_lo_done = sem("silu_done"), sem("hid_done"), sem("h_hi_done"), sem("h_lo_done")
        dve_step = sem("dve_step")
        lat_scaled, lat_hi, lat_lo = sem("lat_scaled"), sem("lat_hi"), sem("lat_lo")
        windowed, mixed_done, mixed_hi, mixed_lo = sem("windowed"), sem("mixed_done"), sem("mixed_hi"), sem("mixed_lo")
        pooled_hi, q_sq_rope = sem("pooled_hi"), sem("q_sq_rope")
        k_rope_done, k_filled, q_rope_done, q_filled = sem("k_rope_done"), sem("k_filled"), sem("q_rope_done"), sem("q_filled")
        k_sq, k_sq_rope, q_sq, head_sums, root_done, factor_done = sem("k_sq"), sem("k_sq_rope"), sem("q_sq"), sem("head_sums"), sem("root_done"), sem("factor_done")
        k_spread, k_normed = sem("k_spread"), sem("k_normed")
        qk_hi, qk_lo, v_hi_done, v_lo_done = sem("qk_hi"), sem("qk_lo"), sem("v_hi_done"), sem("v_lo_done")
        scores_done, max_done, neg_done, exp_done = sem("scores_done"), sem("max_done"), sem("neg_done"), sem("exp_done")
        inv_done, prob_done, prob_dve, trans_done = sem("inv_done"), sem("prob_done"), sem("prob_dve"), sem("trans_done")
        pt_hi_done, pt_lo_done, pt_used = sem("pt_hi_done"), sem("pt_lo_done"), sem("pt_used")
        o_hi_done, o_lo_done = sem("o_hi_done"), sem("o_lo_done")
        C_TRANS, C_PTLO, C_PTUSED, C_OLO = 2 * TT, 3, TT, 1

        def rows(w):
            return w.rearrange("l (k p) n -> l p k n", p=P)

        def gain(l, v, k=0):
            return gains[:, bass.ds(l * v[1] + (v[0] + k), 1)]

        def latent_gain(l, t):
            return gain(l, V_KVL, t) if t < KT else gain(l, V_QL, t - KT)

        def pairs_of(buf, width, blocks=8, at=0):
            return buf[:, at:at + blocks * width].rearrange("p (k n) -> p k n", n=width)

        def chunk_start(c):
            return sum(CHUNKS[:c]) + c * DT // 2

        def used_at(p):
            if p < PAIR_MIX:
                return 2 * p + 2
            if p < PAIR_OUT:
                return [GROUP_MIX + 2, GROUP_MIX + 4, GROUP_MIX + 6, GROUP_MIX + 8, GROUP_UK, GROUP_UQ,
                        GROUP_POOL, GROUP_OUT][p - PAIR_MIX]
            if p < PAIR_FFN2:
                return GROUP_OUT + 4 * (p - PAIR_OUT) + 4
            return GROUP_FFN2 + 2 * (p - PAIR_FFN2) + 2

        def wait_evac(eng, l, g, back=0):
            start, add = (g, 0) if isinstance(g, int) else g
            if GROUP_UK <= start - back < GROUP_POOL:
                eng.wait_ge(evac_act, l * ACT_GROUPS + start - back - GROUP_UK + 1)
            else:
                skipped = ACT_GROUPS if start - back >= GROUP_POOL else 0
                eng.wait_ge(evac_done, l * DVE_GROUPS + (start - back - skipped + 1 + BANKS) + add)

        def split_parts(p, raw, split):
            if not isinstance(p, int) or p not in (PAIR_MIX + 6, PAIR_MIX + 7):
                return [(raw[:, :], split[:, :])]
            slots = 2 if p == PAIR_MIX + 6 else 1
            v_raw, v_split = (b[:, 0:1024 * slots].rearrange("p (k n) -> p k n", k=slots) for b in (raw, split))
            heads = v_raw[:, :, 0:HEADS * QK].rearrange("p k (h n) -> p k h n", n=QK)
            out = []
            for a, b, c0 in ((0, QK_NOPE, 0), (QK_NOPE, QK, HEADS * QK_NOPE)):
                dst = v_split[:, :, c0:c0 + HEADS * (b - a)].rearrange("p k (h n) -> p k h n", n=b - a)
                out.append((heads[:, :, :, a:b], dst))
            if slots == 1:
                out.append((raw[:, 1024:1024 + PG * P], split[:, 1024:1024 + PG * P]))
            return out

        def out_bank(half, d):
            return (OUT, SPREAD + 1)[d - (DT - 2)] if half == 0 and d >= DT - 2 else d % BANKS

        def wait_x(eng, l, n, d):
            if n == 0:
                by_act = d >= DVE_TILES
                eng.wait_ge(x_done[by_act], d - DVE_TILES * by_act + 1)
            else:
                end = (GROUP_MIX, GROUP_FFN2, GROUPS)[n - 1]
                wait_evac(eng, l, end - DT + d)

        M_POOL, M_PE, M_Q = KT, KT + PG, KT + PG + 1
        Q_ORDER = (2, 0, 1)

        block = ctx.enter_context(nc.Block())

        @block.sync
        def _(sp):
            for t in range(TT):
                sp.dma_start(x_tok[:, t, :], x_in[0, t * P:(t + 1) * P, :]).then_inc(x_loaded[t], 16)

            def wait_free(l, p):
                sp.wait_ge(lo_split, l * PAIRS + p + 1)

            def load_columns(l, p, b, w, r0, blocks, col, width=256):
                wait_free(l, p)
                half = blocks // 2
                dst = pairs_of(w_raw[b], width, blocks)
                for k in (half, 0):
                    sp.dma_start(dst[:, k:k + half, :],
                                 rows(w)[l, :, r0 + k:r0 + k + half, col]).then_inc(raw_loaded[b], 16)

            def load_ffn(l, p0, w_gu, w_down):
                for c, n in enumerate(CHUNKS):
                    pc, f0 = p0 + chunk_start(c), P * sum(CHUNKS[:c])
                    with sp.Fori(0, n // 2) as i:
                        load_columns(l, pc + 2 * i, 0, w_gu, 0, DT, bass.ds(f0 + 256 * i, 256))
                        load_columns(l, pc + 2 * i + 1, 1, w_gu, 0, DT, bass.ds(F + f0 + 256 * i, 256))
                    with sp.Fori(0, DT // 4) as i:
                        for b in range(2):
                            load_columns(l, pc + n + 2 * i + b, b, w_down, f0 // P, n,
                                         bass.ds(512 * i + 256 * b, 256))

            with sp.Fori(0, DEPTH) as l:
                load_ffn(l, 0, ffn1_w_gu, ffn1_w_down)
                p = PAIR_MIX
                load_columns(l, p, p % RING, w_in, 0, DT, slice(O_KV, O_KV + 256))
                load_columns(l, p + 1, (p + 1) % RING, w_in, 0, DT, slice(O_POOL, O_POOL + 256))
                load_columns(l, p + 2, p % RING, w_in, 0, DT, slice(O_POOL + 256, O_POOL + 512))
                wait_free(l, p + 3)
                for at, col, width in ((0, O_PE - QK_NOPE, QK), (1024, 256, P)):
                    sp.dma_start(w_raw[(p + 3) % RING][:, at:at + DT * width].rearrange("p (k n) -> p k n", k=DT),
                                 rows(w_in)[l, :, :, col:col + width]).then_inc(raw_loaded[(p + 3) % RING], 16)
                load_columns(l, p + 4, p % RING, w_in, 0, DT, slice(0, 256))
                p += 5
                wait_free(l, p)
                for at, w in ((0, w_uk), (1024, w_uv)):
                    sp.dma_start(w_raw[p % RING][:, at:at + 1024].rearrange("p (k n) -> p k n", k=KT),
                                 rows(w)[l]).then_inc(raw_loaded[p % RING], 16)
                p += 1
                wait_free(l, p)
                for k in range(2):
                    sp.dma_start(w_raw[p % RING][:, 1024 * k:1024 * k + HEADS * QK],
                                 rows(w_uq)[l, :, k, :]).then_inc(raw_loaded[p % RING], 16)
                p += 1
                wait_free(l, p)
                sp.dma_start(w_raw[p % RING][:, 0:HEADS * QK], rows(w_uq)[l, :, 2, :]).then_inc(raw_loaded[p % RING], 16)
                sp.dma_start(w_raw[p % RING][:, 1024:1024 + PG * P].rearrange("p (g n) -> p g n", g=PG),
                             w_pool.rearrange("l g c d -> l c g d")[l]).then_inc(raw_loaded[p % RING], 16)
                for n in range(OUT_PAIRS):
                    r0, c0 = (CAT, 0)[n // 2], 512 * (n % 2)
                    load_columns(l, PAIR_OUT + n, n % 2, w_out, r0, 4, slice(c0, c0 + 512), 512)
                load_ffn(l, PAIR_FFN2, ffn2_w_gu, ffn2_w_down)
            for p in range(RING):
                wait_free(DEPTH, p)
                sp.dma_start(pairs_of(w_raw[p], 256), rows(ffn1_w_gu)[0, :, :, 0:256]).then_inc(raw_loaded[p], 32)
            for half in range(2):
                for t in range(TT):
                    sp.wait_ge(y_copied[half], t + 1)
                    part = slice(512 * half, 512 * half + 512)
                    sp.dma_start(y_out[0, t * P:(t + 1) * P, part], y_tok[:, t, part]).then_inc(y_stored, 16)
            sp.wait_ge(y_stored, 16 * 2 * TT)

        @block.scalar
        def _(act):
            act.sem_inc(hi_split, RING)
            act.wait_ge(memset_done, 1)
            for v, w in ((V_FFN1, ffn1_norm), (V_MIX, mix_norm), (V_FFN2, ffn2_norm), (V_QL, q_lat_norm),
                         (V_KVL, kv_lat_norm), (V_PS, pool_scale)):
                act.dma_start(gain_rows[v[0]:v[0] + DEPTH * v[1], :], w.rearrange("l (k p) -> (l k) p", p=P)).then_inc(gains_loaded, 16)
            for v, w in ((V_QN, q_norm), (V_KN, k_norm)):
                act.dma_start(gain_rows[v[0]:v[0] + DEPTH, 0:QK_NOPE], w[:, 0:QK_NOPE]).then_inc(gains_loaded, 16)
            for j in range(P // QK_ROPE):
                act.dma_start(gain_rows[V_QPE[0]:V_QPE[0] + DEPTH, j * QK_ROPE:(j + 1) * QK_ROPE],
                              q_norm[:, QK_NOPE:QK]).then_inc(gains_loaded, 16)
            act.dma_start(gain_rows[V_KPE[0]:V_KPE[0] + DEPTH, QK_NOPE:QK], k_norm[:, QK_NOPE:QK]).then_inc(gains_loaded, 16)

            def split_hi(l, b, loaded, used, p=0):
                act.wait_ge(raw_loaded[b], l * (16 * PAIRS) + loaded)
                if used is not None:
                    act.wait_ge(acc_done, l * GROUPS + used)
                for src, dst in split_parts(p, w_raw[b], w_hi[b]):
                    last = nc.scalar.activation(dst, src, ACT.Copy)
                last.then_inc(hi_split, 1)

            def split_hi_at(l, p):
                split_hi(l, p % RING, 32 * (p // RING + 1), used_at(p - RING) if p >= RING else None, p)

            def rms(l, n, dst, width):
                act.wait_ge(sums_done, l * NORMS + n + 1)
                nc.scalar.activation(dst[:, :], bank[SUMS][:, :], ACT.Sqrt, bias=eps_t[:, 0:1],
                                     scale=1.0 / width).then_inc(rms_done, 1)

            def gain_x(l, n, v, d):
                wait_x(act, l, n, d)
                nc.scalar.activation(xg_hi[:, d, :], x[:, d, :], ACT.Copy, scale=gain(l, v, d)).then_inc(xg_hi_done, 1)

            def ffn(l, which, p0, g0, norm, next_norm, next_v):
                for c, n in enumerate(CHUNKS):
                    pc = p0 + chunk_start(c)
                    gc = g0 + 2 * (pc - p0)
                    f0 = which * FT + sum(CHUNKS[:c])

                    def gate_up(i, first=False):
                        g = gc + 4 * i
                        split_hi(l, 0, 16 * (pc + 2 * i + 2) + 32, g + 2)
                        if first:
                            rms(l, norm, rstd_x, D)
                        for j in range(2):
                            wait_evac(act, l, (gc + j, 4 * i))
                            nc.scalar.activation(silu[j][:, :], gate[j][:, :], ACT.Silu).then_inc(silu_done, 1)
                        for j in range(2):
                            act.wait_ge(hid_done, l * 2 * FT + f0 + 2 * i + j + 1)
                            nc.scalar.activation(h_hi[:, bass.ds(2 * i + j, 1), :], hid[j][:, :].rearrange("p (o s) -> p o s", o=1),
                                                 ACT.Copy).then_inc(h_hi_done, 1)
                        split_hi(l, 1, 16 * (pc + 2 * i + 2) + 32, g + 4)

                    if c == 0:
                        gate_up(0, True)
                    with act.Fori(1 if c == 0 else 0, n // 2) as i:
                        gate_up(i)
                    pd = pc + n
                    if c < len(CHUNKS) - 1:
                        with act.Fori(0, DT // 4) as i:
                            for b in range(2):
                                split_hi(l, b, 16 * (pd + 2 * i + 2) + 32, g0 + 2 * (pd - p0) + 4 * i + 2 * b + 2)
                    else:
                        finish_x(l, pd, next_norm, next_v)

            def finish_x(l, pd, next_norm, next_v):
                for i in range(DT // 2):
                    for d in (2 * i, 2 * i + 1):
                        gain_x(l, next_norm, next_v, d)
                    split_hi_at(l, pd + i + 2)

            for d in range(DVE_TILES, DT):
                act.wait_ge(x_turned, d + 1)
                nc.scalar.activation(x[:, d, :], bank[d][:, :], ACT.Copy).then_inc(x_done[1], 1)
            split_hi_at(0, 0)
            act.wait_ge(gains_done, 1)
            act.wait_ge(memset_done, 2)
            for d in range(DT):
                gain_x(0, 0, V_FFN1, d)
            split_hi_at(0, 1)
            act.dma_start(cos_t[:, :], rope_cos).then_inc(const_loaded, 16)
            act.dma_start(sin_t[:, :], rope_sin).then_inc(const_loaded, 16)
            act.dma_start(edge[:, :, :].rearrange("p g n -> p (g n)"), pool_edge).then_inc(const_loaded, 16)
            with act.Fori(0, DEPTH) as l:
                ffn(l, 0, 0, 0, N_FFN1, 1, V_MIX)

                rms(l, N_MIX, rstd_x, D)
                split_hi_at(l, PAIR_MIX + 2)

                def latent_hi(before, tiles):
                    for i, t in enumerate(tiles):
                        act.wait_ge(lat_scaled, l * (QT + KT) + before + i + 1)
                        nc.scalar.activation(h_hi[:, t, :], z[:, t, :], ACT.Copy, scale=latent_gain(l, t)).then_inc(lat_hi, 1)

                rms(l, N_KVL, rstd_l, KVL)
                latent_hi(0, range(KT))
                split_hi_at(l, PAIR_MIX + 3)

                def mixed(g):
                    act.wait_ge(mixed_done, l * PG + g + 1)
                    nc.scalar.activation(mix_hi[g], zp[:, g, PAD:PAD + S], ACT.Copy).then_inc(mixed_hi, 1)

                mixed(0)
                split_hi_at(l, PAIR_MIX + 4)
                mixed(1)
                mixed(2)
                act.wait_ge(k_rope_done, l + 1)
                nc.scalar.activation(k_all[QK_NOPE:QK, :, :],
                                     k_rot[QK_NOPE:QK, :].rearrange("p (o s) -> p o s", o=1).to_broadcast([QK_ROPE, HEADS, S]),
                                     ACT.Copy).then_inc(k_filled, 1)
                mixed(3)
                for p in (PAIR_MIX + 5, PAIR_MIX + 6):
                    split_hi_at(l, p)

                def take_group(g, *parts):
                    act.wait_ge(acc_done, l * GROUPS + g + 1)
                    for dst, rows_ in parts:
                        last = nc.scalar.activation(dst, bank[g % BANKS][rows_, :], ACT.Copy)
                    last.then_inc(evac_act, 1)

                LOW, HIGH, ALL = slice(0, 64), slice(64, P), slice(0, P)

                def take_keys(r):
                    take_group(GROUP_UK + r, (k_all[0:64, 2 * r, :], LOW), (k_all[0:64, 2 * r + 1, :], HIGH))

                def take_values(t):
                    take_group(GROUP_UV + t, (v_all[:, t, :], ALL))

                act.wait_ge(acc_done, l * GROUPS + GROUP_UK)
                for i in range(4):
                    nc.scalar.activation(sq_k[i][QK_NOPE:QK, :], k_pe[QK_NOPE:QK, :], ACT.Square).then_inc(k_sq_rope, 1)
                    if i % 2:
                        take_keys(i // 2)
                rms(l, N_QL, rstd_l, QL)
                take_keys(2)
                take_keys(3)
                take_values(0)
                latent_hi(KT, [KT + t for t in Q_ORDER])
                for t in range(1, TT):
                    take_values(t)
                split_hi_at(l, PAIR_MIX + 7)
                act.wait_ge(mixed_lo, l * PG + PG)
                for r in range(2):
                    take_group(GROUP_UQ + r, (q_pe[:, r, :], ALL))
                for r in range(4):
                    take_group(GROUP_UQ + 2 + r, (q_all[0:64, 2 * r, :], LOW), (q_all[0:64, 2 * r + 1, :], HIGH))
                split_hi_at(l, PAIR_MIX + 8)

                def head_root(n, dst, eps, scale):
                    act.wait_ge(head_sums, l * 2 * HEADS + (n + 1) * HEADS)
                    nc.scalar.activation(dst[:, :], bank[SUMS][:, n * 32:n * 32 + 32], ACT.Sqrt,
                                         bias=eps_t[:, eps:eps + 1], scale=scale).then_inc(root_done, 1)

                for g in range(PG):
                    act.wait_ge(acc_done, l * GROUPS + GROUP_POOL + g + 1)
                    nc.scalar.activation(xg_hi[:, CAT + g, :], bank[(GROUP_POOL + g) % BANKS][:, :], ACT.Copy,
                                         scale=gain(l, V_PS, g)).then_inc(pooled_hi, 1)
                split_hi_at(l, PAIR_MIX + 9)
                head_root(0, k_rstd, 0, 1.0 / QK)
                act.wait_ge(evac_act, l * ACT_GROUPS + ACT_GROUPS)
                for h in range(HEADS):
                    j = h % 4
                    nc.scalar.activation(sq_q[h][QK_NOPE:QK, :], q_pe[32 * j:32 * j + 32, h // 4, :],
                                         ACT.Square).then_inc(q_sq_rope, 1)
                act.wait_ge(q_rope_done, 2 * l + 2)
                for j in range(4):
                    for h in (j, j + 4):
                        nc.scalar.activation(q_all[QK_NOPE:QK, h, :], q_rope[32 * j:32 * j + 32, h // 4, :],
                                             ACT.Copy).then_inc(q_filled, 1)

                def split_qk(h, s):
                    ix = slice(h, h + 1) if isinstance(h, int) else bass.ds(h, 1)
                    for src, o in ((q_all, 0), (k_all, 2)):
                        last = nc.scalar.activation(h_hi[0:QK, o + s:o + s + 1, :], src[0:QK, ix, :], ACT.Copy)
                    last.then_inc(qk_hi, 1)

                def exponent(h, s, t):
                    act.wait_ge(trans_done, l * 32 + 4 * h + 4)
                    act.wait_ge(neg_done, l * 16 + 2 * h + t // 2 + 1)
                    col = bass.ds(4 * h + t, 1)
                    nc.scalar.activation(prob[:, s, t, :], bank[t][:, :], ACT.Exp, bias=neg_max[:, s, t:t + 1],
                                         scale=q_rstd[:, col], accum_out=row_sum[:, s, t:t + 1]).then_inc(exp_done, 1)

                def prob_t_hi(h, t):
                    act.wait_ge(pt_used, l * 32 + 4 * h + t + 1)
                    act.wait_ge(trans_done, l * 32 + 4 * h + t + 1 + C_TRANS)
                    nc.scalar.activation(h_hi[:, 4 + t, :], bank[TRANS + t % 3][:, :], ACT.Copy).then_inc(pt_hi_done, 1)

                def split_v(hp):
                    act.wait_ge(pt_used, l * 32 + 8 * hp + C_PTUSED)
                    nc.scalar.activation(v_hi[:, :, :], v_all[:, :, bass.ds(P * hp, P)], ACT.Copy).then_inc(v_hi_done, 1)

                def head_pair(hp, last):
                    for s in range(2):
                        h = 2 * hp + s
                        if s == 0:
                            split_v(hp)
                        if not last:
                            act.wait_ge(scores_done, l * 32 + 4 * h + 4)
                            split_qk(h + 2, s)
                        more = not (last and s == 1)
                        for t in range(3):
                            prob_t_hi(h, t)
                        if more:
                            exponent(h + 1, 1 - s, 0)
                            exponent(h + 1, 1 - s, 1)
                        prob_t_hi(h, 3)
                        if more:
                            exponent(h + 1, 1 - s, 2)
                            exponent(h + 1, 1 - s, 3)
                        act.wait_ge(pt_used, l * 32 + 4 * h + 4 + C_PTUSED)
                        nc.scalar.activation(xg_hi[64 * s:64 * s + 64, bass.ds(CAT + hp, 1), :],
                                             bank[OUT][64 * s:64 * s + 64, :].rearrange("p (o s) -> p o s", o=1),
                                             ACT.Copy).then_inc(o_hi_done, 1)

                act.wait_ge(q_filled, l * HEADS + HEADS)
                for h in range(2):
                    act.wait_ge(k_normed, l * HEADS + h + 1)
                    split_qk(h, h)
                split_hi_at(l, PAIR_MIX + 10)
                head_root(1, q_rstd, 1, 1.0)
                act.wait_ge(k_normed, l * HEADS + HEADS)
                act.wait_ge(factor_done, 2 * l + 2)
                for t in range(TT):
                    exponent(0, 0, t)
                with act.Fori(0, HEADS // 2 - 1) as hp:
                    head_pair(hp, False)
                head_pair(HEADS // 2 - 1, True)
                split_hi_at(l, PAIR_MIX + 11)

                for d in range(4):
                    gain_x(l, 2, V_FFN2, d)
                split_hi_at(l, PAIR_FFN2)
                act.wait_ge(acc_done, l * GROUPS + GROUP_FFN2)
                for d in range(4, DT):
                    gain_x(l, 2, V_FFN2, d)
                split_hi_at(l, PAIR_FFN2 + 1)
                ffn(l, 1, PAIR_FFN2, GROUP_FFN2, N_FFN2, 3, V_NEXT)

            for t in range(TT):
                act.wait_ge(y_turned, t + 1)
                nc.scalar.activation(y_tok[:, t, 0:512], bank[4 + t][:, :], ACT.Copy).then_inc(y_copied[0], 1)

        @block.tensor
        def _(pe):
            pe.sem_inc(trans_done, C_TRANS)
            pe.sem_inc(pt_used, C_PTUSED)
            pe.wait_ge(memset_done, 2)
            pe.wait_ge(ident_done, 1)
            for t in range(TT):
                pe.wait_ge(x_loaded[t], 16)
                for d in range(DT):
                    last = nc.tensor.transpose(bank[d][:, t * P:(t + 1) * P], x_tok[:, t, d * P:(d + 1) * P], ident[:, :])
                    if t == TT - 1:
                        last.then_inc(x_turned, 1)
            pe.wait_ge(gains_loaded, 16 * 13)
            pe.wait_ge(x_done[0], DVE_TILES)
            nc.tensor.transpose(bank[SUMS][:, 0:P], gain_rows[:, :], ident[:, :]).then_inc(gains_turned, 1)

            def mm3(out, whi, wlo, xhi, xlo, first, last):
                nc.tensor.matmul(out, whi, xhi, start=first, stop=False)
                nc.tensor.matmul(out, whi, xlo, start=False, stop=False)
                return nc.tensor.matmul(out, wlo, xhi, start=False, stop=last)

            def wait_pair(l, p):
                pe.wait_ge(lo_split, l * PAIRS + p + 1 + RING)

            def wait_bank(l, g):
                wait_evac(pe, l, g, BANKS)

            def sums(l, n, src):
                pe.wait_ge(sumsq_done, l * NORMS + n + 1)
                if n == N_QL:
                    pe.wait_ge(rms_done, l * NORMS + n)
                nc.tensor.matmul(bank[SUMS][:, :], ones[:, :], src[:, :], start=True, stop=True).then_inc(sums_done, 1)

            def column_tile(l, g, bk, b, c0, width, hi, lo, order, ready, blocks=DT, cols=P, at=0):
                wait_bank(l, g)
                whi, wlo = pairs_of(w_hi[b], width, blocks, at), pairs_of(w_lo[b], width, blocks, at)
                for n, k in enumerate(order):
                    ready(k)
                    last = mm3(bank[bk][0:cols, :], whi[:, n, c0:c0 + cols], wlo[:, n, c0:c0 + cols],
                               hi[:, k, :], lo[:, k, :], n == 0, n == blocks - 1)
                return last.then_inc(acc_done, 1)

            def wait_xg(l, n):
                def ready(k):
                    pe.wait_ge(xg_lo_done, (3 * l + n) * DT + k + 1)
                return ready

            def nothing(k):
                pass

            def ffn(l, which, p0, g0, norm, x_norm):
                for c, n in enumerate(CHUNKS):
                    pc, gc = p0 + chunk_start(c), g0 + 2 * chunk_start(c)
                    f0 = which * FT + sum(CHUNKS[:c])

                    def gate_up(i, first):
                        for b in range(2):
                            wait_pair(l, pc + 2 * i + b)
                            for j in range(2):
                                column_tile(l, (gc + 2 * b + j, 4 * i), 2 * b + j, b, P * j, 256, xg_hi, xg_lo,
                                                   range(DT), wait_xg(l, x_norm) if first and b + j == 0 else nothing)
                                if first and b == 0 and j == 1:
                                    sums(l, norm, sumsq_x)

                    if c == 0:
                        gate_up(0, True)
                    with pe.Fori(1 if c == 0 else 0, n // 2) as i:
                        gate_up(i, False)

                    def wait_h(k):
                        pe.wait_ge(h_lo_done, l * 2 * FT + f0 + k + 1)

                    with pe.Fori(0, DT // 4) as i:
                        for b in range(2):
                            wait_pair(l, pc + n + 2 * i + b)
                            for j in range(2):
                                column_tile(l, (gc + 2 * n + 2 * b + j, 4 * i), 2 * b + j, b, P * j, 256, h_hi, h_lo,
                                            range(n), wait_h if b + j == 0 else nothing, blocks=n)

            with pe.Fori(0, DEPTH) as l:
                ffn(l, 0, 0, 0, N_FFN1, 0)

                g = GROUP_MIX
                for p in range(5):
                    wait_pair(l, PAIR_MIX + p)
                    for j in range(2):
                        c0, width, at, cols = (P * j, 256, 0, P) if p != 3 else (0, (QK, P)[j], 1024 * j, (QK, P)[j])
                        column_tile(l, g, g % BANKS, (PAIR_MIX + p) % RING, c0, width, xg_hi, xg_lo, range(DT),
                                    wait_xg(l, 1) if g == GROUP_MIX else nothing, cols=cols, at=at)
                        if g == GROUP_MIX:
                            sums(l, N_MIX, sumsq_x)
                        if g == GROUP_MIX + 3:
                            sums(l, N_KVL, sumsq_l[0])
                        g += 1

                b = (PAIR_MIX + 5) % RING
                wait_pair(l, PAIR_MIX + 5)
                pe.wait_ge(lat_lo, l * (QT + KT) + KT)
                for r in range(4):
                    wait_bank(l, GROUP_UK + r)
                    for k in range(KT):
                        c0 = 512 * k + P * r
                        last = mm3(bank[(GROUP_UK + r) % BANKS][:, :], w_hi[b][:, c0:c0 + P], w_lo[b][:, c0:c0 + P],
                                   h_hi[:, k, :], h_lo[:, k, :], k == 0, k == KT - 1)
                    last.then_inc(acc_done, 1)
                    if r == 2:
                        sums(l, N_QL, sumsq_l[1])
                def head_sum(n, h):
                    for squares in ((k_sq, k_sq_rope), (q_sq, q_sq_rope))[n]:
                        pe.wait_ge(squares, l * HEADS + h + 1 if squares is not k_sq_rope else 4 * l + 4)
                    sq = sq_q[h] if n else sq_k[h % 4]
                    for t in range(TT):
                        col = n * 32 + h * TT + t
                        last = nc.tensor.matmul(bank[SUMS][:, col:col + 1], sq[0:QK, t * P:(t + 1) * P],
                                                ones[0:QK, 0:1], start=True, stop=True)
                    last.then_inc(head_sums, 1)

                for t in range(TT):
                    wait_bank(l, GROUP_UV + t)
                    for k in range(KT):
                        c_hi, c_lo = (h[:, k, t * P:(t + 1) * P] for h in (h_hi, h_lo))
                        wv_hi, wv_lo = (w[b][:, 1024 + 512 * k:1536 + 512 * k] for w in (w_hi, w_lo))
                        last = mm3(bank[(GROUP_UV + t) % BANKS][:, :], c_hi, c_lo, wv_hi, wv_lo, k == 0, k == KT - 1)
                    last.then_inc(acc_done, 1)
                    if t >= 2:
                        if t == 2:
                            pe.wait_ge(rms_done, l * NORMS + N_QL + 1)
                        head_sum(0, t - 2)

                b0, b1 = (PAIR_MIX + 6) % RING, (PAIR_MIX + 7) % RING

                def uq(k, r):
                    b, c0 = (b0, 1024 * k) if k < 2 else (b1, 0)
                    c0 += (4, 5, 0, 1, 2, 3)[r] * P
                    if k == 0:
                        wait_bank(l, GROUP_UQ + r)
                    last = mm3(bank[(GROUP_UQ + r) % BANKS][:, :], w_hi[b][:, c0:c0 + P], w_lo[b][:, c0:c0 + P],
                               h_hi[:, KT + k, :], h_lo[:, KT + k, :], k == 0, k == QT - 1)
                    if k == QT - 1:
                        last.then_inc(acc_done, 1)

                wait_pair(l, PAIR_MIX + 6)
                pe.wait_ge(lat_lo, l * (QT + KT) + QT + KT)
                for k in range(QT):
                    if k == 2:
                        wait_pair(l, PAIR_MIX + 7)
                    for r in range(4):
                        uq(k, r)
                    head_sum(0, 2 + k)
                for r in (4, 5):
                    for k in range(QT):
                        uq(k, r)
                head_sum(0, 5)

                for g in range(PG):
                    wait_bank(l, GROUP_POOL + g)
                    pe.wait_ge(mixed_lo, l * PG + g + 1)
                    c0 = 1024 + P * g
                    mm3(bank[(GROUP_POOL + g) % BANKS][:, :], w_hi[b1][:, c0:c0 + P], w_lo[b1][:, c0:c0 + P],
                        mix_hi[g], mix_lo[g], True, True).then_inc(acc_done, 1)
                for h in (6, 7):
                    head_sum(0, h)

                def wait_pooled(k):
                    wait_evac(pe, l, GROUP_POOL + k - CAT)

                def wait_attended(k):
                    pe.wait_ge(o_lo_done, l * HEADS + 2 * (k - CAT) + 2 + C_OLO)

                def project(half, d, ready):
                    p = PAIR_OUT + 2 * half + d // 4
                    if d % 4 == 0:
                        wait_pair(l, p)
                    column_tile(l, GROUP_OUT + DT * half + d, out_bank(half, d), p % RING, P * (d % 4), 512, xg_hi, xg_lo,
                                range(CAT, DT), ready if d == 0 else nothing, blocks=4)

                def spread(h):
                    pe.wait_ge(factor_done, 2 * l + 1)
                    if h >= 2:
                        pe.wait_ge(k_normed, l * HEADS + h - 1)
                    for t in range(TT):
                        col = h * TT + t
                        last = nc.tensor.matmul(bank[SPREAD + h % 2][0:QK, t * P:(t + 1) * P],
                                                k_rstd[:, col:col + 1].to_broadcast([P, QK]), ident[:, :],
                                                start=True, stop=True)
                    last.then_inc(k_spread, 1)

                Q_SUMS = [], [0], [1], [2, 3], [4, 5], [6, 7]
                for d in range(DT - 2):
                    project(0, d, wait_pooled)
                    if d < 4:
                        spread(2 * d)
                        spread(2 * d + 1)
                    for h in Q_SUMS[d]:
                        head_sum(1, h)

                def scores(h, s, t, first=False):
                    if t == 0:
                        pe.wait_ge(qk_lo, l * 8 + h + 1)
                    if first:
                        wait_evac(pe, l, GROUP_OUT + (4 + t if t < 2 else t))
                    else:
                        pe.wait_ge(exp_done, l * 32 + 4 * h - 4 + t + 1)
                    mm3(bank[t][:, :], h_hi[0:QK, s, t * P:(t + 1) * P], h_lo[0:QK, s, t * P:(t + 1) * P],
                        h_hi[0:QK, 2 + s, :], h_lo[0:QK, 2 + s, :], True, True).then_inc(scores_done, 1)

                def turn(h, s, t):
                    pe.wait_ge(pt_lo_done, l * 32 + 4 * h + t + 1)
                    if t == 2:
                        wait_evac(pe, l, GROUP_OUT + DT - 1)
                    for q in range(TT):
                        if t == 0:
                            pe.wait_ge((prob_done, prob_dve)[q % 2], l * 16 + 2 * h + q // 2 + 1)
                        last = nc.tensor.transpose(bank[TRANS + t % 3][:, q * P:(q + 1) * P],
                                                   prob[:, s, q, t * P:(t + 1) * P], ident[:, :])
                    last.then_inc(trans_done, 1)

                def values(h, s, hp, t):
                    pe.wait_ge(pt_lo_done, l * 32 + 4 * h + t + 1 + C_PTLO)
                    if t == 0:
                        pe.wait_ge(o_lo_done, l * 8 + h + 1)
                        if s == 0:
                            pe.wait_ge(v_lo_done, l * 4 + hp + 1)
                    nc.tensor.matmul(bank[OUT][:, :], v_hi[:, t, :], h_hi[:, 4 + t, :], start=t == 0, stop=False)
                    nc.tensor.matmul(bank[OUT][:, :], v_lo[:, t, :], h_hi[:, 4 + t, :], start=False, stop=False)
                    nc.tensor.matmul(bank[OUT][:, :], v_hi[:, t, :], h_lo[:, 4 + t, :], start=False,
                                     stop=t == TT - 1).then_inc(pt_used, 1)

                def step_head(hp, s, more):
                    h = 2 * hp + s
                    if more:
                        scores(h + 1, 1 - s, 0)
                        scores(h + 1, 1 - s, 1)
                    for t in range(3):
                        turn(h, s, t)
                    if more:
                        scores(h + 1, 1 - s, 2)
                        scores(h + 1, 1 - s, 3)
                    turn(h, s, 3)
                    for t in range(TT):
                        values(h, s, hp, t)

                for t in range(TT):
                    scores(0, 0, t, True)
                for d in (DT - 2, DT - 1):
                    pe.wait_ge(k_normed, l * HEADS + HEADS)
                    project(0, d, nothing)

                def head_pair(hp, last):
                    step_head(hp, 0, True)
                    step_head(hp, 1, not last)

                with pe.Fori(0, HEADS // 2 - 1) as hp:
                    head_pair(hp, False)
                head_pair(HEADS // 2 - 1, True)

                for d in range(DT):
                    project(1, d, wait_attended)
                ffn(l, 1, PAIR_FFN2, GROUP_FFN2, N_FFN2, 2)

            for half in range(2):
                pe.wait_ge(evac_done, DEPTH * DVE_GROUPS + BANKS - 4 * (1 - half))
                for t in range(TT):
                    for d in range(4):
                        last = nc.tensor.transpose(bank[4 * (1 - half) + t][:, d * P:(d + 1) * P],
                                                   x[:, 4 * half + d, t * P:(t + 1) * P], ident[:, :])
                    last.then_inc(y_turned, 1)

        @block.vector
        def _(dve):
            V = nc.vector
            dve.sem_inc(evac_done, BANKS)
            dve.sem_inc(lo_split, RING)
            dve.sem_inc(pt_lo_done, C_PTLO)
            dve.sem_inc(o_lo_done, C_OLO)
            V.memset(gain_rows[:, :], 1.0).then_inc(memset_done, 1)
            V.memset(ones[:, :], 1.0)
            V.memset(eps_t[:, 0:1], EPS)
            V.memset(eps_t[:, 1:2], EPS * QK).then_inc(memset_done, 1)
            for d in range(DVE_TILES):
                dve.wait_ge(x_turned, d + 1)
                V.tensor_copy(x[:, d, :], bank[d][:, :]).then_inc(x_done[0], 1)
            dve.wait_ge(gains_turned, 1)
            V.tensor_copy(gains[:, :], bank[SUMS][:, 0:P]).then_inc(gains_done, 1)
            dve.wait_ge(gains_done, 1)
            for l in range(DEPTH):
                k_col, q_col = V_KN[0] + l, V_QN[0] + l
                V.tensor_tensor(gains_qk[:, l:l + 1], gains[:, k_col:k_col + 1], gains[:, q_col:q_col + 1],
                                ALU.mult).then_inc(gains_done, 1)
            dve.wait_ge(gains_done, 1 + DEPTH)

            def gain_x(l, n, v, d):
                dve.wait_ge(xg_hi_done, (3 * l + n) * DT + d + 1)
                wait_x(dve, l, n, d)
                V.scalar_tensor_tensor(out=xg_lo[:, d, :], in0=x[:, d, :], scalar=gain(l, v, d),
                                       in1=xg_hi[:, d, :].bitcast(F32), op0=ALU.mult, op1=ALU.subtract).then_inc(xg_lo_done, 1)

            def split_lo(l, p, b):
                dve.wait_ge(hi_split, l * PAIRS + p + 1 + RING)
                for (src, dst), (_, hi) in zip(split_parts(p, w_raw[b], w_lo[b]), split_parts(p, w_raw[b], w_hi[b])):
                    last = V.tensor_tensor(dst, src, hi.bitcast(F32), ALU.subtract)
                last.then_inc(lo_split, 1)

            def split_lo_at(l, p):
                split_lo(l, p, p % RING)

            def wait_group(l, g):
                start, add = (g, 0) if isinstance(g, int) else g
                dve.wait_ge(acc_done, l * GROUPS + start + 1 + add)
                skipped = ACT_GROUPS if start >= GROUP_POOL else 0
                dve.wait_ge(evac_done, l * DVE_GROUPS + (start - skipped + BANKS) + add)

            def rstd(l, n, dst):
                dve.wait_ge(rms_done, l * NORMS + n + 1)
                V.reciprocal(dst[:, :], dst[:, :]).then_inc(rstd_done, 1)

            def wait_rstd(l, n):
                dve.wait_ge(rstd_done, l * NORMS + n + 1)

            def add_to_x(l, g, bk, d, factor):
                wait_group(l, g)
                xd = x[:, d, :] if isinstance(d, int) else x[:, bass.ds(d, 1), :]
                ps = bank[bk][:, :] if isinstance(d, int) else bank[bk][:, :].rearrange("p (o s) -> p o s", o=1)
                V.scalar_tensor_tensor(out=xd, in0=ps, scalar=factor, in1=xd, op0=ALU.mult, op1=ALU.add).then_inc(evac_done, 1)

            def finish_x(l, pd, gd, factor, next_norm, next_v):
                for i in range(DT // 2):
                    for d in (2 * i, 2 * i + 1):
                        add_to_x(l, gd + d, d % BANKS, d, factor)
                        gain_x(l, next_norm, next_v, d)
                    split_lo_at(l, pd + i + 2)

            def ffn(l, which, p0, g0, norm, next_norm, next_v):
                for c, n in enumerate(CHUNKS):
                    pc, gc = p0 + chunk_start(c), g0 + 2 * chunk_start(c)
                    f0 = which * FT + sum(CHUNKS[:c])
                    def gate_up(i, first=False):
                        split_lo(l, pc + 2 * i + 2, 0)
                        if first:
                            rstd(l, norm, rstd_x)
                        wait_rstd(l, norm)
                        for j in range(2):
                            wait_group(l, (gc + j, 4 * i))
                            V.tensor_tensor(gate[j][:, :], bank[j][:, :], rstd_x[:, :], ALU.mult).then_inc(evac_done, 1)
                        for j in range(2):
                            f = l * 2 * FT + f0 + 2 * i + j
                            wait_group(l, (gc + 2 + j, 4 * i))
                            V.tensor_tensor(up[j][:, :], bank[2 + j][:, :], rstd_x[:, :], ALU.mult).then_inc(evac_done, 1)
                            wait_evac(dve, l, (gc + 2 + j, 4 * i))
                            dve.wait_ge(silu_done, f + 1)
                            V.tensor_tensor(hid[j][:, :], silu[j][:, :], up[j][:, :], ALU.mult).then_inc(hid_done, 1)
                            dve.wait_ge(h_hi_done, f + 1)
                            dve.wait_ge(hid_done, f + 1)
                            o1 = "p (o s) -> p o s"
                            V.tensor_tensor(h_lo[:, bass.ds(2 * i + j, 1), :], hid[j][:, :].rearrange(o1, o=1),
                                            h_hi[:, bass.ds(2 * i + j, 1), :].bitcast(F32), ALU.subtract).then_inc(h_lo_done, 1)
                        split_lo(l, pc + 2 * i + 3, 1)

                    if c == 0:
                        gate_up(0, True)
                    with dve.Fori(1 if c == 0 else 0, n // 2) as i:
                        gate_up(i)
                    pd, gd = pc + n, gc + 2 * n
                    if c < len(CHUNKS) - 1:
                        with dve.Fori(0, DT // 4) as i:
                            for b in range(2):
                                for j in range(2):
                                    add_to_x(l, (gd + 2 * b + j, 4 * i), 2 * b + j, 4 * i + 2 * b + j, 0.5)
                                split_lo(l, pd + 2 * i + b + 2, b)
                    else:
                        finish_x(l, pd, gd, 0.5, next_norm, next_v)

            split_lo_at(0, 0)
            for d in range(DT):
                gain_x(0, 0, V_FFN1, d)
            split_lo_at(0, 1)
            dve.wait_ge(const_loaded, 48)
            swap = [(i + 16) % 32 for i in range(32)]
            with dve.Fori(0, DEPTH) as l:
                step = [0]

                def link(ins):
                    step[0] += 1
                    ins.then_inc(dve_step, 1)
                    dve.wait_ge(dve_step, l * DVE_STEPS + step[0])

                ffn(l, 0, 0, 0, N_FFN1, 1, V_MIX)

                rstd(l, N_MIX, rstd_x)
                wait_rstd(l, N_MIX)
                M = GROUP_MIX
                ALL = slice(0, P)

                def scale_group(m, dst, rows_=ALL):
                    wait_group(l, M + m)
                    V.tensor_tensor(dst, bank[(M + m) % BANKS][rows_, :], rstd_x[rows_, :], ALU.mult).then_inc(evac_done, 1)

                def scale_latents(tiles):
                    for t in tiles:
                        V.tensor_tensor(z[:, t, :], z[:, t, :], rstd_l[:, :], ALU.mult).then_inc(lat_scaled, 1)

                def latents_lo(before, tiles):
                    for i, t in enumerate(tiles):
                        dve.wait_ge(lat_scaled, l * (QT + KT) + before + i + 1)
                        dve.wait_ge(lat_hi, l * (QT + KT) + before + i + 1)
                        V.scalar_tensor_tensor(out=h_lo[:, t, :], in0=z[:, t, :], scalar=latent_gain(l, t),
                                               in1=h_hi[:, t, :].bitcast(F32), op0=ALU.mult, op1=ALU.subtract).then_inc(lat_lo, 1)

                def scale_pool(g):
                    scale_group(M_POOL + g, zp[:, g, PAD:PAD + S])

                def mix(g):
                    dve.wait_ge(windowed, l * PG + g + 1)
                    V.scalar_tensor_tensor(out=zp[:, g, PAD:PAD + S], in0=win_s[:, PAD:PAD + S], scalar=0.5 ** (g + 1),
                                           in1=zp[:, g, PAD:PAD + S], op0=ALU.mult, op1=ALU.subtract).then_inc(mixed_done, 1)

                def mix_split(g):
                    dve.wait_ge(mixed_done, l * PG + g + 1)
                    dve.wait_ge(mixed_hi, l * PG + g + 1)
                    V.tensor_tensor(mix_lo[g], zp[:, g, PAD:PAD + S], mix_hi[g].bitcast(F32), ALU.subtract).then_inc(mixed_lo, 1)

                def rope(dst, src, g, scaled, tmp, rows_):
                    link(V.tensor_scalar(scaled, src, g, None, ALU.mult))
                    V.tensor_tensor(dst, scaled, cos_t[rows_, :], ALU.mult)
                    link(V.stream_shuffle(tmp, scaled, swap))
                    link(V.tensor_tensor(tmp, tmp, sin_t[rows_, :], ALU.mult))
                    return V.tensor_tensor(dst, dst, tmp, ALU.add)

                R = slice(QK_NOPE, QK)
                for t in range(KT):
                    scale_group(t, z[:, t, :])
                split_lo_at(l, PAIR_MIX + 2)
                for side in (slice(0, PAD), slice(PAD + S, PW)):
                    V.memset(zp[:, :, side], 0.0)
                scale_pool(0)
                scale_pool(1)
                rstd(l, N_KVL, rstd_l)
                wait_rstd(l, N_KVL)
                scale_latents(range(KT))
                latents_lo(0, range(KT))
                split_lo_at(l, PAIR_MIX + 3)
                scale_pool(2)
                mix(0)
                scale_pool(3)
                mix_split(0)
                split_lo_at(l, PAIR_MIX + 4)
                mix(1)
                scale_group(M_PE, k_pe[R, :], R)
                dve.wait_ge(evac_done, l * DVE_GROUPS + GROUP_MIX + M_PE + 1 + BANKS)
                rope(k_rot[R, :], k_pe[R, :], gains[R, bass.ds(l + V_KPE[0], 1)], k_all[R, 0, :], k_all[R, 1, :], R).then_inc(k_rope_done, 1)
                mix_split(1)
                mix(2)
                scale_group(M_Q, z[:, KT + Q_ORDER[0], :])
                mix_split(2)
                mix(3)
                scale_group(M_Q + 1, z[:, KT + Q_ORDER[1], :])
                mix_split(3)
                split_lo_at(l, PAIR_MIX + 5)
                scale_group(M_Q + 2, z[:, KT + Q_ORDER[2], :])
                split_lo_at(l, PAIR_MIX + 6)
                rstd(l, N_QL, rstd_l)
                wait_rstd(l, N_QL)
                scale_latents([KT + t for t in Q_ORDER])
                latents_lo(KT, [KT + t for t in Q_ORDER])
                split_lo_at(l, PAIR_MIX + 7)
                dve.wait_ge(lat_lo, l * (QT + KT) + QT + KT)
                for r in range(2):
                    wait_evac(dve, l, GROUP_UQ + r)
                    rope(q_rope[:, r, :], q_pe[:, r, :], gain(l, V_QPE), rot_a[:, :], rot_b[:, :], ALL).then_inc(q_rope_done, 1)
                    dve.wait_ge(q_rope_done, 2 * l + r + 1)
                split_lo_at(l, PAIR_MIX + 8)

                def head_factor(n, dst):
                    dve.wait_ge(root_done, 2 * l + n + 1)
                    V.reciprocal(dst[:, :], dst[:, :]).then_inc(factor_done, 1)

                for g in range(PG):
                    wait_group(l, GROUP_POOL + g)
                    dve.wait_ge(pooled_hi, l * PG + g + 1)
                    V.scalar_tensor_tensor(out=xg_lo[:, CAT + g, :], in0=bank[(GROUP_POOL + g) % BANKS][:, :],
                                           scalar=gain(l, V_PS, g), in1=xg_hi[:, CAT + g, :].bitcast(F32),
                                           op0=ALU.mult, op1=ALU.subtract).then_inc(evac_done, 1)
                head_factor(0, k_rstd)
                dve.wait_ge(k_filled, l + 1)
                for d in range(DT - 2):
                    add_to_x(l, GROUP_OUT + d, out_bank(0, d), d, 1.0)
                    if d < 4:
                        for h in (2 * d, 2 * d + 1):
                            dve.wait_ge(k_spread, l * HEADS + h + 1)
                            V.scalar_tensor_tensor(out=k_all[0:QK, h, :], in0=k_all[0:QK, h, :], scalar=gains_qk[0:QK, bass.ds(l, 1)],
                                                   in1=bank[SPREAD + h % 2][0:QK, :], op0=ALU.mult, op1=ALU.mult).then_inc(k_normed, 1)
                    if d == 0:
                        split_lo_at(l, PAIR_MIX + 9)
                    if d == 4:
                        split_lo_at(l, PAIR_MIX + 10)
                head_factor(1, q_rstd)

                dve.wait_ge(factor_done, 2 * l + 2)

                def maximum(h, s, t, n=1):
                    dve.wait_ge(scores_done, l * 32 + 4 * h + t + n)
                    V.reduce_max(row_max[:, s, t:t + n], psum[:, t:t + n, :], AX_X).then_inc(max_done, 1)

                def negate(h, s, i):
                    dve.wait_ge(max_done, l * 24 + 3 * h + (1, 3)[i])
                    V.scalar_tensor_tensor(out=neg_max[:, s, 2 * i:2 * i + 2], in0=row_max[:, s, 2 * i:2 * i + 2], scalar=-1.0,
                                           in1=q_rstd[:, bass.ds(4 * h + 2 * i, 2)], op0=ALU.mult,
                                           op1=ALU.mult).then_inc(neg_done, 1)

                def inverse(h, s, i):
                    dve.wait_ge(exp_done, l * 32 + 4 * h + 2 * i + 2)
                    V.reciprocal(row_inv[:, s, 2 * i:2 * i + 2], row_sum[:, s, 2 * i:2 * i + 2]).then_inc(inv_done, 1)

                def normalise(h, s, t):
                    dve.wait_ge(inv_done, l * 16 + 2 * h + t // 2 + 1)
                    V.tensor_scalar(prob[:, s, t, :], prob[:, s, t, :], row_inv[:, s, t:t + 1], None,
                                    ALU.mult).then_inc(prob_dve, 1)

                def prob_t_lo(h, t):
                    dve.wait_ge(pt_hi_done, l * 32 + 4 * h + t + 1)
                    V.tensor_tensor(h_lo[:, 4 + t, :], bank[TRANS + t % 3][:, :], h_hi[:, 4 + t, :].bitcast(F32),
                                    ALU.subtract).then_inc(pt_lo_done, 1)

                def head_pair(hp, last):
                    for s in range(2):
                        h, more = 2 * hp + s, not (last and s == 1)
                        if more:
                            maximum(h + 1, 1 - s, 0, 2)
                        prob_t_lo(h, 0)
                        if more:
                            negate(h + 1, 1 - s, 0)
                        prob_t_lo(h, 1)
                        if more:
                            maximum(h + 1, 1 - s, 2)
                            maximum(h + 1, 1 - s, 3)
                        prob_t_lo(h, 2)
                        if more:
                            negate(h + 1, 1 - s, 1)
                            inverse(h + 1, 1 - s, 0)
                        prob_t_lo(h, 3)
                        if more:
                            normalise(h + 1, 1 - s, 1)
                            inverse(h + 1, 1 - s, 1)
                            normalise(h + 1, 1 - s, 3)
                        dve.wait_ge(o_hi_done, l * 8 + h + 1)
                        V.tensor_tensor(xg_lo[64 * s:64 * s + 64, bass.ds(CAT + hp, 1), :],
                                        bank[OUT][64 * s:64 * s + 64, :].rearrange("p (o s) -> p o s", o=1),
                                        xg_hi[64 * s:64 * s + 64, bass.ds(CAT + hp, 1), :].bitcast(F32),
                                        ALU.subtract).then_inc(o_lo_done, 1)

                maximum(0, 0, 0, 2)
                negate(0, 0, 0)
                maximum(0, 0, 2)
                maximum(0, 0, 3)
                negate(0, 0, 1)
                inverse(0, 0, 0)
                normalise(0, 0, 1)
                inverse(0, 0, 1)
                normalise(0, 0, 3)
                for d in (DT - 2, DT - 1):
                    add_to_x(l, GROUP_OUT + d, out_bank(0, d), d, 1.0)
                with dve.Fori(0, HEADS // 2 - 1) as hp:
                    head_pair(hp, False)
                head_pair(HEADS // 2 - 1, True)

                split_lo_at(l, PAIR_MIX + 11)
                for n in range(2):
                    for d in range(4 * n, 4 * n + 4):
                        add_to_x(l, GROUP_OUT + DT + d, d % BANKS, d, 1.0)
                        if n == 0:
                            gain_x(l, 2, V_FFN2, d)
                    if n == 0:
                        split_lo_at(l, PAIR_FFN2)
                for d in range(4, DT):
                    gain_x(l, 2, V_FFN2, d)
                split_lo_at(l, PAIR_FFN2 + 1)
                ffn(l, 1, PAIR_FFN2, GROUP_FFN2, N_FFN2, 3, V_NEXT)
                assert step[0] == DVE_STEPS, step[0]

            for t in range(TT):
                dve.wait_ge(y_turned, TT + t + 1)
                V.tensor_copy(y_tok[:, t, 512:1024], bank[t][:, :]).then_inc(y_copied[1], 1)

        @block.gpsimd
        def _(pool):
            G = nc.gpsimd
            G.memset(ident[:, :], 0.0).then_inc(pool_step, 1)
            pool.wait_ge(pool_step, 1)
            G.affine_select(out=ident[:, :], in_=ident[:, :], compare_op=ALU.not_equal, fill=1.0,
                            base=0, pattern=[[-1, P]], channel_multiplier=1).then_inc(ident_done, 1)
            step = [0]

            def link(l, ins, base):
                step[0] += 1
                ins.then_inc(pool_step, 1)
                pool.wait_ge(pool_step, l * POOL_STEPS + base + step[0])

            def sum_squares(l, tiles, total, wait, base):
                for n, t in enumerate(tiles):
                    wait(n)
                    sq = G.tensor_tensor(total[:, :] if n == 0 else square[:, :], t, t, ALU.mult)
                    if n:
                        link(l, sq, base)
                        last = G.tensor_tensor(total[:, :], total[:, :], square[:, :], ALU.add)
                        if n < len(tiles) - 1:
                            link(l, last, base)
                    else:
                        first = sq
                        link(l, first, base)
                last.then_inc(sumsq_done, 1)

            def x_squares(l, n, base):
                sum_squares(l, [x[:, d, :] for d in range(DT)], sumsq_x,
                            lambda d: wait_x(pool, l, n, d), base)

            x_squares(0, 0, 1)
            B = 1 + step[0]
            assert step[0] == X_LINKS
            step[0] = 0
            with pool.Fori(0, DEPTH) as l:
                x_squares(l, 1, B)
                sum_squares(l, [z[:, t, :] for t in range(KT)], sumsq_l[0],
                            lambda t: wait_evac(pool, l, GROUP_MIX + t), B)
                for g in range(PG):
                    wait_evac(pool, l, GROUP_MIX + M_POOL + g)
                    src, a, b = zp[:, g, :], 0, PW
                    for n in range(g + 1):
                        s0, s1 = (1, 0) if n == 0 else (2 ** (n - 1), 2 ** (n - 1))
                        lo, hi = a + s0, b - s1
                        final = n == g
                        dst = win_s if final else (win_a, win_b)[n % 2]
                        if final and g >= 1:
                            pool.wait_ge(mixed_done, l * PG + g)
                        src0 = src[:, lo - s0:hi - s0]
                        src1 = src[:, lo + s1:hi + s1]
                        link(l, G.tensor_tensor(dst[:, lo:hi], src0, src1, ALU.add), B)
                        src, a, b = dst, lo, hi
                    G.tensor_tensor(win_s[:, PAD:2 * PAD], win_s[:, PAD:2 * PAD], edge[:, g, 0:PAD], ALU.mult)
                    G.tensor_tensor(win_s[:, S:S + PAD], win_s[:, S:S + PAD], edge[:, g, PAD:2 * PAD],
                                    ALU.mult).then_inc(windowed, 1)
                sum_squares(l, [z[:, KT + t, :] for t in Q_ORDER], sumsq_l[1],
                            lambda t: wait_evac(pool, l, GROUP_MIX + M_Q + t), B)
                for h in range(HEADS):
                    if h % 2 == 0:
                        wait_evac(pool, l, GROUP_UK + h // 2)
                    if h >= 4:
                        pool.wait_ge(head_sums, l * 2 * HEADS + h - 3)
                    G.tensor_tensor(sq_k[h % 4][0:QK_NOPE, :], k_all[0:QK_NOPE, h, :], k_all[0:QK_NOPE, h, :],
                                    ALU.mult).then_inc(k_sq, 1)
                pool.wait_ge(acc_done, l * GROUPS + GROUP_OUT)
                for h in range(HEADS):
                    if h % 2 == 0:
                        wait_evac(pool, l, GROUP_UQ + 2 + h // 2)
                    G.tensor_tensor(sq_q[h][0:QK_NOPE, :], q_all[0:QK_NOPE, h, :], q_all[0:QK_NOPE, h, :],
                                    ALU.mult).then_inc(q_sq, 1)

                def split_qk(h, s, dyn):
                    ix = bass.ds(h, 1) if dyn else slice(h, h + 1)
                    pool.wait_ge(qk_hi, l * 8 + h + 1)
                    for src, o in ((q_all, 0), (k_all, 2)):
                        last = G.tensor_tensor(h_lo[0:QK, o + s:o + s + 1, :], src[0:QK, ix, :],
                                               h_hi[0:QK, o + s:o + s + 1, :].bitcast(F32), ALU.subtract)
                    last.then_inc(qk_lo, 1)

                def normalise(h, s, t):
                    pool.wait_ge(inv_done, l * 16 + 2 * h + t // 2 + 1)
                    G.tensor_tensor(prob[:, s, t, :], prob[:, s, t, :], row_inv[:, s, t:t + 1].to_broadcast([P, S]),
                                    ALU.mult).then_inc(prob_done, 1)

                def split_v(hp):
                    pool.wait_ge(v_hi_done, l * 4 + hp + 1)
                    G.tensor_tensor(v_lo[:, :, :], v_all[:, :, bass.ds(P * hp, P)], v_hi[:, :, :].bitcast(F32),
                                    ALU.subtract).then_inc(v_lo_done, 1)

                for h in range(2):
                    split_qk(h, h, False)
                for t in (0, 2):
                    normalise(0, 0, t)

                def head_pair(hp, last):
                    for s in range(2):
                        h = 2 * hp + s
                        if s == 0:
                            split_v(hp)
                        if not last:
                            split_qk(h + 2, s, True)
                        if not (last and s == 1):
                            for t in (0, 2):
                                normalise(h + 1, 1 - s, t)

                with pool.Fori(0, HEADS // 2 - 1) as hp:
                    head_pair(hp, False)
                head_pair(HEADS // 2 - 1, True)
                x_squares(l, 2, B)
                x_squares(l, 3, B)
                assert step[0] == POOL_STEPS, step[0]


_INS = ["x", "ffn1_norm", "ffn1_w_gu", "ffn1_w_down", "mix_norm", "w_in", "q_lat_norm", "kv_lat_norm",
        "w_uq", "w_uk", "w_uv", "q_norm", "k_norm", "w_pool", "pool_scale", "w_out",
        "ffn2_norm", "ffn2_w_gu", "ffn2_w_down"]


def shape_tables(seq):
    import numpy as np

    half = QK_ROPE // 2
    inv = np.float32(10000.0) ** (-np.arange(0, QK_ROPE, 2, dtype=np.float32) / np.float32(QK_ROPE))
    ang = np.arange(seq, dtype=np.float32)[None, :] * inv.astype(np.float32)[:, None]
    cos, sin = np.cos(ang).astype(np.float32), np.sin(ang).astype(np.float32)
    groups = P // QK_ROPE
    rope_cos = np.tile(np.concatenate([cos, cos]), (groups, 1))
    rope_sin = np.tile(np.concatenate([-sin, sin]), (groups, 1))
    pos = np.concatenate([np.arange(PAD), np.arange(seq - PAD, seq)])
    edge = []
    for w in (2, 4, 8, 16):
        count = np.minimum(pos + w // 2, seq) - np.maximum(pos - w // 2, 0)
        edge.append(w / count)
    edge = np.tile(np.concatenate(edge).astype(np.float32)[None, :], (P, 1))
    assert rope_cos.shape == (P, seq) and half == 16
    return {"rope_cos": rope_cos, "rope_sin": rope_sin, "pool_edge": edge}


def kernel(**inputs):
    import numpy as np
    import concourse.bacc as bacc
    from concourse.bass_utils import run_bass_kernel_spmd

    nc = bacc.Bacc("TRN2", target_bir_lowering=False, num_devices=1)
    arrays, args = {}, []
    given = {name: np.ascontiguousarray(inputs[name]) for name in _INS}
    shape = given["x"].shape
    given.update(shape_tables(shape[1]))
    for name, a in given.items():
        arrays[f"in_{name}"] = a
        args.append(nc.dram_tensor(f"in_{name}", a.shape, mybir.dt.from_np(a.dtype), kind="ExternalInput").ap())
    args.append(nc.dram_tensor("out_y", shape, F32, kind="ExternalOutput").ap())
    build_trunk(nc, *args)
    r = run_bass_kernel_spmd(nc, [arrays], core_ids=[0])
    return r.results[0]["out_y"]
```
